# Optimizing a Trainium2 kernel written in Bass

```python
import math
import jax
import jax.numpy as jnp
from jax import lax
import numpy as np

D_MODEL = 1024
BATCH = 1
SEQ = 1024
DEPTH = 1
DEC_BATCH = 8
DEC_SEQ = 4
PAST_LEN = 4096
PAGE_SIZE = 128

D_MIX = D_MODEL
HG_WIDTH = D_MIX // 2
HG_HEADS = 4
HG_DK = HG_WIDTH // HG_HEADS
HG_DV = HG_DK
HG_CHUNK = 64
NSA_WIDTH = D_MIX - HG_WIDTH
NSA_HEADS = 8
NSA_DK = NSA_WIDTH // NSA_HEADS
NSA_KV_HEADS = 2
NSA_GROUP = NSA_HEADS // NSA_KV_HEADS
CMP_STRIDE = 16
CMP_BLOCK = 32
CMP_PARTS = CMP_BLOCK // CMP_STRIDE
CMP_HIDDEN = 4 * NSA_DK
SLC_BLOCK = 64
SLC_TOPK = 16
WINDOW = 512
WIN_QBLOCK = 128
SLC_QBLOCK = 16
N_KV_SLOTS = 4
D_FF = 2816
CONV_W = 3
EPS = 1e-6
COL_KV = N_KV_SLOTS * NSA_KV_HEADS * NSA_DK
COL_WIN = 2 * NSA_KV_HEADS * NSA_DK
COL_GATE = 3 * NSA_HEADS
SPLITS = (HG_WIDTH, HG_WIDTH, HG_WIDTH, HG_WIDTH, NSA_WIDTH, COL_KV, COL_WIN, COL_GATE)
D_IN = 4 * HG_WIDTH + NSA_WIDTH + COL_KV + COL_WIN + COL_GATE

kernel_name = "hgrn2_nsa_convffn_hybrid_step"

def rmsnorm(x, g):
    xf = x.astype(jnp.float32)
    xf = xf * lax.rsqrt(jnp.mean(xf * xf, axis=-1, keepdims=True) + EPS)
    return xf.astype(x.dtype) * g

def masked_softmax(s, mask):
    s = jnp.where(mask, s.astype(jnp.float32), -jnp.inf)
    m = jnp.max(s, axis=-1, keepdims=True)
    m = jnp.where(jnp.isfinite(m), m, 0.0)
    e = jnp.where(mask, jnp.exp(s - m), 0.0)
    d = jnp.sum(e, axis=-1, keepdims=True)
    return e / jnp.where(d > 0, d, 1.0)

def hgrn2_scan(q, logf, k, v, s0):
    B, T, H, DK = q.shape
    DV = v.shape[-1]
    C = min(HG_CHUNK, T)
    pad = (-T) % C
    if pad:
        pw = ((0, 0), (0, pad), (0, 0), (0, 0))
        q, logf, k, v = (jnp.pad(a, pw) for a in (q, logf, k, v))
    n = (T + pad) // C

    def chunks(a):
        return a.reshape(B, n, C, H, a.shape[-1]).transpose(1, 0, 3, 2, 4)

    causal = jnp.tril(jnp.ones((C, C), dtype=bool))[:, :, None]

    def step(s, xs):
        qb, fb, kb, vb = xs
        a = jnp.cumsum(fb.astype(jnp.float32), axis=2)
        decay = jnp.exp(jnp.where(causal, a[:, :, :, None, :] - a[:, :, None, :, :], -jnp.inf))
        att = jnp.einsum('bhtk,bhsk,bhtsk->bhts', qb, kb, decay)
        o = jnp.einsum('bhts,bhsv->bhtv', att, vb) + jnp.einsum('bhtk,bhkv->bhtv', qb * jnp.exp(a), s)
        a_end = a[:, :, -1:, :]
        s = jnp.exp(a_end[:, :, 0, :, None]) * s + jnp.einsum('bhsk,bhsv->bhkv', kb * jnp.exp(a_end - a), vb)
        return s, o

    s_fin, o = lax.scan(step, s0.astype(jnp.float32), tuple(chunks(a) for a in (q, logf, k, v)))
    o = o.transpose(1, 0, 3, 2, 4).reshape(B, n * C, H, DV)[:, :T]
    return o, s_fin

def hgrn2_mixer(q_raw, f_raw, i_raw, g_raw, lb, norm_w, s0):
    B, T, _ = q_raw.shape
    fr = f_raw.astype(jnp.float32)
    lb = lb.astype(jnp.float32)
    f = lb + (1.0 - lb) * jax.nn.sigmoid(fr)
    k = (1.0 - lb) * jax.nn.sigmoid(-fr)
    q = jax.nn.silu(q_raw)
    heads = lambda a: a.reshape(B, T, HG_HEADS, a.shape[-1] // HG_HEADS)
    o, s_fin = hgrn2_scan(heads(q), heads(jnp.log(f)), heads(k), heads(i_raw), s0)
    o = rmsnorm(o, norm_w.reshape(HG_HEADS, HG_DV)).reshape(B, T, HG_WIDTH) * jax.nn.silu(g_raw)
    return o, s_fin.astype(s0.dtype)

def compress_rows(rows, pe, w1, w2):
    B, S, G, D = rows.shape
    n_chunks = S // CMP_STRIDE
    n_blk = n_chunks - CMP_PARTS + 1
    ch = rows[:, :n_chunks * CMP_STRIDE].reshape(B, n_chunks, CMP_STRIDE, G, D)
    proj = jnp.einsum('bnsgd,psdh->pbngh', ch, w1)
    bias = jnp.einsum('psd,psdh->ph', pe, w1)
    h = proj[0, :, 0:n_blk] + bias[0]
    for p in range(1, CMP_PARTS):
        h = h + proj[p, :, p:p + n_blk] + bias[p]
    return jnp.einsum('bngh,hd->bngd', jax.nn.silu(h), w2)

def cmp_attend(q, kc, vc, qpos):
    N = kc.shape[1]
    blk_end = jnp.arange(N) * CMP_STRIDE + CMP_BLOCK - 1
    mask = blk_end[None, :] <= qpos[:, None]
    s = jnp.einsum('btgrd,bngd->bgrtn', q, kc) * (NSA_DK ** -0.5)
    p = masked_softmax(s, mask[None, None, None])
    return jnp.einsum('bgrtn,bngd->btgrd', p, vc), p

def select_blocks(p_cmp, qpos, n_slc):
    N = p_cmp.shape[-1]
    i = jnp.arange(N)[:, None]
    j = jnp.arange(n_slc)[None, :]
    lo = jnp.maximum(i * CMP_STRIDE, j * SLC_BLOCK)
    hi = jnp.minimum(i * CMP_STRIDE + CMP_BLOCK, (j + 1) * SLC_BLOCK)
    overlap = jnp.maximum(hi - lo, 0).astype(jnp.float32) / CMP_STRIDE
    imp = jnp.einsum('bgrtn,nj->btgj', p_cmp, overlap)
    cur = qpos // SLC_BLOCK
    jj = jnp.arange(n_slc)[None, :]
    valid = jj <= cur[:, None]
    forced = (jj == 0) | (jj == cur[:, None]) | (jj == cur[:, None] - 1)
    score = jnp.where(forced[None, :, None, :], jnp.inf, jnp.where(valid[None, :, None, :], imp, -jnp.inf))
    vals, idx = lax.top_k(score, min(SLC_TOPK, n_slc))
    return idx, vals > -jnp.inf

def slc_attend(q, ks, vs, idx, sel_ok, qpos):
    B, T, G, R, D = q.shape
    S = ks.shape[1]
    n_slc = -(-S // SLC_BLOCK)
    pad = n_slc * SLC_BLOCK - S
    ks_t = jnp.pad(ks, ((0, 0), (0, pad), (0, 0), (0, 0))).transpose(0, 2, 1, 3)
    vs_t = jnp.pad(vs, ((0, 0), (0, pad), (0, 0), (0, 0))).transpose(0, 2, 1, 3)
    QB = SLC_QBLOCK if T % SLC_QBLOCK == 0 else T
    nb = T // QB
    bi = jnp.arange(B)[:, None, None, None]
    gi = jnp.arange(G)[None, None, :, None]

    def block(xs):
        qb, ib, okb, pb = xs
        tok = ib[..., None] * SLC_BLOCK + jnp.arange(SLC_BLOCK)
        ok = okb[..., None] & (tok <= pb[None, :, None, None, None])
        tok = tok.reshape(B, QB, G, -1)
        ok = ok.reshape(B, QB, G, -1)
        kg = ks_t[bi, gi, tok]
        vg = vs_t[bi, gi, tok]
        s = jnp.einsum('bqgrd,bqgnd->bqgrn', qb, kg) * (NSA_DK ** -0.5)
        p = masked_softmax(s, ok[:, :, :, None, :])
        return jnp.einsum('bqgrn,bqgnd->bqgrd', p, vg)

    blk = lambda a: a.reshape((B, nb, QB) + a.shape[2:]).swapaxes(0, 1)
    o = lax.map(block, (blk(q), blk(idx), blk(sel_ok), qpos.reshape(nb, QB)))
    return o.swapaxes(0, 1).reshape(B, T, G, R, D)

def win_attend(q, kw, vw, qpos, kpos):
    B, T, G, R, D = q.shape
    Sk = kw.shape[1]
    off = Sk - T
    QB = WIN_QBLOCK if T % WIN_QBLOCK == 0 else T
    nb = T // QB
    KB = QB + WINDOW
    padw = ((0, 0), (WINDOW, 0), (0, 0), (0, 0))
    kp = jnp.pad(kw, padw)
    vp = jnp.pad(vw, padw)
    kpos_p = jnp.pad(kpos, (WINDOW, 0))
    real = jnp.arange(Sk + WINDOW) >= WINDOW
    idx = off + jnp.arange(nb)[:, None] * QB + jnp.arange(KB)[None, :]
    kb = kp[:, idx]
    vb = vp[:, idx]
    qp = qpos.reshape(nb, QB)[:, :, None]
    kpb = kpos_p[idx][:, None, :]
    mask = real[idx][:, None, :] & (kpb <= qp) & (kpb > qp - WINDOW)
    qb = q.reshape(B, nb, QB, G, R, D)
    s = jnp.einsum('bnqgrd,bnkgd->bngrqk', qb, kb) * (NSA_DK ** -0.5)
    p = masked_softmax(s, mask[None, :, None, None])
    o = jnp.einsum('bngrqk,bnkgd->bnqgrd', p, vb)
    return o.reshape(B, T, G, R, D)

def nsa_mixer(q_raw, kv_all, win_all, gate_raw, qpos, win_kpos, pe, w1, w2):
    B, T, _ = q_raw.shape
    q = q_raw.reshape(B, T, NSA_KV_HEADS, NSA_GROUP, NSA_DK)
    kc = compress_rows(kv_all[:, :, 0], pe[0], w1[0], w2[0])
    vc = compress_rows(kv_all[:, :, 1], pe[1], w1[1], w2[1])
    o_cmp, p_cmp = cmp_attend(q, kc, vc, qpos)
    n_slc = -(-kv_all.shape[1] // SLC_BLOCK)
    idx, sel_ok = select_blocks(p_cmp, qpos, n_slc)
    o_slc = slc_attend(q, kv_all[:, :, 2], kv_all[:, :, 3], idx, sel_ok, qpos)
    o_win = win_attend(q, win_all[:, :, 0], win_all[:, :, 1], qpos, win_kpos)
    g = jax.nn.sigmoid(gate_raw.astype(jnp.float32)).reshape(B, T, 3, NSA_KV_HEADS, NSA_GROUP)[..., None]
    o = g[:, :, 0] * o_cmp + g[:, :, 1] * o_slc + g[:, :, 2] * o_win
    return o.reshape(B, T, NSA_WIDTH)

def conv_ffn(h, conv_past, w_gate, w_val, conv_w, conv_b, w_down):
    T = h.shape[1]
    u = h @ w_gate
    u_ext = jnp.concatenate([conv_past.astype(u.dtype), u], axis=1)
    c = conv_b + u_ext[:, 0:T] * conv_w[0]
    for j in range(1, CONV_W):
        c = c + u_ext[:, j:j + T] * conv_w[j]
    y = (jax.nn.gelu(c) * (h @ w_val)) @ w_down
    return y, u_ext[:, T:]

def layer(x, kv_past, win_past, s0, conv_past, qpos, win_kpos, win_keep,
          lb, norm1, w_in, hg_norm, cmp_pe, cmp_w1, cmp_w2, w_out, norm2, w_gate, w_val, conv_w, conv_b, w_down):
    B, T, _ = x.shape
    z = rmsnorm(x, norm1) @ w_in
    q_hg, f_hg, i_hg, g_hg, q_nsa, kv_new, win_new, gate = jnp.split(z, np.cumsum(SPLITS)[:-1].tolist(), axis=-1)
    o_hg, s_fin = hgrn2_mixer(q_hg, f_hg, i_hg, g_hg, lb, hg_norm, s0)
    kv_new = kv_new.reshape(B, T, N_KV_SLOTS, NSA_KV_HEADS, NSA_DK)
    win_new = win_new.reshape(B, T, 2, NSA_KV_HEADS, NSA_DK)
    kv_all = kv_new if kv_past is None else jnp.concatenate([kv_past.astype(kv_new.dtype), kv_new], axis=1)
    win_all = win_new if win_past is None else jnp.concatenate([win_past.astype(win_new.dtype), win_new], axis=1)
    o_nsa = nsa_mixer(q_nsa, kv_all, win_all, gate, qpos, win_kpos, cmp_pe, cmp_w1, cmp_w2)
    x = x + (jnp.concatenate([o_hg, o_nsa], axis=-1).astype(x.dtype) @ w_out)
    y, conv_new = conv_ffn(rmsnorm(x, norm2), conv_past, w_gate, w_val, conv_w, conv_b, w_down)
    x = x + y.astype(x.dtype)
    return x, kv_new, win_all[:, -win_keep:], s_fin, conv_new

def setup_inputs(seed: int = 0) -> dict:
    key = jax.random.key(seed)
    ks = jax.random.split(key, 24)
    f32 = jnp.float32
    nrm = lambda k, shape, scale=1.0: scale * jax.random.normal(k, shape, f32)
    n_pages = PAST_LEN // PAGE_SIZE
    n_used = DEC_BATCH * n_pages
    n_pool = n_used + n_used // 4
    win_len = min(WINDOW, PAST_LEN)
    page_table = jax.random.permutation(ks[3], n_pool)[:n_used].reshape(DEC_BATCH, n_pages).astype(jnp.int32)
    return {
        "x_prompt": nrm(ks[0], (BATCH, SEQ, D_MODEL)),
        "x_sample": nrm(ks[1], (DEC_BATCH, DEC_SEQ, D_MODEL)),
        "cache_nsa_kv": nrm(ks[2], (DEPTH, n_pool, PAGE_SIZE, N_KV_SLOTS, NSA_KV_HEADS, NSA_DK)),
        "cache_win_kv": nrm(ks[4], (DEPTH, DEC_BATCH, win_len, 2, NSA_KV_HEADS, NSA_DK)),
        "state_hgrn": nrm(ks[5], (DEPTH, DEC_BATCH, HG_HEADS, HG_DK, HG_DV), 0.3),
        "state_ffn_conv": nrm(ks[6], (DEPTH, DEC_BATCH, CONV_W - 1, D_FF)),
        "page_table": page_table,
        "norm1": 1.0 + nrm(ks[7], (DEPTH, D_MODEL), 0.05),
        "w_in": nrm(ks[8], (DEPTH, D_MODEL, D_IN), D_MODEL ** -0.5),
        "hg_lb_logits": nrm(ks[9], (DEPTH + 1, HG_WIDTH)),
        "hg_norm": 1.0 + nrm(ks[10], (DEPTH, HG_WIDTH), 0.05),
        "cmp_pe": nrm(ks[11], (DEPTH, 2, CMP_PARTS, CMP_STRIDE, NSA_DK), 0.5),
        "cmp_w1": nrm(ks[12], (DEPTH, 2, CMP_PARTS, CMP_STRIDE, NSA_DK, CMP_HIDDEN), (CMP_BLOCK * NSA_DK) ** -0.5),
        "cmp_w2": nrm(ks[13], (DEPTH, 2, CMP_HIDDEN, NSA_DK), CMP_HIDDEN ** -0.5),
        "w_out": nrm(ks[14], (DEPTH, D_MIX, D_MODEL), D_MIX ** -0.5),
        "norm2": 1.0 + nrm(ks[15], (DEPTH, D_MODEL), 0.05),
        "w_gate": nrm(ks[16], (DEPTH, D_MODEL, D_FF), D_MODEL ** -0.5),
        "w_val": nrm(ks[17], (DEPTH, D_MODEL, D_FF), D_MODEL ** -0.5),
        "conv_w": nrm(ks[18], (DEPTH, CONV_W, D_FF), CONV_W ** -0.5),
        "conv_b": nrm(ks[19], (DEPTH, D_FF), 0.02),
        "w_down": nrm(ks[20], (DEPTH, D_FF, D_MODEL), D_FF ** -0.5),
        "norm_f": 1.0 + nrm(ks[21], (D_MODEL,), 0.05),
    }

def reference(x_prompt, x_sample, cache_nsa_kv, cache_win_kv, state_hgrn, state_ffn_conv, page_table,
              norm1, w_in, hg_lb_logits, hg_norm, cmp_pe, cmp_w1, cmp_w2, w_out, norm2,
              w_gate, w_val, conv_w, conv_b, w_down, norm_f):
    B, T = x_prompt.shape[:2]
    Bd, Td = x_sample.shape[:2]
    past = page_table.shape[1] * PAGE_SIZE
    win_len = cache_win_kv.shape[2]
    qpos_p = jnp.arange(T)
    qpos_s = past + jnp.arange(Td)
    win_kpos_s = past - win_len + jnp.arange(win_len + Td)
    lb_all = jnp.cumsum(jax.nn.softmax(hg_lb_logits.astype(jnp.float32), axis=0), axis=0)
    hp, hs = x_prompt, x_sample
    kv_p, kv_s, win_p, win_s, hg_p, hg_s, cv_p, cv_s = [], [], [], [], [], [], [], []
    for l in range(DEPTH):
        w = (lb_all[l], norm1[l], w_in[l], hg_norm[l], cmp_pe[l], cmp_w1[l], cmp_w2[l], w_out[l],
             norm2[l], w_gate[l], w_val[l], conv_w[l], conv_b[l], w_down[l])
        s0_p = jnp.zeros((B, HG_HEADS, HG_DK, HG_DV), hp.dtype)
        c0_p = jnp.zeros((B, CONV_W - 1, D_FF), hp.dtype)
        hp, a, b, c, d = layer(hp, None, None, s0_p, c0_p, qpos_p, qpos_p, min(WINDOW, T), *w)
        kv_p.append(a); win_p.append(b); hg_p.append(c); cv_p.append(d)
        kv_past = cache_nsa_kv[l][page_table].reshape(Bd, past, N_KV_SLOTS, NSA_KV_HEADS, NSA_DK)
        hs, a, b, c, d = layer(hs, kv_past, cache_win_kv[l], state_hgrn[l], state_ffn_conv[l],
                               qpos_s, win_kpos_s, win_len, *w)
        kv_s.append(a); win_s.append(b); hg_s.append(c); cv_s.append(d)
    y_prompt = rmsnorm(hp, norm_f)
    y_sample = rmsnorm(hs, norm_f)
    return (y_prompt, y_sample, jnp.stack(kv_p), jnp.stack(kv_s), jnp.stack(win_p), jnp.stack(win_s),
            jnp.stack(hg_p), jnp.stack(hg_s), jnp.stack(cv_p), jnp.stack(cv_s))


_drawn_inputs = setup_inputs


def setup_inputs(seed=0):
    import zlib

    import numpy as np

    out = dict(_drawn_inputs(seed))
    spreads = {}
    factors = {'conv_b': 5.743}
    for name, (base, spread) in spreads.items():
        noise = np.random.default_rng([zlib.crc32(name.encode()), seed]).standard_normal(out[name].shape)
        drawn = base * np.exp(spread * noise) if base else spread * noise
        out[name] = jnp.asarray(drawn.astype(out[name].dtype))
    for name, factor in factors.items():
        out[name] = (out[name] * factor).astype(out[name].dtype)
    return out
```

```python
from contextlib import ExitStack

import concourse.bass as bass
from concourse import mybir

F32 = mybir.dt.float32
I32 = mybir.dt.int32
U32 = mybir.dt.uint32
ALU = mybir.AluOpType
ACT = mybir.ActivationFunctionType
AX = mybir.AxisListType

P = 128
D = 1024
KD = D // P
T = 1024
DB, DS = 8, 4
DT = DB * DS
TOK = T + DT
NT = T // P + 1
HGW = 512
HH = 4
NH, NG, DK = 8, 2, 64
R = NH // NG
PAST, PAGE = 4096, 128
NPAGE = PAST // PAGE
WIN = 512
D_IN = 6 * HGW + 256 + 24
FF = 2816
EPS = 1e-6
BIG = 1e30
SCALE = DK ** -0.5
NCP = T // 16
NCD = PAST // 16
NSB = 65


class Steps:

    def __init__(self, eng, sem, base=0):
        self.eng, self.sem, self.base, self.n = eng, sem, base, 0

    def __call__(self, ins):
        self.n += 1
        ins.then_inc(self.sem, 1)
        self.eng.wait_ge(self.sem, self.base + self.n)
def shape_constants():
    import numpy as np

    c = {"c_ident": np.eye(P, dtype=np.float32)}
    s, t = np.arange(P)[:, None], np.arange(P)[None, :]
    levels = [(s // (2 * h) == t // (2 * h)) & (s % (2 * h) < h) & (t % (2 * h) >= h) for h in HALVES] + [s == t]
    c["c_hmask"] = np.stack(levels, 1).astype(np.float32)
    at = np.arange(TOK)
    c["c_reset"] = np.tile(np.where(at < T, at % P, (at - T) % DS) > 0, (P, 1)).astype(np.float32)
    c["c_rowsel"] = (np.arange(DT)[:, None] // DS == np.arange(DB)[None, :]).astype(np.float32)
    row_t = np.arange(16) // R
    wm = np.zeros((64, 2 * DS), np.float32)
    for g in range(NG):
        for q in range(16):
            wm[48 * g + q, 0:row_t[q] + 1] = -BIG
            wm[48 * g + q, DS + row_t[q] + 1:] = -BIG
    c["c_wmask"] = wm
    c["c_nmask"] = np.where(np.arange(DS)[None, :] > np.tile(row_t, NG)[:, None], -BIG, 0.0).astype(np.float32)
    n, j = np.arange(2 * P)[:, None], np.arange(64)[None, :]
    over = np.maximum(np.minimum(16 * n + 32, 64 * j + 64) - np.maximum(16 * n, 64 * j), 0) / 16.0
    c["c_overlap"] = np.ascontiguousarray(over.reshape(2, P, 64).transpose(1, 0, 2)).astype(np.float32)
    chunk = np.arange(2 * P).reshape(2, P)
    c["c_spread"] = np.stack([(chunk[k][None, :] // 4 == np.arange(64)[:, None]) for k in range(2)], 1).astype(np.float32)
    c["c_part"] = (np.arange(P) % 8).astype(np.float32)[:, None]
    i, k = np.arange(P)[:, None], np.arange(P)[None, :]
    c["c_causal"] = np.where(k > i, -BIG, 0.0).astype(np.float32)
    c["c_older"] = np.where(k <= i, -BIG, 0.0).astype(np.float32)
    qpos = (np.arange(T // P)[None, :, None] * P + np.arange(P)[:, None, None])
    c["c_cmask"] = np.where(np.arange(NCP - 1)[None, None, :] * 16 + 31 > qpos, -BIG, 0.0).astype(np.float32)
    return c


def project_in(nc, io, keep, scratch, consts_sb):
    qh, fg, qn = keep["qh"], keep["fg"], keep["qn"]
    ident = consts_sb["ident"]
    FM = [("q_hg", 0), ("f_hg", HGW), ("q_nsa", 4 * HGW)]
    TM = [(2 * HGW, 512, 0), (3 * HGW, 512, 512), (5 * HGW, 512, 1024), (6 * HGW, D_IN - 6 * HGW, 1536)]
    GROUPS = [(c, 512) for _, c in FM] + [(c, w) for c, w, _ in TM]
    N_T = [(0, 352), (352, 352), (704, 352)]

    units = []
    for g in range(len(FM)):
        for m in range(4):
            for n0, nw in N_T:
                units.append(("fm", g, m, n0, nw))
    for g in range(len(TM)):
        for t in range(NT):
            units.append(("tm", g, t, 0, TM[g][1]))
    first_tm = sum(u[0] == "fm" for u in units)

    with ExitStack() as ctx:
        sb = lambda name, shape: ctx.enter_context(nc.sbuf_tensor(name, shape, F32))
        sem = lambda name: ctx.enter_context(nc.semaphore(name))
        xin = sb("xin", [P, 3, D])
        xn = sb("xn", [P, 2, D])
        sq = sb("sq", [P, D])
        ss = sb("ss", [P, NT])
        rstd = sb("rstd", [P, NT])
        rt = sb("rt", [P, NT])
        g1 = sb("g1", [P, KD])
        xnT = sb("xnT", [P, KD, TOK])
        wbuf = sb("wbuf", [P, 2, KD, 512])
        stage = sb("stage", [P, 4, 512])
        bank = [ctx.enter_context(nc.psum_tensor(f"pj{i}", [P, 512], F32)) for i in range(8)]

        x_in = [sem(f"p1_x_in{i}") for i in range(3)]
        ss_ready = sem("p1_ss_ready")
        root_ready = sem("p1_root_ready")
        rstd_ready = sem("p1_rstd_ready")
        xn_ready = sem("p1_xn_ready")
        xT_ready = sem("p1_xT_ready")
        xT_kept = sem("p1_xT_kept")
        g1_in = sem("p1_g1_in")
        w_in_s = [consts_sb["soft"][f"p1_w_in{i}"] for i in range(2)]
        unit_ready = sem("p1_unit_ready")
        kept = [sem("p1_kept_dve"), sem("p1_kept_act")]
        stored = [sem(f"p1_stored{i}") for i in range(4)]
        cached = consts_sb["soft"]["p1_cached"]

        def rows(t):
            return P if t < NT - 1 else DT

        def evacuate(eng, u, kind, g, a, n0, nw, copy):
            eng.wait_ge(unit_ready, u + 1)
            b = bank[u % 8]
            if kind == "fm" and g < 2:
                copy((qh, fg)[g][:, a, n0:n0 + nw], b[:, 0:nw]).then_inc(kept[u % 2], 1)
            elif kind == "fm":
                copy(qn[:, 2 * a, n0:n0 + nw], b[0:64, 0:nw])
                copy(qn[:, 2 * a + 1, n0:n0 + nw], b[64:128, 0:nw]).then_inc(kept[u % 2], 1)
            else:
                j = u - first_tm
                if j >= 4:
                    eng.wait_ge(stored[j % 4], 16 * (j // 4))
                r = rows(a)
                copy(stage[0:r, j % 4, 0:nw], b[0:r, 0:nw]).then_inc(kept[u % 2], 1)

        block = ctx.enter_context(nc.Block())

        @block.sync
        def _(sp):
            sp.dma_start(g1[:], io["norm1"].rearrange("a (k p) -> p (a k)", p=P), allow_slow_non_contiguous=True).then_inc(g1_in, 16)
            for t in range(NT):
                if t >= 3:
                    sp.wait_ge(xn_ready, t - 2)
                src = io["x_prompt"][0, t * P:(t + 1) * P, :] if t < NT - 1 else io["x_sample"].rearrange("b t d -> (b t) d")
                sp.dma_start(xin[0:rows(t), t % 3, :], src).then_inc(x_in[t % 3], 16)
            for j in range(NT * len(TM)):
                u = first_tm + j
                g, t = units[u][1], units[u][2]
                w, c0 = TM[g][1], TM[g][2]
                sp.wait_ge(kept[u % 2], u // 2 + 1)
                sp.dma_start(scratch["z_tok"][t * P:t * P + rows(t), c0:c0 + w],
                             stage[0:rows(t), j % 4, 0:w]).then_inc(stored[j % 4], 16)
            for i in range(4):
                sp.wait_ge(stored[i], 16 * (NT * len(TM) // 4))

        @block.gpsimd
        def _(pool):
            for j, (c, w) in enumerate(GROUPS):
                if j >= 2:
                    pool.wait_ge(unit_ready, 12 * (j - 1) if j - 2 < len(FM) else first_tm + NT * (j - 1 - len(FM)))
                pool.dma_start(wbuf[:, j % 2, :, 0:w], io["w_in"][0].rearrange("(k p) n -> p k n", p=P)[:, :, c:c + w]
                               ).then_inc(w_in_s[j % 2], 16)
            pool.dma_start(io["win_s"][0, :, 0:WIN - DS], io["cache_win_kv"][0, :, DS:WIN]).then_inc(cached, 16)
            pool.wait_ge(cached, 16)

        @block.scalar
        def _(act):
            act.wait_ge(ss_ready, 1)
            for t in range(NT):
                act.wait_ge(x_in[t % 3], 16 * (t // 3 + 1))
                if t >= 1:
                    act.wait_ge(root_ready, t)
                r = rows(t)
                nc.scalar.activation(sq[0:r, :], xin[0:r, t % 3, :], ACT.Square, accum_out=ss[0:r, t:t + 1]).then_inc(ss_ready, 1)
                act.wait_ge(rstd_ready, 2 * t + 1)
                nc.scalar.activation(rt[0:r, t:t + 1], rstd[0:r, t:t + 1], ACT.Sqrt).then_inc(root_ready, 1)
            for u, (kind, g, a, n0, nw) in enumerate(units):
                if u % 2 == 1:
                    evacuate(act, u, kind, g, a, n0, nw, lambda o, i: nc.scalar.copy(o, i))

        @block.vector
        def _(dve):
            nc.vector.memset(ss[:], 1.0).then_inc(ss_ready, 1)
            dve.wait_ge(g1_in, 16)
            for t in range(NT):
                r = rows(t)
                dve.wait_ge(ss_ready, t + 2)
                nc.vector.tensor_scalar(rstd[0:r, t:t + 1], ss[0:r, t:t + 1], 1.0 / D, EPS, ALU.mult, ALU.add).then_inc(rstd_ready, 1)
                dve.wait_ge(root_ready, t + 1)
                nc.vector.reciprocal(rstd[0:r, t:t + 1], rt[0:r, t:t + 1]).then_inc(rstd_ready, 1)
                dve.wait_ge(rstd_ready, 2 * t + 2)
                if t >= 2:
                    dve.wait_ge(xT_ready, 2 * (t - 1))
                nc.vector.tensor_scalar(xn[0:r, t % 2, :], xin[0:r, t % 3, :], rstd[0:r, t:t + 1], None, ALU.mult).then_inc(xn_ready, 1)
                for h in range(2):
                    dve.wait_ge(xT_ready, 2 * t + h + 1)
                    nc.vector.tensor_tensor(xnT[:, 4 * h:4 * h + 4, t * P:t * P + r],
                                            bank[(2 * t + h) % 8][:].rearrange("p (k c) -> p k c", k=4)[:, :, 0:r],
                                            g1[:, 4 * h:4 * h + 4].unsqueeze(2).to_broadcast([P, 4, r]), ALU.mult).then_inc(xT_kept, 1)
            for u, (kind, g, a, n0, nw) in enumerate(units):
                if u % 2 == 0:
                    evacuate(dve, u, kind, g, a, n0, nw, lambda o, i: nc.vector.tensor_copy(o, i))

        @block.tensor
        def _(pe):
            pe.wait_ge(consts_sb["in"], 16)
            for t in range(NT):
                r = rows(t)
                pe.wait_ge(xn_ready, t + 1)
                for h in range(2):
                    n = 2 * t + h
                    if n >= 8:
                        pe.wait_ge(xT_kept, n - 7)
                    for k in range(4):
                        last = nc.tensor.transpose(bank[n % 8][:, k * P:k * P + r],
                                                   xn[0:r, t % 2, (4 * h + k) * P:(4 * h + k + 1) * P], ident[0:r, 0:r])
                    last.then_inc(xT_ready, 1)
            pe.wait_ge(xT_kept, 2 * NT)
            seen = -1
            for u, (kind, g, a, n0, nw) in enumerate(units):
                j = g if kind == "fm" else len(FM) + g
                if j != seen:
                    pe.wait_ge(w_in_s[j % 2], 16 * (j // 2 + 1))
                    seen = j
                if u >= 8:
                    pe.wait_ge(kept[u % 2], (u - 8) // 2 + 1)
                for k in range(KD):
                    if kind == "fm":
                        last = nc.tensor.matmul(bank[u % 8][:, 0:nw], wbuf[:, j % 2, k, a * P:(a + 1) * P],
                                                xnT[:, k, n0:n0 + nw], start=(k == 0), stop=(k == KD - 1))
                    else:
                        r = rows(a)
                        last = nc.tensor.matmul(bank[u % 8][0:r, 0:nw], xnT[:, k, a * P:a * P + r],
                                                wbuf[:, j % 2, k, 0:nw], start=(k == 0), stop=(k == KD - 1))
                last.then_inc(unit_ready, 1)
HALVES = (64, 32, 16, 8, 4, 2, 1)


def hgrn(nc, io, keep, scratch, consts_sb):
    qh, fg = keep["qh"], keep["fg"]
    ident = consts_sb["ident"]
    NL = len(HALVES)
    NC = T // P

    with ExitStack() as ctx:
        sb = lambda name, shape: ctx.enter_context(nc.sbuf_tensor(name, shape, F32))
        sem = lambda name: ctx.enter_context(nc.semaphore("p2_" + name))
        kk = sb("kk", [P, HH, TOK])
        v_tok = sb("v_tok", [P, NT, HGW])
        o_tok = sb("o_tok", [P, NT, HGW])
        W = sb("W", [P, NL, TOK])
        g_tok = W[:].rearrange("p l t -> p (l t)")[:, 0:NT * HGW].rearrange("p (t n) -> p t n", t=NT)
        Q, K, A = sb("Q", [P, TOK]), sb("K", [P, TOK]), sb("A", [P, TOK])
        EA, QA, KE = sb("EA", [P, TOK]), sb("QA", [P, TOK]), sb("KE", [P, TOK])
        vd = sb("vd", [DT, P])
        vsel = sb("vsel", [DT, DB, P])
        KEt = sb("KEt", [P, NC, P])
        KEtd = sb("KEtd", [DT, P])
        hmask = sb("hmask", [P, NL + 1, P])
        prod = sb("prod", [P, NL + 1, P])
        prodd = sb("prodd", [DT, 3, DT])
        attT = sb("attT", [P, 2, P])
        attTd = sb("attTd", [DT, DT])
        S = sb("S", [P, P])
        S0 = sb("S0", [P, DB, P])
        oTd = sb("oTd", [P, DT])
        rowsel = sb("rowsel", [DT, DB])
        reset = sb("reset", [P, TOK])
        lgt = sb("lgt", [P, 2, HH])
        lmax, lb, oml, lsum = (sb(n, [P, HH]) for n in ("lmax", "lb", "oml", "lsum"))
        oss = sb("oss", [P, NT * HH])
        ort = sb("ort", [P, NT * HH])
        normw = sb("normw", [P, HGW])
        pa = [ctx.enter_context(nc.psum_tensor(f"pa{i}", [P, 4, P], F32)) for i in range(4)]
        po = [ctx.enter_context(nc.psum_tensor(f"po{i}", [P, 512], F32)) for i in range(2)]
        ps = ctx.enter_context(nc.psum_tensor("ps", [P, 512], F32))
        pd = ctx.enter_context(nc.psum_tensor("pd", [P, 512], F32))

        small_in, v_in, g_in, s0_in = sem("small_in"), sem("v_in"), sem("g_in"), sem("s0_in")
        lb_step = sem("lb_step")
        lexp_ready, lb_ready = sem("lexp_ready"), sem("lb_ready")
        gates_ready, f_ready, logf_ready, a_ready = sem("gates_ready"), sem("f_ready"), sem("logf_ready"), sem("a_ready")
        copied, d_ready, e_ready, w_ready = sem("copied"), sem("d_ready"), sem("e_ready"), sem("w_ready")
        keT_ready, keT_kept = sem("keT_ready"), sem("keT_kept")
        att_ready, prod_ready, attT_ready = sem("att_ready"), sem("prod_ready"), sem("attT_ready")
        o_ready, o_kept, st_ready, s_ready = sem("o_ready"), sem("o_kept"), sem("st_ready"), sem("s_ready")
        s_out = sem("s_out")
        attd_ready, prodd_ready, attTd_ready, oTd_ready, oTd_kept = (sem(n) for n in (
            "attd_ready", "prodd_ready", "attTd_ready", "oTd_ready", "oTd_kept"))
        od_ready, std_ready, s0_step, s0_done, s0_out = (sem(n) for n in (
            "od_ready", "std_ready", "s0_step", "s0_done", "s0_out"))
        norm_step, oroot_ready, gsilu_ready, oms_ready, o_done, o_out, copies_out = (sem(n) for n in (
            "norm_step", "oroot_ready", "gsilu_ready", "oms_ready", "o_done", "o_out", "copies_out"))

        block = ctx.enter_context(nc.Block())

        def halves(x, h):
            n = TOK if 2 * h <= DS else T
            return x[:, 0:n].rearrange("p (b t) -> p b t", t=2 * h)

        @block.sync
        def _(sp):
            sp.dma_start(lgt[:], io["hg_lb_logits"].rearrange("l (h p) -> p l h", p=P), allow_slow_non_contiguous=True).then_inc(small_in, 16)
            sp.dma_start(reset[:], io["c_reset"]).then_inc(small_in, 16)
            sp.dma_start(hmask[:], io["c_hmask"]).then_inc(small_in, 16)
            sp.dma_start(rowsel[:], io["c_rowsel"]).then_inc(small_in, 16)
            sp.dma_start(normw[:], io["hg_norm"].to_broadcast([P, HGW])).then_inc(small_in, 16)
            sp.dma_start(v_tok[:, 0:NC, :], scratch["z_tok"][0:T, 0:HGW].rearrange("(t p) n -> p t n", p=P)).then_inc(v_in, 16)
            sp.dma_start(v_tok[0:DT, NC, :], scratch["z_tok"][T:TOK, 0:HGW]).then_inc(v_in, 16)
            z = scratch["z_tok"]
            sp.dma_start(scratch["q_T"], keep["qn"][:]).then_inc(copies_out, 16)
            sp.dma_start(io["kv_p"][0, 0].rearrange("t s g d -> t (s g d)"), z[0:T, 1024:1536]).then_inc(copies_out, 16)
            sp.dma_start(io["kv_s"][0].rearrange("b t s g d -> (b t) (s g d)"), z[T:TOK, 1024:1536]).then_inc(copies_out, 16)
            sp.dma_start(io["win_p"][0, 0].rearrange("t s g d -> t (s g d)"), z[T - WIN:T, 1536:1792]).then_inc(copies_out, 16)
            sp.dma_start(io["win_s"][0, :, WIN - DS:WIN].rearrange("b t s g d -> b t (s g d)"),
                         z[T:TOK, 1536:1792].rearrange("(b t) n -> b t n", b=DB)).then_inc(copies_out, 16)
            sp.sem_inc(s0_out, 16)
            sp.sem_inc(s_out, 16)
            with sp.Fori(0, HH) as h:
                sp.wait_ge(s0_out, 16 * h + 16)
                sp.dma_start(S0[:], io["state_hgrn"][0, :, bass.ds(h, 1), :, :].rearrange("b o k v -> k (b o) v")).then_inc(s0_in, 16)
                sp.wait_ge(s_ready, (NC + 1) * (h + 1))
                sp.dma_start(io["hg_p"][0, 0, bass.ds(h, 1)].rearrange("o k v -> k (o v)"), S[:]).then_inc(s_out, 16)
                sp.wait_ge(s0_done, h + 2)
                sp.dma_start(io["hg_s"][0, :, bass.ds(h, 1), :, :].rearrange("b o k v -> k (b o) v"), S0[:]).then_inc(s0_out, 16)
            sp.wait_ge(o_kept, HH * (NC + 1) + 1)
            sp.dma_start(g_tok[:, 0:NC, :], z[0:T, HGW:2 * HGW].rearrange("(t p) n -> p t n", p=P)).then_inc(g_in, 16)
            sp.dma_start(g_tok[0:DT, NC, :], z[T:TOK, HGW:2 * HGW]).then_inc(g_in, 16)
            sp.wait_ge(o_done, 1)
            sp.dma_start(scratch["o_mix"][0:T, 0:HGW].rearrange("(t p) n -> p t n", p=P), o_tok[:, 0:NC, :]).then_inc(o_out, 16)
            sp.dma_start(scratch["o_mix"][T:TOK, 0:HGW], o_tok[0:DT, NC, :]).then_inc(o_out, 16)
            sp.wait_ge(o_out, 32)
            sp.wait_ge(copies_out, 80)
            sp.wait_ge(s_out, 16 * HH + 16)
            sp.wait_ge(s0_out, 16 * HH + 16)

        @block.scalar
        def _(act):
            act.wait_ge(lb_step, 2)
            nc.scalar.activation(lgt[:], lgt[:], ACT.Exp).then_inc(lexp_ready, 1)
            nc.scalar.activation(kk[:], fg[:], ACT.Sigmoid, scale=-1.0).then_inc(gates_ready, 1)
            act.wait_ge(gates_ready, 1)
            nc.scalar.activation(fg[:], fg[:], ACT.Sigmoid).then_inc(gates_ready, 1)
            nc.scalar.activation(qh[:], qh[:], ACT.Silu).then_inc(gates_ready, 1)
            act.wait_ge(f_ready, HH)
            nc.scalar.activation(fg[:], fg[:], ACT.Ln).then_inc(logf_ready, 1)
            act.wait_ge(gates_ready, 3)
            act.wait_ge(v_in, 32)
            act.sem_inc(o_kept, 1)
            with act.Fori(0, HH) as h:
                act.wait_ge(s0_done, h + 1)
                act.wait_ge(a_ready, h + 1)
                row = lambda x: x[:, bass.ds(h, 1), :].rearrange("p o t -> p (o t)")
                nc.scalar.copy(A[:], row(fg)).then_inc(copied, 1)
                nc.scalar.copy(Q[:], row(qh)).then_inc(copied, 1)
                nc.scalar.copy(K[:], row(kk)).then_inc(copied, 1)
                nc.scalar.copy(vd[:], v_tok[0:DT, NC, bass.ds(h * P, P)]).then_inc(copied, 1)
                act.wait_ge(copied, 4 * h + 1)
                nc.scalar.activation(EA[:], A[:], ACT.Exp).then_inc(e_ready, 1)
                act.wait_ge(d_ready, (NL + 1) * h + 1)
                nc.scalar.activation(KE[:], KE[:], ACT.Exp).then_inc(e_ready, 1)
                for l, half in enumerate(HALVES):
                    act.wait_ge(d_ready, (NL + 1) * h + l + 2)
                    n = TOK if 2 * half <= DS else T
                    nc.scalar.activation(W[:, l, 0:n], W[:, l, 0:n], ACT.Exp).then_inc(e_ready, 1)
                for j in range(2):
                    act.wait_ge(keT_ready, 3 * h + j + 1)
                    nc.scalar.copy(KEt[:, 4 * j:4 * j + 4, :], pa[j][:]).then_inc(keT_kept, 1)
                act.wait_ge(keT_ready, 3 * h + 3)
                nc.scalar.copy(KEtd[:], pd[0:DT, 384:512]).then_inc(keT_kept, 1)
                for c in range(NC):
                    act.wait_ge(o_ready, NC * h + c + 1)
                    nc.scalar.copy(o_tok[:, c, bass.ds(h * P, P)], po[c % 2][:, 0:P]).then_inc(o_kept, 1)
                act.wait_ge(oTd_ready, h + 1)
                nc.scalar.copy(oTd[:], pd[:, 128:160]).then_inc(oTd_kept, 1)
                act.wait_ge(od_ready, h + 1)
                nc.scalar.copy(o_tok[0:DT, NC, bass.ds(h * P, P)], pd[0:DT, 256:384]).then_inc(o_kept, 1)
            act.wait_ge(oms_ready, 1)
            nc.scalar.activation(ort[:], oss[:], ACT.Sqrt).then_inc(oroot_ready, 1)
            act.wait_ge(g_in, 32)
            nc.scalar.activation(g_tok[:, 0:NC, :], g_tok[:, 0:NC, :], ACT.Silu)
            nc.scalar.activation(g_tok[0:DT, NC, :], g_tok[0:DT, NC, :], ACT.Silu).then_inc(gsilu_ready, 1)

        @block.vector
        def _(dve):
            dve.wait_ge(small_in, 80)
            step = Steps(dve, lb_step)
            step(nc.vector.tensor_tensor(lmax[:], lgt[:, 0, :], lgt[:, 1, :], ALU.max))
            step(nc.vector.tensor_tensor(lgt[:], lgt[:], lmax[:].unsqueeze(1).to_broadcast([P, 2, HH]), ALU.subtract))
            dve.wait_ge(lexp_ready, 1)
            step(nc.vector.tensor_tensor(lsum[:], lgt[:, 0, :], lgt[:, 1, :], ALU.add))
            step(nc.vector.reciprocal(lsum[:], lsum[:]))
            step(nc.vector.tensor_tensor(lb[:], lgt[:, 0, :], lsum[:], ALU.mult))
            step(nc.vector.tensor_scalar(oml[:], lb[:], -1.0, 1.0, ALU.mult, ALU.add))
            nc.vector.memset(o_tok[:, NC, :], 0.0).then_inc(lb_ready, 1)
            for h in range(HH):
                dve.wait_ge(gates_ready, 2)
                nc.vector.tensor_scalar(kk[:, h, :], kk[:, h, :], oml[:, h:h + 1], None, ALU.mult)
                nc.vector.tensor_scalar(fg[:, h, :], fg[:, h, :], oml[:, h:h + 1], lb[:, h:h + 1], ALU.mult, ALU.add).then_inc(f_ready, 1)
            dve.wait_ge(logf_ready, 1)
            for h in range(HH):
                nc.vector.tensor_tensor_scan(fg[:, h, :], reset[:], fg[:, h, :], 0.0, ALU.mult, ALU.add).then_inc(a_ready, 1)
            dve.wait_ge(lb_ready, 1)
            for ahead in (s0_done, attT_ready, prod_ready):
                dve.sem_inc(ahead, 1)
            with dve.Fori(0, HH) as h:
                dve.wait_ge(copied, 4 * h + 4)
                ch = lambda x: x[:, 0:T].rearrange("p (c t) -> p c t", t=P)
                dc = lambda x: x[:, T:TOK].rearrange("p (c t) -> p c t", t=DS)
                nc.vector.tensor_tensor(ch(KE), ch(A)[:, :, P - 1:P].to_broadcast([P, NC, P]), ch(A), ALU.subtract)
                nc.vector.tensor_tensor(dc(KE), dc(A)[:, :, DS - 1:DS].to_broadcast([P, DB, DS]), dc(A), ALU.subtract).then_inc(d_ready, 1)
                for l, half in enumerate(HALVES):
                    a, w = halves(A, half), halves(W[:, l, :], half)
                    mid = a[:, :, half - 1:half].to_broadcast([P, a.shape[1], half])
                    nc.vector.tensor_tensor(w[:, :, 0:half], mid, a[:, :, 0:half], ALU.subtract)
                    nc.vector.tensor_tensor(w[:, :, half:], a[:, :, half:], mid, ALU.subtract).then_inc(d_ready, 1)
                base = (NL + 2) * h
                dve.wait_ge(e_ready, base + 1)
                nc.vector.tensor_tensor(QA[:], EA[:], Q[:], ALU.mult).then_inc(w_ready, 1)
                dve.wait_ge(e_ready, base + 2)
                nc.vector.tensor_tensor(KE[:], KE[:], K[:], ALU.mult).then_inc(w_ready, 1)
                for l, half in enumerate(HALVES):
                    w = halves(W[:, l, :], half)
                    dve.wait_ge(e_ready, base + l + 3)
                    nc.vector.tensor_tensor(w[:, :, 0:half], w[:, :, 0:half], halves(K, half)[:, :, 0:half], ALU.mult)
                    nc.vector.tensor_tensor(w[:, :, half:], w[:, :, half:], halves(Q, half)[:, :, half:], ALU.mult).then_inc(w_ready, 1)
                nc.vector.tensor_tensor(vsel[:], vd[:].unsqueeze(1).to_broadcast([DT, DB, P]),
                                        rowsel[:].unsqueeze(2).to_broadcast([DT, DB, P]), ALU.mult).then_inc(w_ready, 1)
                dve.wait_ge(s_out, 16 * h + 16)
                nc.vector.memset(S[:], 0.0).then_inc(s_ready, 1)

                def picked(c):
                    dve.wait_ge(att_ready, NC * h + c + 1)
                    dve.wait_ge(attT_ready, NC * h + c + 1)
                    b = 2 * (c % 2)
                    nc.vector.tensor_tensor(prod[:, 0:4, :], pa[b][:], hmask[:, 0:4, :], ALU.mult)
                    nc.vector.tensor_tensor(prod[:, 4:8, :], pa[b + 1][:], hmask[:, 4:8, :], ALU.mult).then_inc(prod_ready, 1)
                    dve.wait_ge(prod_ready, NC * h + c + 2)
                    if c >= 2:
                        dve.wait_ge(o_ready, NC * h + c - 1)
                    nc.vector.tensor_reduce(attT[:, c % 2, :], prod[:].rearrange("p l t -> p t l"), AX.X, ALU.add).then_inc(attT_ready, 1)

                picked(0)
                for c in range(NC):
                    if c + 1 < NC:
                        picked(c + 1)
                    dve.wait_ge(st_ready, NC * h + c + 1)
                    dve.wait_ge(s_ready, (NC + 1) * h + c + 1)
                    nc.vector.scalar_tensor_tensor(S[:], S[:], EA[:, c * P + P - 1:c * P + P], ps[:, 0:P], ALU.mult, ALU.add).then_inc(s_ready, 1)
                dve.wait_ge(attd_ready, h + 1)
                nc.vector.tensor_tensor(prodd[:], pd[0:DT, 0:96].rearrange("p (l t) -> p l t", l=3), hmask[0:DT, 5:8, 0:DT],
                                        ALU.mult).then_inc(prodd_ready, 1)
                dve.wait_ge(prodd_ready, h + 1)
                nc.vector.tensor_reduce(attTd[:], prodd[:].rearrange("p l t -> p t l"), AX.X, ALU.add).then_inc(attTd_ready, 1)
                dve.wait_ge(std_ready, h + 1)
                nc.vector.tensor_tensor(S0[:], S0[:], dc(EA)[:, :, DS - 1:DS].to_broadcast([P, DB, P]), ALU.mult).then_inc(s0_step, 1)
                dve.wait_ge(s0_step, h + 1)
                nc.vector.tensor_tensor(S0[:, 0:4, :], S0[:, 0:4, :], pa[2][:], ALU.add)
                nc.vector.tensor_tensor(S0[:, 4:8, :], S0[:, 4:8, :], pa[3][:], ALU.add).then_inc(s0_done, 1)
            dve.wait_ge(o_kept, HH * (NC + 1) + 1)
            step = Steps(dve, norm_step)
            sqr = v_tok
            step(nc.vector.tensor_tensor(sqr[:], o_tok[:], o_tok[:], ALU.mult))
            step(nc.vector.tensor_reduce(oss[:], sqr[:].rearrange("p t (h v) -> p (t h) v", h=HH), AX.X, ALU.add))
            nc.vector.tensor_scalar(oss[:], oss[:], 1.0 / P, EPS, ALU.mult, ALU.add).then_inc(oms_ready, 1)
            dve.wait_ge(oroot_ready, 1)
            step(nc.vector.reciprocal(ort[:], ort[:]))
            o36 = o_tok[:].rearrange("p t (h v) -> p (t h) v", h=HH)
            step(nc.vector.tensor_tensor(o36, o36, ort[:].unsqueeze(2).to_broadcast([P, NT * HH, P]), ALU.mult))
            step(nc.vector.tensor_tensor(o_tok[:], o_tok[:], normw[:].unsqueeze(1).to_broadcast([P, NT, HGW]), ALU.mult))
            dve.wait_ge(gsilu_ready, 1)
            nc.vector.tensor_tensor(o_tok[:, 0:NC, :], o_tok[:, 0:NC, :], g_tok[:, 0:NC, :], ALU.mult)
            nc.vector.tensor_tensor(o_tok[0:DT, NC, :], o_tok[0:DT, NC, :], g_tok[0:DT, NC, :], ALU.mult).then_inc(o_done, 1)

        @block.tensor
        def _(pe):
            with pe.Fori(0, HH) as h:
                wb = (NL + 3) * h
                pe.wait_ge(w_ready, wb + 2)
                pe.wait_ge(prod_ready, NC * h + 1)
                for j in range(2):
                    for c in range(4):
                        last = nc.tensor.transpose(pa[j][:, c, :], KE[:, (4 * j + c) * P:(4 * j + c + 1) * P], ident[:])
                    last.then_inc(keT_ready, 1)
                pe.wait_ge(o_kept, (NC + 1) * h + 1)
                nc.tensor.transpose(pd[0:DT, 384:512], KE[:, T:TOK], ident[:]).then_inc(keT_ready, 1)
                pe.wait_ge(w_ready, wb + NL + 3)
                pe.wait_ge(keT_kept, 3 * h + 3)
                pe.wait_ge(s0_done, h + 1)

                def products(c):
                    b = 2 * (c % 2)
                    if c >= 2:
                        pe.wait_ge(prod_ready, NC * h + c)
                    x = slice(c * P, c * P + P)
                    for l in range(NL):
                        nc.tensor.matmul(pa[b + l // 4][:, l % 4, :], W[:, l, x], W[:, l, x], start=True, stop=True)
                    nc.tensor.matmul(pa[b + 1][:, 3, :], K[:, x], Q[:, x], start=True, stop=True).then_inc(att_ready, 1)

                products(0)
                for c in range(NC):
                    if c + 1 < NC:
                        products(c + 1)
                    v = v_tok[:, c, bass.ds(h * P, P)]
                    pe.wait_ge(attT_ready, NC * h + c + 2)
                    if c >= 2:
                        pe.wait_ge(o_kept, (NC + 1) * h + c)
                    nc.tensor.matmul(po[c % 2][:, 0:P], attT[:, c % 2, :], v, start=True, stop=False)
                    pe.wait_ge(s_ready, (NC + 1) * h + c + 1)
                    nc.tensor.matmul(po[c % 2][:, 0:P], QA[:, c * P:c * P + P], S[:], start=False, stop=True).then_inc(o_ready, 1)
                    nc.tensor.matmul(ps[:, 0:P], KEt[:, c, :], v, start=True, stop=True).then_inc(st_ready, 1)
                for j in range(2):
                    nc.tensor.matmul(pd[0:DT, j * DT:(j + 1) * DT], W[:, 5 + j, T:TOK], W[:, 5 + j, T:TOK], start=True, stop=True)
                nc.tensor.matmul(pd[0:DT, 2 * DT:3 * DT], K[:, T:TOK], Q[:, T:TOK], start=True, stop=True).then_inc(attd_ready, 1)
                pe.wait_ge(attTd_ready, h + 1)
                nc.tensor.matmul(pd[:, 128:160], vd[:], attTd[:], start=True, stop=False)
                pe.wait_ge(s0_in, 16 * (h + 1))
                for b in range(DB):
                    last = nc.tensor.matmul(pd[:, 128 + DS * b:128 + DS * b + DS], S0[:, b, :], QA[:, T + DS * b:T + DS * b + DS],
                                            start=False, stop=(b == DB - 1))
                last.then_inc(oTd_ready, 1)
                pe.wait_ge(prod_ready, NC * (h + 1) + 1)
                for j in range(2):
                    last = nc.tensor.matmul(pa[2 + j][:].rearrange("p b v -> p (b v)"), KEtd[:],
                                            vsel[:, 4 * j:4 * j + 4, :].rearrange("p b v -> p (b v)"), start=True, stop=True)
                last.then_inc(std_ready, 1)
                pe.wait_ge(oTd_kept, h + 1)
                nc.tensor.transpose(pd[0:DT, 256:384], oTd[:], ident[:]).then_inc(od_ready, 1)


def sample_attention(nc, io, keep, scratch, consts_sb):
    ident = consts_sb["ident"]
    kcT_p, vc_p = keep["kcT_p"], keep["vc_p"]
    z = scratch["z_tok"]
    ROWTOK = 16
    NTL = 2 * DB

    with ExitStack() as ctx:
        sb = lambda name, shape, dt=F32: ctx.enter_context(nc.sbuf_tensor("a3_" + name, shape, dt))
        sem = lambda name: ctx.enter_context(nc.semaphore("p3_" + name))
        X = [sb(f"X{i}", [P, ROWTOK, 4, NG, DK]) for i in range(4)]
        XT = [sb(f"XT{i}", [P, 8, NG, P]) for i in range(2)]
        KsT = [sb(f"KsT{i}", [P, 4, P]) for i in range(2)]
        w1 = sb("w1", [P, 2, 2, 8, 256])
        w2 = sb("w2", [P, 2, 2, DK])
        pe_T = sb("pe_T", [P, 2, 2, 8])
        bias = sb("bias", [P, 4])
        hs = XT[0][:].rearrange("p s g c -> p (s g c)").rearrange("p (k m g n) -> p k m g n", k=2, m=2, g=NG)
        kcT = sb("kcT", [P, 256])
        vc = sb("vc", [P, 2, NG, DK])
        qblk = sb("qblk", [P, DB, 64])
        qb = sb("qb", [P, 64])
        qc = sb("qc", [P, 32])
        new_tok = XT[1][0:DT].rearrange("p s g c -> p (s g c)")[:, 0:512]
        knT = sb("knT", [P, 2, DT])
        vn = sb("vn", [DS, 2, 512])
        Kw = sb("Kw", [P, 4, 256])
        KwT = KsT[0][:].rearrange("p s c -> p (s c)")
        PwT = KsT[1][:].rearrange("p s c -> p (s c)")[:, 0:320]
        wmask = sb("wmask", [64, 2 * DS])
        PS = sb("PS", [P, 2, ROWTOK, 32])
        q_raw = PS[:].rearrange("p k s q -> p (k s q)")[:, 0:R * DT].rearrange("p (r t) -> p r t", r=R)
        Sw = PS[0:64].rearrange("p k s q -> p (k s q)")[:, 0:WIN + DS]
        col = sb("col", [P, 24])
        nmw, dw, rw, nmc, dc, rc, rs = (col[0:64, i:i + 1] for i in range(7))
        m1, m2, mm, nm = (col[0:32, i:i + 1] for i in range(8, 12))
        gates = sb("gates", [64, DB, 3])
        ob = sb("ob", [64, 2, DK])
        Pc = sb("Pc", [64, 256])
        PcT = sb("PcT", [P, 2, 64])
        PcS = sb("PcS", [P, 2, 8])
        overlap = sb("overlap", [P, 2, 64])
        imp = sb("imp", [8, 62])
        top = sb("top", [8, 8])
        sel = sb("sel", [8, 64])
        selT = sb("selT", [64, 8])
        spread = sb("spread", [64, 2, P])
        c0 = sb("c0", [P, 2, 8])
        mx = sb("mx", [P, 2, 32])
        mxx = sb("mxx", [P, 32])
        nmask = sb("nmask", [32, DS])
        sn = sb("sn", [32, DS])
        diag = sb("diag", [32, 32])
        ones = sb("ones", [P, P])
        cc = sb("cc", [P, 2, 32])
        dp = sb("dp", [P, 2, 32])
        PnT = sb("PnT", [DS, 32])
        page = sb("page", [P, NTL], I32)
        pagef = sb("pagef", [P, NTL])
        part = sb("part", [P, 1])
        idx = sb("idx", [P, NTL], U32)
        ph = [ctx.enter_context(nc.psum_tensor(f"ph{i}", [P, 512], F32)) for i in range(4)]
        tb = [ctx.enter_context(nc.psum_tensor(f"tb{i}", [P, 512], F32)) for i in range(2)]
        st = [ctx.enter_context(nc.psum_tensor(f"st{i}", [P, 512], F32)) for i in range(2)]

        (page_in, small_in, w_in1, xp_in, idx_ready, setup_step, setup_done, bias_ready, bias_kept, kn_ready, kn_kept,
         prompt_done, gates_ready) = (sem(n) for n in (
             "page_in", "small_in", "w_in", "xp_in", "idx_ready", "setup_step", "setup_done", "bias_ready", "bias_kept",
             "kn_ready", "kn_kept", "prompt_done", "gates_ready"))
        w_carry = sem("w_carry")
        x_in = [consts_sb["soft"][f"p3_x_in{i}"] for i in range(4)]
        tr_ready, s_done, proj_ready, hs_ready = (sem(n) for n in ("tr_ready", "s_done", "proj_ready", "hs_ready"))
        kept = [sem("kept_dve"), sem("kept_act")]
        (kw_in, q_ready, w_tr, w_kT, w_s, w_step, w_max, w_e, w_pT, w_pk, w_o, w_done) = (sem(n) for n in (
            "kw_in", "q_ready", "w_tr", "w_kT", "w_s", "w_step", "w_max", "w_e", "w_pT", "w_pk", "w_o", "w_done"))
        (c_kv, c_kc, c_vc, c_s, c_step, c_max, c_e, c_p, c_pT, c_pk, c_o, c_sel) = (sem(n) for n in (
            "c_kv", "c_kc", "c_vc", "c_s", "c_step", "c_max", "c_e", "c_p", "c_pT", "c_pk", "c_o", "c_sel"))
        (l_sT, l_sk, l_mask, l_step, l_mx, l_mT, l_D, l_mb, l_x, l_e, l_dp, l_nT, l_nk, pv_ready, b_done, b_out) = (
            sem(n) for n in ("l_sT", "l_sk", "l_mask", "l_step", "l_mx", "l_mT", "l_D", "l_mb", "l_x", "l_e", "l_dp",
                             "l_nT", "l_nk", "pv_ready", "b_done", "b_out"))

        block = ctx.enter_context(nc.Block())
        cache_rows = io["cache_nsa_kv"][0].rearrange("n (c t) s g d -> (n c) (t s g d)", t=ROWTOK)

        def move_pairs(who, kv, q, rows, copy):
            src = tb[who][:].rearrange("p (s u c) -> p s u c", s=2, u=2)
            for g in range(NG):
                for u in range(2):
                    last = copy(XT[kv][64 * u:64 * u + 64, 2 * q:2 * q + 2, g, 0:rows], src[64 * g:64 * g + 64, :, u, 0:rows])
            last.then_inc(kept[who], 1)

        def move_transposed(eng, who, n, e, copy):
            eng.wait_ge(tr_ready, 12 * n + e + 9)
            if 4 <= e < 8:
                if e >= 6:
                    eng.wait_ge(s_done, 4 * n + e - 5)
                copy(KsT[who][:].rearrange("p s c -> p (s c)"), tb[who][:]).then_inc(kept[who], 1)
            else:
                move_pairs(who, e // 8, e % 4, P, copy)

        @block.gpsimd
        def _(pool):
            pool.wait_ge(idx_ready, 1)
            for n in range(NTL):
                if n >= 4:
                    pool.wait_ge(pv_ready, (n - 4) // 2 + 2)
                elif n == 3:
                    pool.wait_ge(prompt_done, 1)
                nc.gpsimd.indirect_dma_start(X[n % 4][:].rearrange("p t s g d -> p (t s g d)"), None, cache_rows,
                                             bass.IndirectOffsetOnAxis(ap=idx[:, n:n + 1], axis=0)).then_inc(x_in[n % 4], 16)

        @block.sync
        def _(sp):
            flat = io["page_table"].rearrange("b (h p) -> (b h) p", h=2)
            for c in range(8):
                sp.dma_start(page[c:P:8, :], flat.rearrange("n p -> p n"), allow_slow_non_contiguous=True).then_inc(page_in, 16)
            sp.dma_start(part[:], io["c_part"]).then_inc(page_in, 16)
            sp.dma_start(X[3][0:NCP].rearrange("p t s g d -> p (t s g d)"),
                         io["kv_p"][0, 0].rearrange("(c t) s g d -> c (t s g d)", t=ROWTOK)).then_inc(xp_in, 16)
            sp.dma_start(w1[:].rearrange("p k q s h -> p (k q s) h"),
                         io["cmp_w1"][0].rearrange("k q (s u) d h -> (u d) (k q s) h", u=2)).then_inc(w_in1, 16)
            for k in range(2):
                sp.dma_start(pe_T[:, k], io["cmp_pe"][0, k].rearrange("q (s u) d -> (u d) q s", u=2),
                             allow_slow_non_contiguous=True).then_inc(w_in1, 16)
            sp.dma_start(w2[:], io["cmp_w2"][0].rearrange("k (h p) d -> p k h d", p=P)).then_inc(w_in1, 16)
            for dst, src in ((wmask, "c_wmask"), (overlap, "c_overlap"), (spread, "c_spread"), (nmask, "c_nmask")):
                sp.dma_start(dst[:], io[src]).then_inc(small_in, 16)
            for g in range(NG):
                sp.dma_start(q_raw[64 * g:64 * g + 64], scratch["q_T"][:, R * g:R * g + R, T:TOK]).then_inc(small_in, 16)
            sp.dma_start(new_tok[:], z[T:TOK, 1280:1792]).then_inc(small_in, 16)
            sp.wait_ge(setup_done, 1)
            for g in range(NG):
                for t in range(DS):
                    for k in range(3):
                        sp.dma_start(gates[48 * g + R * t:48 * g + R * t + R, :, k:k + 1],
                                     z[T:TOK, 1792 + 8 * k + 4 * g:1792 + 8 * k + 4 * g + 4].rearrange("(b t) r -> t r b", t=DS)[t].unsqueeze(2),
                                     allow_slow_non_contiguous=True).then_inc(gates_ready, 16)
            sp.sem_inc(b_out, 32)
            with sp.Fori(0, DB // 2) as i:
                for j in range(2):
                    b = 2 * i + j
                    sp.wait_ge(w_done, b + 1)
                    sp.dma_start(Kw[:], io["cache_win_kv"][0, bass.ds(b, 1)].rearrange("o (c p) s g d -> p (o c) (s g d)", p=P)
                                 ).then_inc(kw_in, 16)
                    sp.dma_start(vn[:, j, :], z[bass.ds(DS * b + T, DS), 1280:1792]).then_inc(kw_in, 16)
                    sp.wait_ge(b_done, b + 2)
                    for g in range(NG):
                        dst = scratch["o_mix"][bass.ds(DS * b + T, DS), HGW + 256 * g:HGW + 256 * g + 256]
                        sp.dma_start(dst.rearrange("t (r d) -> t r d", d=DK), ob[48 * g:48 * g + 16, 0, :]).then_inc(b_out, 16)
            sp.wait_ge(b_out, 32 * DB + 32)

        @block.scalar
        def _(act):
            act.wait_ge(gates_ready, 16 * 24)
            nc.scalar.activation(gates[:], gates[:], ACT.Sigmoid).then_inc(gates_ready, 1)
            act.wait_ge(bias_ready, 1)
            nc.scalar.copy(bias[:], st[0][:, 0:4]).then_inc(bias_kept, 1)
            for e in range(1, 8, 2):
                act.wait_ge(tr_ready, e + 1)
                move_pairs(1, e // 4, e % 4, NCP, nc.scalar.copy)
            act.wait_ge(bias_kept, 1)
            for k in range(2):
                act.wait_ge(proj_ready, k + 1)
                for m in range(2):
                    nc.scalar.activation(hs[:, k, m, :, 0:NCP - 1], ph[2 * k + m][:].rearrange("p (g n) -> p g n", g=NG)[:, :, 0:NCP - 1],
                                         ACT.Silu, bias=bias[:, 2 * k + m:2 * k + m + 1]).then_inc(hs_ready, 1)
            act.wait_ge(c_kv, 2)
            nc.scalar.copy(vc_p[0:NCP - 1].rearrange("p g d -> p (g d)"), tb[1][0:NCP - 1, 0:P]).then_inc(c_vc, 1)
            act.wait_ge(w_done, 1)
            with act.Fori(0, DB // 2) as i:
                for j in range(2):
                    b = 2 * i + j
                    act.wait_ge(w_max, b + 1)
                    nc.scalar.activation(Sw[:], Sw[:], ACT.Exp, bias=nmw, scale=SCALE, accum_out=dw).then_inc(w_e, 1)
                    for k in range(2):
                        n = 2 * b + k
                        for e in range(1, 12, 2):
                            move_transposed(act, 1, n, e, nc.scalar.copy)
                    for k in range(2):
                        act.wait_ge(proj_ready, 2 * (2 * b + 1) + k + 3)
                        for m in range(2):
                            nc.scalar.activation(hs[:, k, m, :, 0:NCD - 1],
                                                 ph[2 * k + m][:].rearrange("p (g n) -> p g n", g=NG)[:, :, 0:NCD - 1],
                                                 ACT.Silu, bias=bias[:, 2 * k + m:2 * k + m + 1]).then_inc(hs_ready, 1)
                    act.wait_ge(c_kv, 2 * b + 4)
                    nc.scalar.copy(vc[:, 0].rearrange("p g d -> p (g d)"), tb[1][:, 0:P])
                    nc.scalar.copy(vc[0:P - 1, 1].rearrange("p g d -> p (g d)"), tb[1][0:P - 1, P:2 * P]).then_inc(c_vc, 1)
                    act.wait_ge(c_max, b + 1)
                    nc.scalar.activation(Pc[:, 0:NCD - 1], tb[0][0:64, 0:NCD - 1], ACT.Exp, bias=nmc, scale=SCALE,
                                         accum_out=dc).then_inc(c_e, 1)
                    for k in range(2):
                        act.wait_ge(l_x, 2 * b + k + 1)
                        nc.scalar.activation(PS[:, k], PS[:, k], ACT.Exp, scale=SCALE).then_inc(l_e, 1)
                    nc.scalar.activation(sn[:], sn[:], ACT.Exp, bias=nm, scale=SCALE).then_inc(l_e, 1)

        @block.vector
        def _(dve):
            dve.wait_ge(page_in, 16 * 9)
            step = Steps(dve, setup_step)
            step(nc.vector.tensor_copy(pagef[:], page[:]))
            step(nc.vector.tensor_scalar(pagef[:], pagef[:], 8.0, part[:, 0:1], ALU.mult, ALU.add))
            nc.vector.tensor_copy(idx[:], pagef[:]).then_inc(idx_ready, 1)
            nc.vector.memset(gates[:], 0.0).then_inc(setup_done, 1)
            nc.vector.memset(ones[:], 1.0)
            nc.vector.memset(sel[:], 1.0)
            step(nc.vector.memset(qblk[:], 0.0))
            dve.wait_ge(small_in, 16 * 7)
            for g in range(NG):
                step(nc.vector.tensor_copy(qblk[64 * g:64 * g + 64, :, 48 * g:48 * g + 16].rearrange("p b (t r) -> p r b t", r=R),
                                           q_raw[64 * g:64 * g + 64].rearrange("p r (b t) -> p r b t", t=DS)))
            dve.wait_ge(kn_ready, 1)
            nc.vector.tensor_copy(knT[:].rearrange("p a t -> p (a t)"), st[1][:, 0:64]).then_inc(kn_kept, 1)
            for e in range(0, 8, 2):
                dve.wait_ge(tr_ready, e + 1)
                move_pairs(0, e // 4, e % 4, NCP, nc.vector.tensor_copy)
            dve.wait_ge(c_kv, 1)
            nc.vector.tensor_scalar(kcT_p[:], tb[0][0:64, 0:P].rearrange("p (g n) -> p g n", g=NG)[:, :, 0:NCP - 1],
                                    SCALE, None, ALU.mult).then_inc(c_kc, 1)
            dve.wait_ge(gates_ready, 16 * 24 + 1)
            for ahead in (b_done, pv_ready, w_done, kn_kept):
                dve.sem_inc(ahead, 1)
            with dve.Fori(0, DB // 2) as i:
                for j in range(2):
                    b = 2 * i + j
                    gate = lambda k: gates[:, bass.ds(b, 1), k:k + 1].rearrange("p o k -> p (o k)")
                    dve.wait_ge(pv_ready, b + 1)
                    qsrc = qblk[:, bass.ds(b, 1), :].rearrange("p o q -> p (o q)")
                    nc.vector.tensor_copy(qb[:], qsrc)
                    nc.vector.tensor_copy(qc[:, 0:16], qblk[:, bass.ds(b, 1), 0:16].rearrange("p o q -> p (o q)"))
                    nc.vector.tensor_copy(qc[:, 16:32], qblk[:, bass.ds(b, 1), 48:64].rearrange("p o q -> p (o q)")).then_inc(q_ready, 1)
                    dve.wait_ge(w_tr, b + 1)
                    nc.vector.tensor_copy(KwT[:], tb[0][:]).then_inc(w_kT, 1)
                    dve.wait_ge(w_s, b + 1)
                    step = Steps(dve, w_step, 3 * b)
                    nc.vector.tensor_copy(Sw[:, DS:WIN], tb[0][0:64, DS:])
                    nc.vector.tensor_tensor(Sw[:, 0:DS], tb[0][0:64, 0:DS], wmask[:, 0:DS], ALU.add)
                    step(nc.vector.tensor_tensor(Sw[:, WIN:], tb[1][0:64, 0:DS], wmask[:, DS:], ALU.add))
                    step(nc.vector.tensor_reduce(nmw, Sw[:], AX.X, ALU.max, negate=True))
                    nc.vector.tensor_scalar(nmw, nmw, SCALE, None, ALU.mult).then_inc(w_max, 1)
                    dve.wait_ge(w_pT, b + 1)
                    nc.vector.tensor_copy(PwT[:, 0:256], tb[0][:, 0:256])
                    nc.vector.tensor_copy(PwT[0:DS, 256:320], tb[0][0:DS, 256:320]).then_inc(w_pk, 1)
                    dve.wait_ge(w_e, b + 1)
                    step(nc.vector.reciprocal(rw, dw))
                    dve.wait_ge(w_o, b + 1)
                    dve.wait_ge(b_out, 32 * b + 32)
                    nc.vector.tensor_scalar(ob[:, 0, :], tb[1][0:64, 0:DK], rw, gate(2), ALU.mult, ALU.mult).then_inc(w_done, 1)
                    for k in range(2):
                        n = 2 * b + k
                        for e in range(0, 12, 2):
                            move_transposed(dve, 0, n, e, nc.vector.tensor_copy)
                            if e == 8:
                                dve.wait_ge(s_done, 4 * n + 4)
                                nc.vector.tensor_reduce(mx[:, k, :], st[k][:].rearrange("p (s q) -> p q s", q=32), AX.X, ALU.max)
                    dve.wait_ge(c_kv, 2 * b + 3)
                    nc.vector.tensor_copy(kcT[:, 0:NCD - 1], tb[0][:, 0:NCD - 1]).then_inc(c_kc, 1)
                    dve.wait_ge(c_s, b + 1)
                    step = Steps(dve, c_step, 10 * b)
                    step(nc.vector.tensor_reduce(nmc, tb[0][0:64, 0:NCD - 1], AX.X, ALU.max, negate=True))
                    nc.vector.tensor_scalar(nmc, nmc, SCALE, None, ALU.mult).then_inc(c_max, 1)
                    dve.wait_ge(c_e, b + 1)
                    step(nc.vector.reciprocal(rc, dc))
                    nc.vector.tensor_scalar(Pc[:, 0:NCD - 1], Pc[:, 0:NCD - 1], rc, None, ALU.mult).then_inc(c_p, 1)
                    dve.wait_ge(c_pT, b + 1)
                    nc.vector.tensor_copy(PcT[:, 0, :], tb[1][:, 0:64])
                    step(nc.vector.tensor_copy(PcT[0:P - 1, 1, :], tb[1][0:P - 1, 64:128]))
                    for k in range(2):
                        r = P - k
                        for g in range(NG):
                            last = nc.vector.tensor_reduce(PcS[0:r, k, 4 * g:4 * g + 4],
                                                           PcT[0:r, k, 48 * g:48 * g + 16].rearrange("p (t r) -> p t r", r=R),
                                                           AX.X, ALU.add)
                    last.then_inc(c_pk, 1)
                    dve.wait_ge(c_o, b + 1)
                    nc.vector.scalar_tensor_tensor(ob[:, 0, :], tb[0][0:64, 0:DK], gate(0), ob[:, 0, :], ALU.mult, ALU.add)
                    step(nc.vector.tensor_copy(imp[:], tb[1][0:8, 1:63]))
                    dve.sem_inc(w_carry, 1)
                    step(nc.vector.max(top[:], imp[:]))
                    dve.sem_inc(w_carry, 1)
                    step(nc.vector.match_replace(imp[:], top[:], imp[:], -1.0))
                    dve.sem_inc(w_carry, 1)
                    step(nc.vector.max(top[:], imp[:]))
                    step(nc.vector.memset(top[:, 5:8], -1.0))
                    dve.sem_inc(w_carry, 1)
                    step(nc.vector.match_replace(imp[:], top[:], imp[:], -1.0))
                    nc.vector.tensor_scalar(sel[:, 1:63], imp[:], 0.0, None, ALU.is_lt).then_inc(c_sel, 1)
                    dve.wait_ge(l_sT, b + 1)
                    nc.vector.tensor_copy(selT[:], tb[1][0:64, 0:8]).then_inc(l_sk, 1)
                    dve.wait_ge(l_mask, b + 1)
                    step2 = Steps(dve, l_step, 7 * b)
                    step2(nc.vector.tensor_scalar(c0[:].rearrange("p a q -> p (a q)"), tb[1][:, 0:16], BIG, -BIG, ALU.mult, ALU.add))
                    step2(nc.vector.tensor_tensor(mx[:].rearrange("p a (q r) -> p (a q) r", r=R), mx[:].rearrange("p a (q r) -> p (a q) r", r=R),
                                                  c0[:].rearrange("p a q -> p (a q)").unsqueeze(2).to_broadcast([P, 16, R]), ALU.add))
                    nc.vector.tensor_tensor(mxx[:], mx[:, 0, :], mx[:, 1, :], ALU.max).then_inc(l_mx, 1)
                    dve.wait_ge(l_mT, b + 1)
                    nc.vector.tensor_reduce(m1, tb[0][0:32, 0:P], AX.X, ALU.max)
                    step2(nc.vector.tensor_tensor(sn[:], tb[0][0:32, P:P + DS], nmask[:], ALU.add))
                    step2(nc.vector.tensor_reduce(m2, sn[:], AX.X, ALU.max))
                    step2(nc.vector.tensor_tensor(mm, m1, m2, ALU.max))
                    nc.vector.tensor_scalar(nm, mm, -SCALE, None, ALU.mult)
                    nc.vector.tensor_scalar(diag[:], ident[0:32, 0:32], mm, None, ALU.mult).then_inc(l_D, 1)
                    dve.wait_ge(l_mb, b + 1)
                    for k in range(2):
                        last = nc.vector.tensor_tensor(cc[:, k, :].rearrange("p (q r) -> p q r", r=R),
                                                       c0[:, k, :].unsqueeze(2).to_broadcast([P, 8, R]),
                                                       tb[1][:, 0:32].rearrange("p (q r) -> p q r", r=R), ALU.subtract)
                    step2(last)
                    for k in range(2):
                        nc.vector.tensor_tensor(PS[:, k], st[k][:].rearrange("p (s q) -> p s q", q=32),
                                                cc[:, k, :].unsqueeze(1).to_broadcast([P, ROWTOK, 32]), ALU.add).then_inc(l_x, 1)
                    dve.wait_ge(l_nT, b + 1)
                    nc.vector.tensor_copy(PnT[:], tb[0][0:DS, 0:32]).then_inc(l_nk, 1)
                    for k in range(2):
                        last = nc.vector.tensor_reduce(dp[:, k, :], PS[:, k].rearrange("p s q -> p q s"), AX.X, ALU.add)
                    last.then_inc(l_dp, 1)
                    dve.wait_ge(pv_ready, b + 2)
                    step2(nc.vector.reciprocal(rs, tb[1][0:64, DK:DK + 1]))
                    step(nc.vector.tensor_scalar(rs, rs, gate(1), None, ALU.mult))
                    nc.vector.scalar_tensor_tensor(ob[:, 0, :], tb[1][0:64, 0:DK], rs, ob[:, 0, :], ALU.mult, ALU.add).then_inc(b_done, 1)
                    assert step.n == 10 and step2.n == 7

        @block.tensor
        def _(pe):
            pe.wait_ge(w_in1, 64)
            for k in range(2):
                for m in range(2):
                    for q in range(2):
                        for s in range(8):
                            last = nc.tensor.matmul(st[0][:, 2 * k + m:2 * k + m + 1], w1[:, k, q, s, m * P:(m + 1) * P],
                                                    pe_T[:, k, q, s:s + 1], start=(q + s == 0), stop=(q + s == 8))
            last.then_inc(bias_ready, 1)
            pe.wait_ge(small_in, 16 * 7)
            for a in range(2):
                last = nc.tensor.transpose(st[1][:, DT * a:DT * a + DT], new_tok[:, 256 * a:256 * a + P], ident[0:DT, 0:DT])
            last.then_inc(kn_ready, 1)

            def transposes(x, bank, slot, q, rows):
                for s in range(4):
                    last = nc.tensor.transpose(tb[bank][:, s * P:s * P + rows], x[0:rows, 4 * q + s, slot].rearrange("p g d -> p (g d)"),
                                               ident[0:rows, 0:rows])
                last.then_inc(tr_ready, 1)

            def project(k, half, rows, between=None):
                for m in range(2):
                    out = ph[2 * k + m][:].rearrange("p (g n) -> p g n", g=NG)
                    for q in range(2):
                        if between:
                            between(2 * m + q)
                        if half is None:
                            dst, src, w = 0, q, rows - 1
                        elif half == 0:
                            dst, src, w = 0, q, P - q
                        else:
                            dst, src, w = P - q, 0, P
                        for s in range(8):
                            last = nc.tensor.matmul(out[:, :, dst:dst + w], w1[:, k, q, s, m * P:(m + 1) * P],
                                                    XT[k][:, s, :, src:src + w], start=(not half and q + s == 0),
                                                    stop=(q == 1 and s == 7), skip_group_check=True)
                last.then_inc(proj_ready, 1)

            def blocks(n_blocks, count, prev):
                pe.wait_ge(hs_ready, prev + 2)
                for g in range(NG):
                    out = tb[0][0:64, 64 * g:64 * g + n_blocks] if count == 1 else tb[0][64 * g:64 * g + 64, 0:n_blocks]
                    for m in range(2):
                        last = nc.tensor.matmul(out, w2[:, 0, m, :], hs[:, 0, m, g, 0:n_blocks],
                                                start=(m == 0), stop=(m == 1))
                last.then_inc(c_kv, 1)
                pe.wait_ge(hs_ready, prev + 4)
                for t in range(count):
                    w = min(P, n_blocks - t * P)
                    for g in range(NG):
                        for m in range(2):
                            last = nc.tensor.matmul(tb[1][0:w, P * t + DK * g:P * t + DK * g + DK], hs[:, 1, m, g, t * P:t * P + w],
                                                    w2[:, 1, m, :], start=(m == 0), stop=(m == 1))
                last.then_inc(c_kv, 1)

            pe.wait_ge(xp_in, 16)
            for e in range(8):
                if e >= 2:
                    pe.wait_ge(kept[e % 2], e // 2)
                transposes(X[3], e % 2, e // 4, e % 4, NCP)
            pe.wait_ge(kept[0], 4)
            pe.wait_ge(kept[1], 4)
            for k in range(2):
                project(k, None, NCP)
            blocks(NCP - 1, 1, 0)
            pe.wait_ge(c_kc, 1)
            pe.wait_ge(c_vc, 1)
            pe.sem_inc(prompt_done, 1)
            pe.wait_ge(kn_kept, 2)
            with pe.Fori(0, DB // 2) as i:
                for j in range(2):
                    b = 2 * i + j
                    newk = lambda a: knT[:, a, bass.ds(DS * b, DS)]
                    pe.wait_ge(b_done, b + 1)
                    pe.wait_ge(kw_in, 32 * (b + 1))
                    for c in range(4):
                        last = nc.tensor.transpose(tb[0][:, c * P:(c + 1) * P], Kw[:, c, 0:P], ident[:])
                    last.then_inc(w_tr, 1)
                    pe.wait_ge(w_kT, b + 1)
                    nc.tensor.matmul(tb[0][0:64, :], qb[:], KwT[:], start=True, stop=True)
                    nc.tensor.matmul(tb[1][0:64, 0:DS], qb[:], newk(1), start=True, stop=True).then_inc(w_s, 1)
                    pe.wait_ge(w_e, b + 1)
                    pe.sem_inc(w_carry, 1)
                    for c in range(4):
                        nc.tensor.transpose(tb[0][:, c * 64:(c + 1) * 64], Sw[:, c * P:(c + 1) * P], ident[0:64, 0:64])
                    nc.tensor.transpose(tb[0][0:DS, 256:320], Sw[:, WIN:], ident[0:64, 0:64]).then_inc(w_pT, 1)
                    pe.wait_ge(w_pk, b + 1)
                    for g in range(NG):
                        out = tb[1][32 * g:32 * g + 32, 0:DK]
                        for c in range(4):
                            nc.tensor.matmul(out, PwT[:, 64 * c + 32 * g:64 * c + 32 * g + 32], Kw[:, c, P + DK * g:P + DK * g + DK],
                                             start=(c == 0), stop=False)
                        last = nc.tensor.matmul(out, PwT[0:DS, 256 + 32 * g:288 + 32 * g],
                                                vn[:, j, 384 + DK * g:384 + DK * g + DK],
                                                start=False, stop=True)
                    last.then_inc(w_o, 1)
                    pe.wait_ge(w_done, b + 2)
                    for k in range(2):
                        x = X[2 * j + k]
                        n = 2 * b + k
                        pe.wait_ge(x_in[2 * j + k], 16 * (i + 1))

                        def scores(e):
                            pe.wait_ge(kept[e % 2], 6 * n + e // 2 + 5)
                            for s in range(4):
                                o = (4 * (e - 4) + s) * 32
                                last = nc.tensor.matmul(st[k][:, o:o + 32], KsT[e % 2][:, s, :], qc[:], start=True, stop=True)
                            last.then_inc(s_done, 1)

                        def turn(e):
                            pe.wait_ge(kept[e % 2], 6 * n + e // 2 + 4)
                            transposes(x, e % 2, (0, 2, 1)[e // 4], e % 4, P)

                        for e in range(8):
                            turn(e)
                            if e >= 5:
                                scores(e - 1)
                        scores(7)
                        project(0, k, P, between=lambda q: turn(8 + q))
                        for w in range(2):
                            pe.wait_ge(kept[w], 6 * n + 10)
                        project(1, k, P)
                    blocks(NCD - 1, 2, 4 * b + 4)
                    pe.wait_ge(c_kc, b + 2)
                    nc.tensor.matmul(tb[0][0:64, 0:NCD - 1], qb[:], kcT[:, 0:NCD - 1], start=True, stop=True).then_inc(c_s, 1)
                    pe.wait_ge(c_p, b + 1)
                    pe.wait_ge(c_vc, b + 2)
                    pe.sem_inc(w_carry, 1)
                    for t in range(2):
                        w = P - t
                        last = nc.tensor.transpose(tb[1][0:w, 64 * t:64 * t + 64], Pc[:, t * P:t * P + w], ident[0:64, 0:64])
                    last.then_inc(c_pT, 1)
                    pe.wait_ge(c_pk, b + 1)
                    for g in range(NG):
                        for t in range(2):
                            w = P - t
                            nc.tensor.matmul(tb[0][32 * g:32 * g + 32, 0:DK], PcT[0:w, t, 32 * g:32 * g + 32], vc[0:w, t, g, :],
                                             start=(t == 0), stop=(t == 1))
                    for t in range(2):
                        w = P - t
                        last = nc.tensor.matmul(tb[1][0:8, 0:64], PcS[0:w, t, :], overlap[0:w, t, :], start=(t == 0), stop=(t == 1))
                    last.then_inc(c_o, 1)
                    pe.wait_ge(c_sel, b + 1)
                    pe.sem_inc(w_carry, 1)
                    nc.tensor.transpose(tb[1][0:64, 0:8], sel[:], ident[0:8, 0:8]).then_inc(l_sT, 1)
                    pe.wait_ge(l_sk, b + 1)
                    for k in range(2):
                        last = nc.tensor.matmul(tb[1][:, 8 * k:8 * k + 8], spread[:, k, :], selT[:], start=True, stop=True)
                    last.then_inc(l_mask, 1)
                    pe.wait_ge(l_mx, b + 1)
                    nc.tensor.transpose(tb[0][0:32, 0:P], mxx[:], ident[:])
                    nc.tensor.matmul(tb[0][0:32, P:P + DS], qc[:], newk(0), start=True, stop=True).then_inc(l_mT, 1)
                    pe.wait_ge(l_D, b + 1)
                    nc.tensor.matmul(tb[1][:, 0:32], ones[0:32, :], diag[:], start=True, stop=True).then_inc(l_mb, 1)
                    pe.wait_ge(l_e, 3 * b + 3)
                    pe.sem_inc(w_carry, 1)
                    nc.tensor.transpose(tb[0][0:DS, 0:32], sn[:], ident[0:32, 0:32]).then_inc(l_nT, 1)
                    pe.wait_ge(l_nk, b + 1)
                    pe.wait_ge(l_dp, b + 1)
                    for g in range(NG):
                        den = tb[1][32 * g:32 * g + 32, DK:DK + 1]
                        for k in range(2):
                            nc.tensor.matmul(den, dp[:, k, :], ones[:, 0:1], start=(k == 0), stop=False)
                        nc.tensor.matmul(den, PnT[:], ones[0:DS, 0:1], start=False, stop=True)
                        out = tb[1][32 * g:32 * g + 32, 0:DK]
                        for k in range(2):
                            for s in range(ROWTOK):
                                nc.tensor.matmul(out, PS[:, k, s, :], X[2 * j + k][:, s, 3, g, :], start=(k + s == 0), stop=False)
                        last = nc.tensor.matmul(out, PnT[:], vn[:, j, 128 + DK * g:128 + DK * g + DK],
                                                start=False, stop=True)
                    last.then_inc(pv_ready, 1)


def prompt_attention(nc, io, keep, scratch, consts_sb):
    ident = consts_sb["ident"]
    kcT_p, vc_p = keep["kcT_p"], keep["vc_p"]
    z = scratch["z_tok"]
    NQ = T // P
    NBK = NCP - 1
    CMP, SLC, WND = 0, 1, 2

    class Item:
        pass

    items, groups, kinds = [], [], []
    for j in range(2):
        for kind in (SLC, WND, CMP):
            kinds.append((j, kind))
            for qt in range(NQ) if kind != CMP else [0]:
                it = Item()
                it.j, it.kind, it.qt, it.n, it.c = j, kind, qt, len(items), len(kinds) - 1
                it.k0 = max(0, qt - 4) if kind == WND else 0
                it.blocks = list(range(NQ)) if kind == CMP else list(range(it.k0, qt + 1))
                it.groups = []
                for a in range(0, len(it.blocks), 4):
                    it.groups.append(len(groups))
                    groups.append((it, a, min(4, len(it.blocks) - a)))
                it.last = kind == CMP or qt == NQ - 1
                items.append(it)
    NI, NGR, NKD = len(items), len(groups), len(kinds)
    assert NI % 2 == 0 and NGR % 2 == 0 and NKD % 2 == 0

    with ExitStack() as ctx:
        sb = lambda name, shape: ctx.enter_context(nc.sbuf_tensor("a4_" + name, shape, F32))
        sem = lambda name: ctx.enter_context(nc.semaphore("p4_" + name))
        kv = sb("kv", [P, NQ, 512])
        KT = sb("KT", [64, 2, NG, T])
        q = sb("q", [64, 2, T])
        Pr = [sb(f"Pr{i}", [P, T]) for i in range(2)]
        PT = [sb(f"PT{i}", [P, 4, P]) for i in range(2)]
        nm = sb("nm", [P, NI])
        nmc = sb("nmc", [P, 2, NQ])
        den = sb("den", [P, NKD, NQ])
        gates = sb("gates", [P, NQ, 24])
        causal = sb("causal", [P, P])
        older = sb("older", [P, P])
        cmask = sb("cmask", [P, NQ, NBK])
        osum = sb("osum", [P, NQ, DK])
        o = sb("o", [P, NQ, NH * DK])
        ps = [ctx.enter_context(nc.psum_tensor(f"s{i}", [P, T], F32)) for i in range(2)]
        pt = [ctx.enter_context(nc.psum_tensor(f"pt{i}", [P, 4, P], F32)) for i in range(2)]
        pv = [ctx.enter_context(nc.psum_tensor(f"pv{i}", [P, NQ, DK], F32)) for i in range(2)]

        kv_in, small_in, kT_ready, q_in, gates_ready = (sem(n) for n in ("kv_in", "small_in", "kT_ready", "q_in0", "gates_ready"))
        q_in = [q_in, sem("q_in1")]
        kT_kept = [sem("kT_kept_dve"), sem("kT_kept_act")]
        s_ready, masked, cmp_step, max_ready, e_ready, t_ready, pv_ready, kind_step, kind_done, o_out, den_ready = (sem(n) for n in (
            "s_ready", "masked", "cmp_step", "max_ready", "e_ready", "t_ready", "pv_ready", "kind_step", "kind_done", "o_out",
            "den_ready"))
        heads_done, w_carry = sem("heads_done"), sem("w_carry")
        kept = [sem("kept_dve"), sem("kept_act")]

        block = ctx.enter_context(nc.Block())

        def move_group(eng, i, k, copy):
            it, a, n = groups[k]
            rows = NBK if it.kind == CMP else P
            eng.wait_ge(pv_ready, NGR * i + k + 1)
            eng.wait_ge(t_ready, NGR * i + k + 1)
            copy(PT[k % 2][0:rows, 0:n, :], pt[k % 2][0:rows, 0:n, :]).then_inc(kept[k % 2], 1)

        def move_keys(eng, e, copy):
            a, g, half = e // 4, e // 2 % 2, e % 2
            eng.wait_ge(kT_ready, e + 1)
            copy(KT[:, a, g, 512 * half:512 * half + 512], pt[e % 2][0:64].rearrange("p b c -> p (b c)")).then_inc(kT_kept[e % 2], 1)

        @block.sync
        def _(sp):
            sp.dma_start(kv[:], z[0:T, 1280:1792].rearrange("(t p) n -> p t n", p=P)).then_inc(kv_in, 16)
            for dst, src in ((causal, "c_causal"), (older, "c_older"), (cmask, "c_cmask")):
                sp.dma_start(dst[:], io[src]).then_inc(small_in, 16)
            sp.dma_start(gates[:], z[0:T, 1792:1816].rearrange("(t p) n -> p t n", p=P)).then_inc(small_in, 16)
            with sp.Fori(0, NH // 2) as i:
                for j in range(2):
                    sp.wait_ge(heads_done, 2 * i + j + 1)
                    sp.dma_start(q[:, j, :], scratch["q_T"][:, bass.ds(2 * i + j, 1), 0:T].rearrange("p o t -> p (o t)")).then_inc(q_in[j], 16)
            sp.wait_ge(kind_done, NKD * (NH // 2) + 2)
            sp.dma_start(scratch["o_mix"][0:T, HGW:D].rearrange("(t p) n -> p t n", p=P), o[:]).then_inc(o_out, 16)
            sp.wait_ge(o_out, 16)

        @block.scalar
        def _(act):
            act.wait_ge(small_in, 16 * 4)
            nc.scalar.activation(gates[:], gates[:], ACT.Sigmoid).then_inc(gates_ready, 1)
            for e in range(1, 8, 2):
                move_keys(act, e, lambda o_, i_: nc.scalar.mul(o_, i_, SCALE))
            act.wait_ge(kT_kept[1], 4)
            act.sem_inc(e_ready, 2)
            act.sem_inc(kept[1], 1)
            with act.Fori(0, NH // 2) as i:

                def probabilities(it):
                    act.wait_ge(max_ready, NI * i + it.n + 1)
                    p = Pr[it.n % 2]
                    if it.kind == CMP:
                        nc.scalar.activation(p[:, 0:NQ * NBK], p[:, 0:NQ * NBK], ACT.Exp).then_inc(e_ready, 1)
                    else:
                        w = len(it.blocks) * P
                        nc.scalar.activation(p[:, 0:w], ps[it.n % 2][:, 0:w], ACT.Exp, bias=nm[:, it.n:it.n + 1],
                                             accum_out=den[:, it.c, it.qt:it.qt + 1]).then_inc(e_ready, 1)

                probabilities(items[0])
                for it in items:
                    if it.n + 1 < NI:
                        probabilities(items[it.n + 1])
                    for k in it.groups:
                        if k % 2 == 1:
                            move_group(act, i, k, nc.scalar.copy)

        @block.vector
        def _(dve):
            for e in range(0, 8, 2):
                move_keys(dve, e, lambda o_, i_: nc.vector.tensor_scalar(o_, i_, SCALE, None, ALU.mult))
            dve.wait_ge(small_in, 16 * 4)
            dve.wait_ge(gates_ready, 1)
            dve.wait_ge(kT_kept[0], 4)
            dve.sem_inc(kept[0], 1)
            dve.sem_inc(kind_done, 2)
            dve.sem_inc(heads_done, 2)
            with dve.Fori(0, NH // 2) as i:
                n_masked, n_cmp, n_kind = NI - 2, 8, 3 * NKD
                at = {"masked": 0}
                cstep = Steps(dve, cmp_step, n_cmp * i)
                kstep = Steps(dve, kind_step, n_kind * i)

                def maximum(it):
                    s = ps[it.n % 2]
                    dve.wait_ge(s_ready, NI * i + it.n + 1)
                    if it.kind == CMP:
                        s3 = s[:, 0:NQ * NBK].rearrange("p (t n) -> p t n", t=NQ)
                        cstep(nc.vector.tensor_tensor(s3, s3, cmask[:], ALU.add))
                        cstep(nc.vector.tensor_reduce(nmc[:, it.j, :], s3, AX.X, ALU.max))
                        dve.sem_inc(heads_done, 1)
                        cstep(nc.vector.tensor_scalar(nmc[:, it.j, :], nmc[:, it.j, :], -BIG / 1e10, None, ALU.max))
                        nc.vector.tensor_tensor(Pr[it.n % 2][:, 0:NQ * NBK].rearrange("p (t n) -> p t n", t=NQ), s3,
                                                nmc[:, it.j, :].unsqueeze(2).to_broadcast([P, NQ, NBK]), ALU.subtract).then_inc(max_ready, 1)
                        return
                    w = len(it.blocks) * P
                    if it.kind == WND and len(it.blocks) == 5:
                        nc.vector.tensor_tensor(s[:, 0:P], s[:, 0:P], older[:], ALU.add)
                    nc.vector.tensor_tensor(s[:, w - P:w], s[:, w - P:w], causal[:], ALU.add).then_inc(masked, 1)
                    at["masked"] += 1
                    dve.wait_ge(masked, n_masked * i + at["masked"])
                    nc.vector.tensor_reduce(nm[:, it.n:it.n + 1], s[:, 0:w], AX.X, ALU.max, negate=True).then_inc(max_ready, 1)

                def finish_kind(it):
                    h = 2 * i + it.j
                    d = den[:, it.c, :]
                    dve.wait_ge(e_ready, NI * i + it.n + 3)
                    if it.kind == CMP:
                        dve.wait_ge(den_ready, 2 * i + it.j + 1)
                        cstep(nc.vector.tensor_scalar(d, d, 1e-30, None, ALU.max))
                    kstep(nc.vector.reciprocal(d, d))
                    gate = gates[:, :, bass.ds(h + 8 * it.kind, 1)].rearrange("p t o -> p (t o)")
                    kstep(nc.vector.tensor_tensor(d, d, gate, ALU.mult))
                    dve.wait_ge(pv_ready, NGR * i + it.groups[-1] + 3)
                    dst = o[:, :, bass.ds(DK * h, DK)]
                    rs = d.unsqueeze(2).to_broadcast([P, NQ, DK])
                    if it.kind == SLC:
                        kstep(nc.vector.tensor_tensor(dst, pv[it.c % 2][:], rs, ALU.mult))
                        dve.sem_inc(kind_done, 1)
                    else:
                        kstep(nc.vector.tensor_tensor(osum[:], pv[it.c % 2][:], rs, ALU.mult))
                        nc.vector.tensor_tensor(dst, dst, osum[:], ALU.add).then_inc(kind_done, 1)

                maximum(items[0])
                pending = None
                for it in items:
                    if it.n + 1 < NI:
                        maximum(items[it.n + 1])
                    if it.kind == CMP:
                        dve.wait_ge(e_ready, NI * i + it.n + 3)
                        nc.vector.tensor_reduce(den[:, it.c, :], Pr[it.n % 2][:, 0:NQ * NBK].rearrange("p (t n) -> p t n", t=NQ),
                                                AX.X, ALU.add).then_inc(den_ready, 1)
                    for k in it.groups:
                        if k % 2 == 0:
                            move_group(dve, i, k, nc.vector.tensor_copy)
                    if pending is not None:
                        finish_kind(pending)
                    pending = it if it.last else None
                finish_kind(pending)
                assert cstep.n == n_cmp and kstep.n == n_kind and at["masked"] == n_masked

        @block.tensor
        def _(pe):
            pe.wait_ge(kv_in, 16)
            for e in range(8):
                a, g, half = e // 4, e // 2 % 2, e % 2
                if e >= 2:
                    pe.wait_ge(kT_kept[e % 2], e // 2)
                for b in range(4):
                    last = nc.tensor.transpose(pt[e % 2][0:64, b, :], kv[:, 4 * half + b, 256 * a + DK * g:256 * a + DK * g + DK], ident[:])
                last.then_inc(kT_ready, 1)
            pe.wait_ge(kT_kept[0], 4)
            pe.wait_ge(kT_kept[1], 4)
            pe.sem_inc(pv_ready, 2)
            with pe.Fori(0, NH // 2) as i:
                grp = i // 2

                def scores(it):
                    s = ps[it.n % 2]
                    pe.wait_ge(e_ready, NI * i + it.n + 1)
                    if it.qt == 0 and it.kind == SLC:
                        pe.wait_ge(q_in[it.j], 16 * i + 16)
                    pe.sem_inc(w_carry, 1)
                    if it.kind == CMP:
                        for t in range(NQ):
                            last = nc.tensor.matmul(s[:, NBK * t:NBK * t + NBK], q[:, it.j, t * P:t * P + P],
                                                    kcT_p[:, bass.ds(grp, 1), :].rearrange("p o n -> p (o n)"), start=True, stop=True)
                    else:
                        w = len(it.blocks) * P
                        for c in range(0, w, 512):
                            n = min(512, w - c)
                            keys = KT[:, it.kind - 1, bass.ds(grp, 1), it.k0 * P + c:it.k0 * P + c + n].rearrange("p o n -> p (o n)")
                            last = nc.tensor.matmul(s[:, c:c + n], q[:, it.j, it.qt * P:it.qt * P + P], keys, start=True, stop=True)
                    last.then_inc(s_ready, 1)

                def turn(k):
                    it, a, n = groups[k]
                    if a == 0:
                        pe.wait_ge(e_ready, NI * i + it.n + 3)
                    pe.wait_ge(kept[k % 2], NGR // 2 * i + k // 2 + 1)
                    if it.kind == CMP:
                        pe.sem_inc(w_carry, 1)
                    for b in range(n):
                        if it.kind == CMP:
                            last = nc.tensor.transpose(pt[k % 2][0:NBK, b, :], Pr[it.n % 2][:, NBK * (a + b):NBK * (a + b) + NBK], ident[:])
                        else:
                            last = nc.tensor.transpose(pt[k % 2][:, b, :], Pr[it.n % 2][:, P * (a + b):P * (a + b) + P], ident[:])
                    last.then_inc(t_ready, 1)

                def values(k):
                    it, a, n = groups[k]
                    if it.qt == 0 and a == 0:
                        pe.wait_ge(kind_done, NKD * i + it.c + 1)
                    pe.wait_ge(kept[k % 2], NGR // 2 * i + k // 2 + 2)
                    if it.kind == CMP:
                        pe.sem_inc(w_carry, 1)
                    for b in range(n):
                        if it.kind == CMP:
                            last = nc.tensor.matmul(pv[it.c % 2][:, a + b, :], PT[k % 2][0:NBK, b, :],
                                                    vc_p[:, bass.ds(grp, 1), :].rearrange("p o d -> p (o d)"), start=True, stop=True)
                        else:
                            last = nc.tensor.matmul(pv[it.c % 2][:, it.qt, :], PT[k % 2][:, b, :],
                                                    kv[:, it.blocks[a + b], bass.ds(grp * DK + (256 * (it.kind - 1) + P), DK)],
                                                    start=(a + b == 0), stop=(a + b == len(it.blocks) - 1))
                    last.then_inc(pv_ready, 1)

                scores(items[0])
                for it in items:
                    if it.n + 1 < NI:
                        scores(items[it.n + 1])
                    for k in it.groups:
                        turn(k)
                        if k > 0:
                            values(k - 1)
                values(NGR - 1)


def rows_of(t):
    return P if t < NT - 1 else DT


def project_out(nc, io, keep, scratch, consts_sb):
    ident, hT = consts_sb["ident"], keep["hT"]
    with ExitStack() as ctx:
        sb = lambda name, shape: ctx.enter_context(nc.sbuf_tensor("a5_" + name, shape, F32))
        sem = lambda name: ctx.enter_context(nc.semaphore("p5_" + name))
        w = sb("w", [P, KD, D])
        o = sb("o", [P, 3, D])
        x = sb("x", [P, 3, D])
        x1 = sb("x1", [P, 2, D])
        xs = sb("xs", [P, 2, D])
        oT = sb("oT", [P, 2, KD, P])
        sq = sb("sq", [P, D])
        ss, rt, g2 = sb("ss", [P, NT]), sb("rt", [P, NT]), sb("g2", [P, KD])
        to = [ctx.enter_context(nc.psum_tensor(f"to{i}", [P, 4, P], F32)) for i in range(2)]
        py = [ctx.enter_context(nc.psum_tensor(f"py{i}", [P, 512], F32)) for i in range(4)]
        th = [ctx.enter_context(nc.psum_tensor(f"th{i}", [P, 4, P], F32)) for i in range(2)]
        soft = consts_sb["soft"]
        w_in, g2_in, x1_out = soft["p5_w_in"], sem("g2_in"), [soft["p5_x1_out0"], soft["p5_x1_out1"]]
        o_in = [sem(f"o_in{i}") for i in range(3)]
        (oT_ready, oT_kept, y_ready, x1_ready, ss_ready, ms_ready, root_ready, rstd_ready, xs_ready, hT_ready, hT_kept) = (
            sem(n) for n in ("oT_ready", "oT_kept", "y_ready", "x1_ready", "ss_ready", "ms_ready", "root_ready", "rstd_ready",
                             "xs_ready", "hT_ready", "hT_kept"))
        block = ctx.enter_context(nc.Block())

        @block.sync
        def _(sp):
            sp.dma_start(g2[:], io["norm2"].rearrange("a (k p) -> p (a k)", p=P), allow_slow_non_contiguous=True).then_inc(g2_in, 16)
            for t in range(NT):
                r = rows_of(t)
                if t >= 3:
                    sp.wait_ge(x1_ready, 2 * (t - 2))
                sp.dma_start(o[0:r, t % 3, :], scratch["o_mix"][t * P:t * P + r, :]).then_inc(o_in[t % 3], 16)
                src = io["x_prompt"][0, t * P:(t + 1) * P, :] if t < NT - 1 else io["x_sample"].rearrange("b t d -> (b t) d")
                sp.dma_start(x[0:r, t % 3, :], src).then_inc(o_in[t % 3], 16)

        @block.gpsimd
        def _(pool):
            pool.dma_start(w[:], io["w_out"][0].rearrange("(k p) n -> p k n", p=P)).then_inc(w_in, 16)
            for t in range(NT):
                r = rows_of(t)
                pool.wait_ge(x1_ready, 2 * t + 2)
                pool.dma_start(scratch["x1"][t * P:t * P + r, :], x1[0:r, t % 2, :]).then_inc(x1_out[t % 2], 16)
            pool.wait_ge(x1_out[0], 16 * 5)
            pool.wait_ge(x1_out[1], 16 * 4)

        @block.scalar
        def _(act):
            for t in range(NT):
                r = rows_of(t)
                for h in range(2):
                    act.wait_ge(oT_ready, 2 * t + h + 1)
                    if h == 0 and t >= 2:
                        act.wait_ge(y_ready, 2 * (t - 1))
                    nc.scalar.copy(oT[:, t % 2, 4 * h:4 * h + 4, 0:r], to[h][:, :, 0:r]).then_inc(oT_kept, 1)
                act.wait_ge(x1_ready, 2 * t + 2)
                if t >= 1:
                    act.wait_ge(ss_ready, t)
                nc.scalar.activation(sq[0:r, :], x1[0:r, t % 2, :], ACT.Square, accum_out=ss[0:r, t:t + 1]).then_inc(ss_ready, 1)
                act.wait_ge(ms_ready, t + 1)
                nc.scalar.activation(rt[0:r, t:t + 1], ss[0:r, t:t + 1], ACT.Sqrt).then_inc(root_ready, 1)

        @block.vector
        def _(dve):
            dve.wait_ge(g2_in, 16)

            def norm(t):
                r = rows_of(t)
                dve.wait_ge(ss_ready, t + 1)
                nc.vector.tensor_scalar(ss[0:r, t:t + 1], ss[0:r, t:t + 1], 1.0 / D, EPS, ALU.mult, ALU.add).then_inc(ms_ready, 1)
                dve.wait_ge(root_ready, t + 1)
                nc.vector.reciprocal(rt[0:r, t:t + 1], rt[0:r, t:t + 1]).then_inc(rstd_ready, 1)
                dve.wait_ge(rstd_ready, t + 1)
                if t >= 2:
                    dve.wait_ge(hT_ready, 2 * (t - 1))
                nc.vector.tensor_scalar(xs[0:r, t % 2, :], x1[0:r, t % 2, :], rt[0:r, t:t + 1], None, ALU.mult).then_inc(xs_ready, 1)

            def keep_hT(t):
                r = rows_of(t)
                for h in range(2):
                    dve.wait_ge(hT_ready, 2 * t + h + 1)
                    nc.vector.tensor_tensor(hT[:, 4 * h:4 * h + 4, t * P:t * P + r], th[h][:, :, 0:r],
                                            g2[:, 4 * h:4 * h + 4].unsqueeze(2).to_broadcast([P, 4, r]), ALU.mult).then_inc(hT_kept, 1)

            for t in range(NT):
                r = rows_of(t)
                dve.wait_ge(o_in[t % 3], 32 * (t // 3 + 1))
                for h in range(2):
                    if h == 0 and t >= 2:
                        dve.wait_ge(x1_out[t % 2], 16 * (t // 2))
                        dve.wait_ge(xs_ready, t - 1)
                    dve.wait_ge(y_ready, 2 * t + h + 1)
                    nc.vector.tensor_tensor(x1[0:r, t % 2, 512 * h:512 * h + 512], py[2 * (t % 2) + h][0:r, :],
                                            x[0:r, t % 3, 512 * h:512 * h + 512], ALU.add).then_inc(x1_ready, 1)
                norm(t)
                if t >= 1:
                    keep_hT(t - 1)
            keep_hT(NT - 1)

        @block.tensor
        def _(pe):
            def turn_o(t):
                r = rows_of(t)
                pe.wait_ge(o_in[t % 3], 32 * (t // 3 + 1))
                for h in range(2):
                    if t >= 1:
                        pe.wait_ge(oT_kept, 2 * (t - 1) + h + 1)
                    for k in range(4):
                        last = nc.tensor.transpose(to[h][:, k, 0:r], o[0:r, t % 3, (4 * h + k) * P:(4 * h + k + 1) * P], ident[0:r, 0:r])
                    last.then_inc(oT_ready, 1)

            def turn_h(t):
                r = rows_of(t)
                pe.wait_ge(xs_ready, t + 1)
                for h in range(2):
                    if t >= 1:
                        pe.wait_ge(hT_kept, 2 * (t - 1) + h + 1)
                    for k in range(4):
                        last = nc.tensor.transpose(th[h][:, k, 0:r], xs[0:r, t % 2, (4 * h + k) * P:(4 * h + k + 1) * P], ident[0:r, 0:r])
                    last.then_inc(hT_ready, 1)

            turn_o(0)
            pe.wait_ge(w_in, 16)
            for t in range(NT):
                r = rows_of(t)
                if t + 1 < NT:
                    turn_o(t + 1)
                pe.wait_ge(oT_kept, 2 * t + 2)
                for h in range(2):
                    if t >= 2:
                        pe.wait_ge(x1_ready, 2 * (t - 2) + h + 1)
                    for k in range(KD):
                        last = nc.tensor.matmul(py[2 * (t % 2) + h][0:r, :], oT[:, t % 2, k, 0:r], w[:, k, 512 * h:512 * h + 512],
                                                start=(k == 0), stop=(k == KD - 1))
                    last.then_inc(y_ready, 1)
                if t >= 1:
                    turn_h(t - 1)
            turn_h(NT - 1)


def feed_forward(nc, io, keep, scratch, consts_sb):
    ident, hy = consts_sb["ident"], keep["hy"]
    hT = keep["hT"]
    y = hy[:].rearrange("p (t n) -> p t n", t=NT)
    NF = FF // P
    UW = 2 + T + DB * (2 + DS)
    PARTS = [(0, 352), (352, 352), (704, 352)]
    QW = D // 4
    with ExitStack() as ctx:
        sb = lambda name, shape: ctx.enter_context(nc.sbuf_tensor("a6_" + name, shape, F32))
        sem = lambda name: ctx.enter_context(nc.semaphore("p6_" + name))
        aT = sb("aT", [P, NF, TOK])
        wd = sb("wd", [P, 2, NF, QW])
        wu = wd[:, 1].rearrange("p f n -> p (f n)")[:, 0:2 * 2 * KD * P].rearrange("p (j a k n) -> p j a k n", j=2, a=2, k=KD)
        U = [sb(f"U{i}", [P, UW]) for i in range(2)]
        C = sb("C", [P, TOK])
        flat = aT[:].rearrange("p f t -> p (f t)")
        small, past = flat[0:4, 0:FF], flat[0:2 * DB, FF:2 * FF]
        small_tail = sb("tail_tok", [2 * DB + 2, FF])
        cw = sb("cw", [P, NF, 4])
        pastT = sb("pastT", [P, NF, 2 * DB])
        tails = sb("tails", [P, NF, 2 * DB + 2])
        cwj = sb("cwj", [P, 2, 4])
        ss, rt = sb("ss", [P, NT]), sb("rt", [P, NT])
        bank = [ctx.enter_context(nc.psum_tensor(f"f{i}", [P, 512], F32)) for i in range(8)]
        (small_in, cw_ready, cw_kept, past_kept, wd_free, u_ready, v_ready, u_kept, c_step, c_ready, g_ready, a_ready) = (
            sem(n) for n in ("small_in", "cw_ready", "cw_kept", "past_kept", "wd_free", "u_ready", "v_ready", "u_kept", "c_step",
                             "c_ready", "g_ready", "a_ready"))
        wu_in = [sem("wu_in0"), sem("wu_in1")]
        wd_in = [consts_sb["soft"][f"p6_wd_in{i}"] for i in range(2)]
        (x1_in, nf_in, d_ready, y_ready, ss_ready, ms_ready, root_ready, out_step, out_ready, y_out, t_ready, t_kept, t_out) = (
            sem(n) for n in ("x1_in", "nf_in", "d_ready", "y_ready", "ss_ready", "ms_ready", "root_ready", "out_step", "out_ready",
                             "y_out", "t_ready", "t_kept", "t_out"))
        junk = U[0][:, 0:D]
        normf = U[1][:, 0:D]
        block = ctx.enter_context(nc.Block())
        prompt = lambda u, s: u[:, s:s + T]
        sample = lambda u, s: u[:, 2 + T:].rearrange("p (b t) -> p b t", b=DB)[:, :, s:s + DS]

        def finish(t):
            dve = nc.vector
            r = rows_of(t)
            dve.wait_ge(ss_ready, t + 1)
            nc.vector.tensor_scalar(ss[0:r, t:t + 1], ss[0:r, t:t + 1], 1.0 / D, EPS, ALU.mult, ALU.add).then_inc(ms_ready, 1)
            dve.wait_ge(root_ready, t + 1)
            nc.vector.reciprocal(rt[0:r, t:t + 1], rt[0:r, t:t + 1]).then_inc(out_step, 1)
            if t == 0:
                dve.wait_ge(nf_in, 16)
            dve.wait_ge(out_step, t + 1)
            nc.vector.scalar_tensor_tensor(y[0:r, t, :], y[0:r, t, :], rt[0:r, t:t + 1], normf[0:r], ALU.mult, ALU.mult).then_inc(out_ready, 1)

        @block.sync
        def _(sp):
            sp.dma_start(small[0:3, :], io["conv_w"][0]).then_inc(small_in, 16)
            sp.dma_start(small[3:4, :], io["conv_b"]).then_inc(small_in, 16)
            sp.dma_start(past, io["state_ffn_conv"][0].rearrange("b t f -> (b t) f")).then_inc(small_in, 16)
            wg = io["w_gate"][0].rearrange("(k p) n -> p k n", p=P)
            wv = io["w_val"][0].rearrange("(k p) n -> p k n", p=P)
            with sp.Fori(0, NF // 2) as i:
                for j in range(2):
                    f = 2 * i + j
                    sp.wait_ge(u_ready, f + 1)
                    sp.dma_start(wu[:, j, 0], wg[:, :, bass.ds(f * P, P)]).then_inc(wu_in[j], 16)
                    sp.wait_ge(v_ready, f + 1)
                    sp.dma_start(wu[:, j, 1], wv[:, :, bass.ds(f * P, P)]).then_inc(wu_in[j], 16)
            sp.wait_ge(v_ready, NF + 2)
            sp.dma_start(y[:, 0:NT - 1, :], scratch["x1"][0:T].rearrange("(t p) n -> p t n", p=P)).then_inc(x1_in, 16)
            sp.dma_start(y[0:DT, NT - 1, :], scratch["x1"][T:TOK]).then_inc(x1_in, 16)
            sp.wait_ge(a_ready, NF + 1)
            sp.dma_start(normf, io["norm_f"].rearrange("(a n) -> a n", a=1).to_broadcast([P, D])).then_inc(nf_in, 16)
            sp.wait_ge(t_kept, 6)
            sp.dma_start(io["cv_p"][0, 0], small_tail[0:2, :]).then_inc(t_out, 16)
            sp.dma_start(io["cv_s"][0].rearrange("b t f -> (b t) f"), small_tail[2:18, :]).then_inc(t_out, 16)
            for t in range(NT):
                sp.wait_ge(out_ready, t + 1)
                dst = io["y_prompt"][0, t * P:(t + 1) * P, :] if t < NT - 1 else io["y_sample"].rearrange("b t d -> (b t) d")
                sp.dma_start(dst, y[0:rows_of(t), t, :]).then_inc(y_out, 16)
            sp.wait_ge(t_out, 32)
            sp.wait_ge(y_out, 16 * NT)

        @block.gpsimd
        def _(pool):
            w = io["w_down"][0].rearrange("(f p) n -> p f n", p=P)
            for c in range(4):
                if c == 1:
                    pool.wait_ge(v_ready, NF + 2)
                if c >= 2:
                    pool.wait_ge(d_ready, NT * (c - 1))
                pool.dma_start(wd[:, c % 2], w[:, :, c * QW:(c + 1) * QW]).then_inc(wd_in[c % 2], 16)

        @block.scalar
        def _(act):
            act.wait_ge(cw_ready, 2)
            nc.scalar.copy(pastT[:].rearrange("p f t -> p (f t)"), bank[7][:, 0:NF * 2 * DB]).then_inc(past_kept, 1)
            with act.Fori(0, NF // 2) as i:
                for j in range(2):
                    f = 2 * i + j
                    act.wait_ge(u_ready, f + 3)
                    act.wait_ge(a_ready, f + 1)
                    nc.scalar.copy(U[j][:, 2:354], bank[0][:, 0:352])
                    nc.scalar.copy(U[j][:, 354:706], bank[1][:, 0:352])
                    nc.scalar.copy(U[j][:, 706:T + 2], bank[2][:, 0:320])
                    nc.scalar.copy(sample(U[j], 2), bank[2][:, 320:352].rearrange("p (b t) -> p b t", b=DB)).then_inc(u_kept, 1)
                    act.wait_ge(c_ready, f + 1)
                    nc.scalar.activation(C[:], C[:], ACT.Gelu_apprx_tanh).then_inc(g_ready, 1)
            for q in range(6):
                act.wait_ge(t_ready, q + 1)
                n = min(4, NF - 4 * q)
                nc.scalar.copy(small_tail[:, 512 * q:512 * q + P * n], bank[6 + q % 2][0:18, 0:P * n]).then_inc(t_kept, 1)
            for t in range(NT):
                r = rows_of(t)
                act.wait_ge(y_ready, 3 * NT + t + 1)
                if t >= 1:
                    act.wait_ge(ss_ready, t)
                else:
                    act.wait_ge(a_ready, NF + 1)
                nc.scalar.activation(junk[0:r], y[0:r, t, :], ACT.Square, accum_out=ss[0:r, t:t + 1]).then_inc(ss_ready, 1)
                act.wait_ge(ms_ready, t + 1)
                nc.scalar.activation(rt[0:r, t:t + 1], ss[0:r, t:t + 1], ACT.Sqrt).then_inc(root_ready, 1)

        @block.vector
        def _(dve):
            dve.wait_ge(cw_ready, 1)
            nc.vector.tensor_copy(cw[:].rearrange("p f t -> p (f t)"), bank[6][:, 0:NF * 4]).then_inc(cw_kept, 1)
            for j in range(2):
                nc.vector.memset(U[j][:, 0:2], 0.0).then_inc(cw_kept, 1)
            dve.wait_ge(past_kept, 1)
            dve.wait_ge(cw_kept, 3)
            dve.sem_inc(a_ready, 1)
            dve.sem_inc(g_ready, 1)
            with dve.Fori(0, NF // 2) as i:
                for j in range(2):
                    f = 2 * i + j
                    step = Steps(dve, c_step, 6 * f)
                    u = U[j]
                    nc.vector.tensor_copy(cwj[:, j, :], cw[:, bass.ds(f, 1), :].rearrange("p o t -> p (o t)"))
                    step(nc.vector.tensor_copy(sample(u, 0)[:, :, 0:2], pastT[:, bass.ds(f, 1), :].rearrange("p o (b t) -> p (o b) t", b=DB)))
                    dve.wait_ge(u_kept, f + 1)
                    wj = lambda k: cwj[:, j, k:k + 1]
                    c_p, c_s = C[:, 0:T], C[:, T:TOK].rearrange("p (b t) -> p b t", b=DB)
                    step(nc.vector.tensor_scalar(c_p, prompt(u, 0), wj(0), wj(3), ALU.mult, ALU.add))
                    step(nc.vector.tensor_scalar(c_s, sample(u, 0), wj(0), wj(3), ALU.mult, ALU.add))
                    step(nc.vector.scalar_tensor_tensor(c_p, prompt(u, 1), wj(1), c_p, ALU.mult, ALU.add))
                    step(nc.vector.scalar_tensor_tensor(c_s, sample(u, 1), wj(1), c_s, ALU.mult, ALU.add))
                    nc.vector.scalar_tensor_tensor(c_p, prompt(u, 2), wj(2), c_p, ALU.mult, ALU.add)
                    nc.vector.scalar_tensor_tensor(c_s, sample(u, 2), wj(2), c_s, ALU.mult, ALU.add).then_inc(c_ready, 1)
                    nc.vector.tensor_copy(tails[:, bass.ds(f, 1), 0:2].rearrange("p o t -> p (o t)"), u[:, T:T + 2])
                    step(nc.vector.tensor_copy(tails[:, bass.ds(f, 1), 2:].rearrange("p o (b t) -> p (o b) t", b=DB),
                                               u[:, 2 + T:].rearrange("p (b t) -> p b t", b=DB)[:, :, DS:DS + 2]))
                    dve.wait_ge(g_ready, f + 2)
                    dve.wait_ge(v_ready, f + 3)
                    for n, (c0, w) in enumerate(PARTS):
                        last = nc.vector.tensor_tensor(aT[:, bass.ds(f, 1), c0:c0 + w].rearrange("p o t -> p (o t)"), bank[3 + n][:, 0:w],
                                                       C[:, c0:c0 + w], ALU.mult)
                    last.then_inc(a_ready, 1)
                    assert step.n == 6
                    dve.wait_ge(a_ready, f + 2)
            dve.wait_ge(x1_in, 32)
            n_y = 0
            for c in range(4):
                for t in range(NT):
                    r = rows_of(t)
                    n_y += 1
                    dve.wait_ge(d_ready, n_y)
                    dst = y[0:r, t, c * QW:(c + 1) * QW]
                    nc.vector.tensor_tensor(dst, dst, bank[t % 3][0:r, 0:QW], ALU.add).then_inc(y_ready, 1)
                    if c == 3 and t >= 1:
                        finish(t - 1)
            finish(NT - 1)

        @block.tensor
        def _(pe):
            pe.wait_ge(small_in, 48)
            for f in range(NF):
                last = nc.tensor.transpose(bank[6][:, 4 * f:4 * f + 4], small[:, f * P:(f + 1) * P], ident[0:4, 0:4])
            last.then_inc(cw_ready, 1)
            for f in range(NF):
                last = nc.tensor.transpose(bank[7][:, 16 * f:16 * f + 16], past[:, f * P:(f + 1) * P], ident[0:16, 0:16])
            last.then_inc(cw_ready, 1)
            pe.wait_ge(cw_kept, 1)
            pe.sem_inc(u_ready, 2)
            pe.sem_inc(v_ready, 2)
            pe.wait_ge(a_ready, 1)
            with pe.Fori(0, NF // 2) as i:
                for j in range(2):
                    f = 2 * i + j
                    pe.wait_ge(wu_in[j], 32 * i + 32)
                    pe.wait_ge(g_ready, f + 1)
                    for a in range(2):
                        if a == 1:
                            pe.wait_ge(a_ready, f + 1)
                        for n, (c0, w) in enumerate(PARTS):
                            for k in range(KD):
                                last = nc.tensor.matmul(bank[3 * a + n][:, 0:w], wu[:, j, a, k, :], hT[:, k, c0:c0 + w],
                                                        start=(k == 0), stop=(k == KD - 1))
                        last.then_inc((u_ready, v_ready)[a], 1)
            n_d = 0
            for c in range(4):
                pe.wait_ge(wd_in[c % 2], 16 * (c // 2 + 1))
                if c == 0:
                    pe.wait_ge(a_ready, NF + 1)
                for t in range(NT):
                    r = rows_of(t)
                    if n_d >= 3:
                        pe.wait_ge(y_ready, n_d - 2)
                    for f in range(NF):
                        last = nc.tensor.matmul(bank[t % 3][0:r, 0:QW], aT[:, f, t * P:t * P + r], wd[:, c % 2, f, :],
                                                start=(f == 0), stop=(f == NF - 1))
                    last.then_inc(d_ready, 1)
                    n_d += 1
                    if c == 0 and t < 6:
                        if t >= 2:
                            pe.wait_ge(t_kept, t - 1)
                        for k in range(min(4, NF - 4 * t)):
                            last = nc.tensor.transpose(bank[6 + t % 2][0:18, k * P:(k + 1) * P], tails[:, 4 * t + k, :], ident[:])
                        last.then_inc(t_ready, 1)


def clear_semaphores(nc, first):
    with nc.Block() as block:
        @block.vector
        def _(dve):
            dve.sem_clear(range(first, 256))


def hybrid_step(nc, io):
    with ExitStack() as ctx:
        sb = lambda name, shape: ctx.enter_context(nc.sbuf_tensor(name, shape, F32))
        scratch = {
            "z_tok": nc.dram_tensor("z_tok", [TOK, 1816], F32).ap(),
            "q_T": nc.dram_tensor("q_T", [64, NH, TOK], F32).ap(),
            "x1": nc.dram_tensor("x1", [TOK, D], F32).ap(),
            "o_mix": nc.dram_tensor("o_mix", [TOK, D], F32).ap(),
        }
        consts = {"ident": sb("ident", [P, P]), "in": ctx.enter_context(nc.semaphore("ident_in"))}
        with nc.Block() as block:
            @block.sync
            def _(sp):
                sp.dma_start(consts["ident"][:], io["c_ident"]).then_inc(consts["in"], 16)
                sp.wait_ge(consts["in"], 16)
        consts["soft"] = {n: ctx.enter_context(nc.semaphore(n)) for n in (
            "p1_w_in0", "p1_w_in1", "p1_cached", "p3_x_in0", "p3_x_in1", "p3_x_in2", "p3_x_in3", "p5_w_in", "p5_x1_out0",
            "p5_x1_out1", "p6_wd_in0", "p6_wd_in1")}
        first = max(s.num for s in [consts["in"], *consts["soft"].values()]) + 1
        keep = {}
        with ExitStack() as mid:
            keep["kcT_p"] = mid.enter_context(nc.sbuf_tensor("kcT_p", [DK, NG, NCP - 1], F32))
            keep["vc_p"] = mid.enter_context(nc.sbuf_tensor("vc_p", [NCP - 1, NG, DK], F32))
            with ExitStack() as low:
                keep["qn"] = low.enter_context(nc.sbuf_tensor("qn", [64, NH, TOK], F32))
                keep["qh"] = low.enter_context(nc.sbuf_tensor("qh", [P, HH, TOK], F32))
                keep["fg"] = low.enter_context(nc.sbuf_tensor("fg", [P, HH, TOK], F32))
                project_in(nc, io, keep, scratch, consts)
                clear_semaphores(nc, first)
                hgrn(nc, io, keep, scratch, consts)
            clear_semaphores(nc, first)
            sample_attention(nc, io, keep, scratch, consts)
            clear_semaphores(nc, first)
            prompt_attention(nc, io, keep, scratch, consts)
        with ExitStack() as high:
            keep["hy"] = high.enter_context(nc.sbuf_tensor("hy", [P, NT * D], F32))
            keep["hT"] = keep["hy"][:, 0:KD * TOK].rearrange("p (k t) -> p k t", k=KD)
            clear_semaphores(nc, first)
            project_out(nc, io, keep, scratch, consts)
            clear_semaphores(nc, first)
            feed_forward(nc, io, keep, scratch, consts)


_INS = ["x_prompt", "x_sample", "cache_nsa_kv", "cache_win_kv", "state_hgrn", "state_ffn_conv", "page_table", "norm1", "w_in",
        "hg_lb_logits", "hg_norm", "cmp_pe", "cmp_w1", "cmp_w2", "w_out", "norm2", "w_gate", "w_val", "conv_w", "conv_b",
        "w_down", "norm_f"]
_OUTS = {"y_prompt": (1, T, D), "y_sample": (DB, DS, D), "kv_p": (1, 1, T, 4, 2, 64), "kv_s": (1, DB, DS, 4, 2, 64),
         "win_p": (1, 1, WIN, 2, 2, 64), "win_s": (1, DB, WIN, 2, 2, 64), "hg_p": (1, 1, HH, 128, 128),
         "hg_s": (1, DB, HH, 128, 128), "cv_p": (1, 1, 2, FF), "cv_s": (1, DB, 2, FF)}


def kernel(**inputs):
    import numpy as _np
    import concourse.bacc as _bacc
    from concourse import mybir as _mybir
    from concourse.bass_utils import run_bass_kernel_spmd as _run

    nc = _bacc.Bacc("TRN2", target_bir_lowering=False, num_devices=1)
    arrays, io = {}, {}
    for name in _INS:
        a = _np.ascontiguousarray(inputs[name])
        arrays[f"in_{name}"] = a
        io[name] = nc.dram_tensor(f"in_{name}", a.shape, _mybir.dt.from_np(a.dtype), kind="ExternalInput").ap()
    for name, a in shape_constants().items():
        arrays[name] = a
        io[name] = nc.dram_tensor(name, a.shape, _mybir.dt.from_np(a.dtype), kind="ExternalInput").ap()
    for name, shape in _OUTS.items():
        io[name] = nc.dram_tensor(f"out_{name}", shape, _mybir.dt.float32, kind="ExternalOutput").ap()
    hybrid_step(nc, io)
    r = _run(nc, [arrays], core_ids=[0])
    return tuple(r.results[0][f"out_{name}"] for name in _OUTS)
```

```python
from contextlib import ExitStack

import concourse.bass as bass
from concourse import mybir

F32 = mybir.dt.float32
F32R = mybir.dt.float32r
I32 = mybir.dt.int32
U32 = mybir.dt.uint32
ALU = mybir.AluOpType
ACT = mybir.ActivationFunctionType
AX = mybir.AxisListType

P = 128
D = 1024
KD = D // P
T = 1024
DB, DS = 8, 4
DT = DB * DS
TOK = T + DT
NT = T // P + 1
HGW = 512
HH = 4
NH, NG, DK = 8, 2, 64
R = NH // NG
PAST, PAGE = 4096, 128
NPAGE = PAST // PAGE
WIN = 512
D_IN = 6 * HGW + 256 + 24
FF = 2816
QW = D // 4
EPS = 1e-6
W1_SHAPE = [P, 2, 2, 8, 256]
BIG = 1e30
SCALE = DK ** -0.5
NCP = T // 16
NCD = PAST // 16
NSB = 65


class Steps:

    def __init__(self, eng, sem, base=0):
        self.eng, self.sem, self.base, self.n = eng, sem, base, 0

    def __call__(self, ins):
        self.n += 1
        ins.then_inc(self.sem, 1)
        self.eng.wait_ge(self.sem, self.base + self.n)
def shape_constants():
    import numpy as np

    c = {"c_ident": np.eye(P, dtype=np.float32)}
    s, t = np.arange(P)[:, None], np.arange(P)[None, :]
    levels = [(s // (2 * h) == t // (2 * h)) & (s % (2 * h) < h) & (t % (2 * h) >= h) for h in HALVES] + [s == t]
    c["c_hmask"] = np.stack(levels, 1).astype(np.float32)
    at = np.arange(TOK)
    c["c_reset"] = np.tile(np.where(at < T, at % P, (at - T) % DS) > 0, (P, 1)).astype(np.float32)
    c["c_rowsel"] = (np.arange(DT)[:, None] // DS == np.arange(DB)[None, :]).astype(np.float32)
    row_t = np.arange(16) // R
    wm = np.zeros((64, 2 * DS), np.float32)
    for g in range(NG):
        for q in range(16):
            wm[48 * g + q, 0:row_t[q] + 1] = -BIG
            wm[48 * g + q, DS + row_t[q] + 1:] = -BIG
    c["c_wmask"] = wm
    c["c_nmask"] = np.where(np.arange(DS)[None, :] > np.tile(row_t, NG)[:, None], -BIG, 0.0).astype(np.float32)
    n, j = np.arange(2 * P)[:, None], np.arange(64)[None, :]
    over = np.maximum(np.minimum(16 * n + 32, 64 * j + 64) - np.maximum(16 * n, 64 * j), 0) / 16.0
    c["c_overlap"] = np.ascontiguousarray(over.reshape(2, P, 64).transpose(1, 0, 2)).astype(np.float32)
    chunk = np.arange(2 * P).reshape(2, P)
    c["c_spread"] = np.stack([(chunk[k][None, :] // 4 == np.arange(64)[:, None]) for k in range(2)], 1).astype(np.float32)
    c["c_part"] = (np.arange(P) % 8).astype(np.float32)[:, None]
    i, k = np.arange(P)[:, None], np.arange(P)[None, :]
    c["c_causal"] = np.where(k > i, -BIG, 0.0).astype(np.float32)
    c["c_older"] = np.where(k <= i, -BIG, 0.0).astype(np.float32)
    qpos = (np.arange(T // P)[None, :, None] * P + np.arange(P)[:, None, None])
    c["c_cmask"] = np.where(np.arange(NCP - 1)[None, None, :] * 16 + 31 > qpos, -BIG, 0.0).astype(np.float32)
    return c


def project_in(nc, io, keep, scratch, consts_sb):
    qh, fg, qn = keep["qh"], keep["fg"], keep["qn"]
    ident = consts_sb["ident"]
    GW = 256
    FM = [0, GW, HGW, HGW + GW, 4 * HGW, 4 * HGW + GW]
    TM = [(2 * HGW + GW * i, GW, GW * i) for i in range(4)] + [(5 * HGW + GW * i, GW, 2 * HGW + GW * i) for i in range(2)]
    TM.append((6 * HGW, D_IN - 6 * HGW, 3 * HGW))
    GROUPS = [(c, GW) for c in FM] + [(c, w) for c, w, _ in TM]
    LW = D_IN - 6 * HGW
    N_T = [(0, 352), (352, 352), (704, 352)]

    units = []
    for g in range(len(FM)):
        for m in range(2):
            for n0, nw in N_T:
                units.append(("fm", g, m, n0, nw))
    for g in range(len(TM)):
        for t in range(NT):
            units.append(("tm", g, t, 0, TM[g][1]))
    first_tm = sum(u[0] == "fm" for u in units)

    with ExitStack() as ctx:
        sb = lambda name, shape: ctx.enter_context(nc.sbuf_tensor(name, shape, F32))
        sem = lambda name: ctx.enter_context(nc.semaphore(name))
        xin = sb("xin", [P, 3, D])
        xn = sb("xn", [P, 2, D])
        ss = sb("ss", [P, NT])
        rstd = sb("rstd", [P, NT])
        rt = sb("rt", [P, NT])
        g1 = sb("g1", [P, KD])
        two = lambda name, shape: ctx.enter_context(nc.sbuf_tensor(name, shape, F32R))
        xH, xL = two("xH", [P, KD, TOK]), two("xL", [P, KD, TOK])
        raw = sb("raw1", [P, KD, LW])
        wH, wL = two("wH1", [P, 2, KD, LW]), two("wL1", [P, 2, KD, LW])
        stage = sb("stage", [P, 4, LW])
        sq = stage[:].rearrange("p s n -> p (s n)")[:, 0:D]
        bank = [ctx.enter_context(nc.psum_tensor(f"pj{i}", [P, 512], F32)) for i in range(8)]

        x_in = [sem(f"p1_x_in{i}") for i in range(3)]
        ss_ready = sem("p1_ss_ready")
        root_ready = sem("p1_root_ready")
        rstd_ready = sem("p1_rstd_ready")
        xn_ready = sem("p1_xn_ready")
        xT_ready = sem("p1_xT_ready")
        xT_kept = sem("p1_xT_kept")
        g1_in = sem("p1_g1_in")
        w_in_s = consts_sb["soft"]["p1_w_in0"]
        xH_ready, wH_ready, wL_ready = sem("p1_xH_ready"), sem("p1_wH_ready"), sem("p1_wL_ready")
        unit_ready = sem("p1_unit_ready")
        kept = [sem("p1_kept_dve"), sem("p1_kept_act")]
        stored = [sem(f"p1_stored{i}") for i in range(4)]
        cached = consts_sb["soft"]["p1_cached"]

        def rows(t):
            return P if t < NT - 1 else DT

        def evacuate(eng, u, kind, g, a, n0, nw, copy):
            eng.wait_ge(unit_ready, u + 1)
            b = bank[u % 8]
            if kind == "fm" and g < 4:
                copy((qh, fg)[g // 2][:, 2 * (g % 2) + a, n0:n0 + nw], b[:, 0:nw]).then_inc(kept[u % 2], 1)
            elif kind == "fm":
                a += 2 * (g % 2)
                copy(qn[:, 2 * a, n0:n0 + nw], b[0:64, 0:nw])
                copy(qn[:, 2 * a + 1, n0:n0 + nw], b[64:128, 0:nw]).then_inc(kept[u % 2], 1)
            else:
                j = u - first_tm
                if j >= 4:
                    eng.wait_ge(stored[j % 4], 16 * (j // 4))
                r = rows(a)
                copy(stage[0:r, j % 4, 0:nw], b[0:r, 0:nw]).then_inc(kept[u % 2], 1)

        def high_part(j):
            w = GROUPS[j][1]
            nc.scalar.wait_ge(w_in_s, 16 * (j + 1))
            if j >= 2:
                nc.scalar.wait_ge(unit_ready, group_start[j - 1])
            nc.scalar.copy(wH[:, j % 2, :, 0:w], raw[:, :, 0:w]).then_inc(wH_ready, 1)

        def rest(j):
            w = GROUPS[j][1]
            nc.vector.wait_ge(wH_ready, j + 1)
            nc.vector.tensor_tensor(wL[:, j % 2, :, 0:w], raw[:, :, 0:w], wH[:, j % 2, :, 0:w].bitcast(F32), ALU.subtract
                                    ).then_inc(wL_ready, 1)

        group_of = lambda u: units[u][1] + (0 if u < first_tm else len(FM))
        group_start = [next(u for u in range(len(units)) if group_of(u) == j) for j in range(len(GROUPS))]
        block = ctx.enter_context(nc.Block())

        @block.sync
        def _(sp):
            sp.dma_start(g1[:], io["norm1"].rearrange("a (k p) -> p (a k)", p=P), allow_slow_non_contiguous=True).then_inc(g1_in, 16)
            for t in range(NT):
                if t >= 3:
                    sp.wait_ge(xn_ready, t - 2)
                src = io["x_prompt"][0, t * P:(t + 1) * P, :] if t < NT - 1 else io["x_sample"].rearrange("b t d -> (b t) d")
                sp.dma_start(xin[0:rows(t), t % 3, :], src).then_inc(x_in[t % 3], 16)
            for j in range(NT * len(TM)):
                u = first_tm + j
                g, t = units[u][1], units[u][2]
                w, c0 = TM[g][1], TM[g][2]
                sp.wait_ge(kept[u % 2], u // 2 + 1)
                sp.dma_start(scratch["z_tok"][t * P:t * P + rows(t), c0:c0 + w],
                             stage[0:rows(t), j % 4, 0:w]).then_inc(stored[j % 4], 16)
            for i in range(4):
                sp.wait_ge(stored[i], 16 * len(range(i, NT * len(TM), 4)))

        @block.gpsimd
        def _(pool):
            for j, (c, w) in enumerate(GROUPS):
                if j >= 1:
                    pool.wait_ge(wL_ready, j)
                pool.dma_start(raw[:, :, 0:w], io["w_in"][0].rearrange("(k p) n -> p k n", p=P)[:, :, c:c + w]).then_inc(w_in_s, 16)
            pool.dma_start(io["win_s"][0, :, 0:WIN - DS], io["cache_win_kv"][0, :, DS:WIN]).then_inc(cached, 16)
            pool.wait_ge(cached, 16)

        @block.scalar
        def _(act):
            act.wait_ge(ss_ready, 1)
            for t in range(NT):
                act.wait_ge(x_in[t % 3], 16 * (t // 3 + 1))
                if t >= 1:
                    act.wait_ge(root_ready, t)
                r = rows(t)
                nc.scalar.activation(sq[0:r, :], xin[0:r, t % 3, :], ACT.Square, accum_out=ss[0:r, t:t + 1]).then_inc(ss_ready, 1)
                act.wait_ge(rstd_ready, 2 * t + 1)
                nc.scalar.activation(rt[0:r, t:t + 1], rstd[0:r, t:t + 1], ACT.Sqrt).then_inc(root_ready, 1)
                if t == 2:
                    high_part(0)
            for u, (kind, g, a, n0, nw) in enumerate(units):
                if u in group_start and group_of(u) + 1 < len(GROUPS):
                    high_part(group_of(u) + 1)
                if u % 2 == 1:
                    evacuate(act, u, kind, g, a, n0, nw, lambda o, i: nc.scalar.copy(o, i))

        @block.vector
        def _(dve):
            nc.vector.memset(ss[:], 1.0).then_inc(ss_ready, 1)
            dve.wait_ge(g1_in, 16)
            for t in range(NT):
                r = rows(t)
                dve.wait_ge(ss_ready, t + 2)
                nc.vector.tensor_scalar(rstd[0:r, t:t + 1], ss[0:r, t:t + 1], 1.0 / D, EPS, ALU.mult, ALU.add).then_inc(rstd_ready, 1)
                dve.wait_ge(root_ready, t + 1)
                nc.vector.reciprocal(rstd[0:r, t:t + 1], rt[0:r, t:t + 1]).then_inc(rstd_ready, 1)
                dve.wait_ge(rstd_ready, 2 * t + 2)
                if t >= 2:
                    dve.wait_ge(xT_ready, 2 * (t - 1))
                nc.vector.tensor_scalar(xn[0:r, t % 2, :], xin[0:r, t % 3, :], rstd[0:r, t:t + 1], None, ALU.mult).then_inc(xn_ready, 1)
                for h in range(2):
                    dve.wait_ge(xT_ready, 2 * t + h + 1)
                    src = bank[(2 * t + h) % 8][:].rearrange("p (k c) -> p k c", k=4)
                    nc.vector.tensor_tensor(xH[:, 4 * h:4 * h + 4, t * P:t * P + r],
                                            src[:, :, 0:r],
                                            g1[:, 4 * h:4 * h + 4].unsqueeze(2).to_broadcast([P, 4, r]), ALU.mult).then_inc(xH_ready, 1)
                    dve.wait_ge(xH_ready, 2 * t + h + 1)
                    for k in range(4):
                        last = nc.vector.scalar_tensor_tensor(xL[:, 4 * h + k, t * P:t * P + r], src[:, k, 0:r],
                                                              g1[:, 4 * h + k:4 * h + k + 1],
                                                              xH[:, 4 * h + k, t * P:t * P + r].bitcast(F32), ALU.mult, ALU.subtract)
                    last.then_inc(xT_kept, 1)
                if t == 2:
                    rest(0)
            for u, (kind, g, a, n0, nw) in enumerate(units):
                if u in group_start and group_of(u) + 1 < len(GROUPS):
                    rest(group_of(u) + 1)
                if u % 2 == 0:
                    evacuate(dve, u, kind, g, a, n0, nw, lambda o, i: nc.vector.tensor_copy(o, i))

        @block.tensor
        def _(pe):
            pe.wait_ge(consts_sb["in"], 16)
            for t in range(NT):
                r = rows(t)
                pe.wait_ge(xn_ready, t + 1)
                for h in range(2):
                    n = 2 * t + h
                    if n >= 8:
                        pe.wait_ge(xT_kept, n - 7)
                    for k in range(4):
                        last = nc.tensor.transpose(bank[n % 8][:, k * P:k * P + r],
                                                   xn[0:r, t % 2, (4 * h + k) * P:(4 * h + k + 1) * P], ident[0:r, 0:r])
                    last.then_inc(xT_ready, 1)
            pe.wait_ge(xT_kept, 2 * NT)
            for u, (kind, g, a, n0, nw) in enumerate(units):
                j = group_of(u)
                if u == group_start[j]:
                    pe.wait_ge(wL_ready, j + 1)
                if u >= 8:
                    pe.wait_ge(kept[u % 2], (u - 8) // 2 + 1)
                for k in range(KD):
                    for part, (wp, xp) in enumerate(((wH, xH), (wL, xH), (wH, xL))):
                        flags = {"start": k + part == 0, "stop": k == KD - 1 and part == 2}
                        if kind == "fm":
                            last = nc.tensor.matmul(bank[u % 8][:, 0:nw], wp[:, j % 2, k, a * P:(a + 1) * P], xp[:, k, n0:n0 + nw], **flags)
                        else:
                            r = rows(a)
                            last = nc.tensor.matmul(bank[u % 8][0:r, 0:nw], xp[:, k, a * P:a * P + r], wp[:, j % 2, k, 0:nw], **flags)
                last.then_inc(unit_ready, 1)


HALVES = (64, 32, 16, 8, 4, 2, 1)


def hgrn(nc, io, keep, scratch, consts_sb):
    qh, fg = keep["qh"], keep["fg"]
    ident = consts_sb["ident"]
    NL = len(HALVES)
    NC = T // P

    with ExitStack() as ctx:
        sb = lambda name, shape: ctx.enter_context(nc.sbuf_tensor(name, shape, F32))
        sem = lambda name: ctx.enter_context(nc.semaphore("p2_" + name))
        kk = sb("kk", [P, HH, TOK])
        v_tok = sb("v_tok", [P, NT, HGW])
        o_tok = sb("o_tok", [P, NT, HGW])
        W = sb("W", [P, NL, TOK])
        g_tok = W[:].rearrange("p l t -> p (l t)")[:, 0:NT * HGW].rearrange("p (t n) -> p t n", t=NT)
        Q, K, A = sb("Q", [P, TOK]), sb("K", [P, TOK]), sb("A", [P, TOK])
        EA, QA, KE = sb("EA", [P, TOK]), sb("QA", [P, TOK]), sb("KE", [P, TOK])
        vd = sb("vd", [DT, P])
        vsel = sb("vsel", [DT, DB, P])
        KEt = sb("KEt", [P, NC, P])
        KEtd = sb("KEtd", [DT, P])
        hmask = sb("hmask", [P, NL + 1, P])
        prod = sb("prod", [P, NL + 1, P])
        prodd = sb("prodd", [DT, 3, DT])
        attT = sb("attT", [P, 2, P])
        attTd = sb("attTd", [DT, DT])
        S = sb("S", [P, P])
        S0 = sb("S0", [P, DB, P])
        oTd = sb("oTd", [P, DT])
        rowsel = sb("rowsel", [DT, DB])
        reset = sb("reset", [P, TOK])
        lgt = sb("lgt", [P, 2, HH])
        lmax, lb, oml, lsum = (sb(n, [P, HH]) for n in ("lmax", "lb", "oml", "lsum"))
        oss = sb("oss", [P, NT * HH])
        ort = sb("ort", [P, NT * HH])
        normw = sb("normw", [P, HGW])
        pa = [ctx.enter_context(nc.psum_tensor(f"pa{i}", [P, 4, P], F32)) for i in range(4)]
        po = [ctx.enter_context(nc.psum_tensor(f"po{i}", [P, 512], F32)) for i in range(2)]
        ps = ctx.enter_context(nc.psum_tensor("ps", [P, 512], F32))
        pd = ctx.enter_context(nc.psum_tensor("pd", [P, 512], F32))

        small_in, v_in, g_in, s0_in = sem("small_in"), sem("v_in"), sem("g_in"), sem("s0_in")
        lb_step = sem("lb_step")
        lexp_ready, lb_ready = sem("lexp_ready"), sem("lb_ready")
        gates_ready, f_ready, logf_ready, a_ready = sem("gates_ready"), sem("f_ready"), sem("logf_ready"), sem("a_ready")
        copied, d_ready, e_ready, w_ready = sem("copied"), sem("d_ready"), sem("e_ready"), sem("w_ready")
        keT_ready, keT_kept = sem("keT_ready"), sem("keT_kept")
        att_ready, prod_ready, attT_ready = sem("att_ready"), sem("prod_ready"), sem("attT_ready")
        o_ready, o_kept, st_ready, s_ready = sem("o_ready"), sem("o_kept"), sem("st_ready"), sem("s_ready")
        s_out, qT_out = sem("s_out"), sem("qT_out")
        attd_ready, prodd_ready, attTd_ready, oTd_ready, oTd_kept = (sem(n) for n in (
            "attd_ready", "prodd_ready", "attTd_ready", "oTd_ready", "oTd_kept"))
        od_ready, std_ready, s0_step, s0_done, s0_out = (sem(n) for n in (
            "od_ready", "std_ready", "s0_step", "s0_done", "s0_out"))
        norm_step, oroot_ready, gsilu_ready, oms_ready, o_done, o_out, copies_out = (sem(n) for n in (
            "norm_step", "oroot_ready", "gsilu_ready", "oms_ready", "o_done", "o_out", "copies_out"))

        block = ctx.enter_context(nc.Block())

        def halves(x, h):
            n = TOK if 2 * h <= DS else T
            return x[:, 0:n].rearrange("p (b t) -> p b t", t=2 * h)

        @block.sync
        def _(sp):
            sp.dma_start(lgt[:], io["hg_lb_logits"].rearrange("l (h p) -> p l h", p=P), allow_slow_non_contiguous=True).then_inc(small_in, 16)
            sp.dma_start(reset[:], io["c_reset"]).then_inc(small_in, 16)
            sp.dma_start(hmask[:], io["c_hmask"]).then_inc(small_in, 16)
            sp.dma_start(rowsel[:], io["c_rowsel"]).then_inc(small_in, 16)
            sp.dma_start(normw[:], io["hg_norm"].to_broadcast([P, HGW])).then_inc(small_in, 16)
            sp.dma_start(v_tok[:, 0:NC, :], scratch["z_tok"][0:T, 0:HGW].rearrange("(t p) n -> p t n", p=P)).then_inc(v_in, 16)
            sp.dma_start(v_tok[0:DT, NC, :], scratch["z_tok"][T:TOK, 0:HGW]).then_inc(v_in, 16)
            z = scratch["z_tok"]
            sp.dma_start(scratch["q_T"], keep["qn"][:]).then_inc(qT_out, 16)
            sp.dma_start(io["kv_p"][0, 0].rearrange("t s g d -> t (s g d)"), z[0:T, 1024:1536]).then_inc(copies_out, 16)
            sp.dma_start(io["kv_s"][0].rearrange("b t s g d -> (b t) (s g d)"), z[T:TOK, 1024:1536]).then_inc(copies_out, 16)
            sp.dma_start(io["win_p"][0, 0].rearrange("t s g d -> t (s g d)"), z[T - WIN:T, 1536:1792]).then_inc(copies_out, 16)
            sp.dma_start(io["win_s"][0, :, WIN - DS:WIN].rearrange("b t s g d -> b t (s g d)"),
                         z[T:TOK, 1536:1792].rearrange("(b t) n -> b t n", b=DB)).then_inc(copies_out, 16)
            sp.sem_inc(s0_out, 16)
            sp.sem_inc(s_out, 16)
            with sp.Fori(0, HH) as h:
                sp.wait_ge(s0_out, 16 * h + 16)
                sp.dma_start(S0[:], io["state_hgrn"][0, :, bass.ds(h, 1), :, :].rearrange("b o k v -> k (b o) v")).then_inc(s0_in, 16)
                sp.wait_ge(s_ready, (NC + 1) * (h + 1))
                sp.dma_start(io["hg_p"][0, 0, bass.ds(h, 1)].rearrange("o k v -> k (o v)"), S[:]).then_inc(s_out, 16)
                sp.wait_ge(s0_done, h + 2)
                sp.dma_start(io["hg_s"][0, :, bass.ds(h, 1), :, :].rearrange("b o k v -> k (b o) v"), S0[:]).then_inc(s0_out, 16)
            sp.wait_ge(o_kept, HH * (NC + 1) + 1)
            sp.dma_start(g_tok[:, 0:NC, :], z[0:T, HGW:2 * HGW].rearrange("(t p) n -> p t n", p=P)).then_inc(g_in, 16)
            sp.dma_start(g_tok[0:DT, NC, :], z[T:TOK, HGW:2 * HGW]).then_inc(g_in, 16)
            sp.wait_ge(o_done, 1)
            sp.dma_start(scratch["o_mix"][0:T, 0:HGW].rearrange("(t p) n -> p t n", p=P), o_tok[:, 0:NC, :]).then_inc(o_out, 16)
            sp.dma_start(scratch["o_mix"][T:TOK, 0:HGW], o_tok[0:DT, NC, :]).then_inc(o_out, 16)
            sp.wait_ge(o_out, 32)
            sp.wait_ge(copies_out, 64)
            sp.wait_ge(s_out, 16 * HH + 16)
            sp.wait_ge(s0_out, 16 * HH + 16)

        @block.gpsimd
        def _(pool):
            pool.wait_ge(qT_out, 16)
            pool.dma_start(keep["w1"][:].rearrange("p k q s h -> p (k q s) h"),
                           io["cmp_w1"][0].rearrange("k q (s u) d h -> (u d) (k q s) h", u=2)).then_inc(consts_sb["soft"]["p3_w1_in"], 16)

        @block.scalar
        def _(act):
            act.wait_ge(lb_step, 2)
            nc.scalar.activation(lgt[:], lgt[:], ACT.Exp).then_inc(lexp_ready, 1)
            nc.scalar.activation(kk[:], fg[:], ACT.Sigmoid, scale=-1.0).then_inc(gates_ready, 1)
            act.wait_ge(gates_ready, 1)
            nc.scalar.activation(fg[:], fg[:], ACT.Sigmoid).then_inc(gates_ready, 1)
            nc.scalar.activation(qh[:], qh[:], ACT.Silu).then_inc(gates_ready, 1)
            act.wait_ge(f_ready, HH)
            nc.scalar.activation(fg[:], fg[:], ACT.Ln).then_inc(logf_ready, 1)
            act.wait_ge(gates_ready, 3)
            act.wait_ge(v_in, 32)
            act.sem_inc(o_kept, 1)
            with act.Fori(0, HH) as h:
                act.wait_ge(s0_done, h + 1)
                act.wait_ge(a_ready, h + 1)
                row = lambda x: x[:, bass.ds(h, 1), :].rearrange("p o t -> p (o t)")
                nc.scalar.copy(A[:], row(fg)).then_inc(copied, 1)
                nc.scalar.copy(Q[:], row(qh)).then_inc(copied, 1)
                nc.scalar.copy(K[:], row(kk)).then_inc(copied, 1)
                nc.scalar.copy(vd[:], v_tok[0:DT, NC, bass.ds(h * P, P)]).then_inc(copied, 1)
                act.wait_ge(copied, 4 * h + 1)
                nc.scalar.activation(EA[:], A[:], ACT.Exp).then_inc(e_ready, 1)
                act.wait_ge(d_ready, (NL + 1) * h + 1)
                nc.scalar.activation(KE[:], KE[:], ACT.Exp).then_inc(e_ready, 1)
                for l, half in enumerate(HALVES):
                    act.wait_ge(d_ready, (NL + 1) * h + l + 2)
                    n = TOK if 2 * half <= DS else T
                    nc.scalar.activation(W[:, l, 0:n], W[:, l, 0:n], ACT.Exp).then_inc(e_ready, 1)
                for j in range(2):
                    act.wait_ge(keT_ready, 3 * h + j + 1)
                    nc.scalar.copy(KEt[:, 4 * j:4 * j + 4, :], pa[j][:]).then_inc(keT_kept, 1)
                act.wait_ge(keT_ready, 3 * h + 3)
                nc.scalar.copy(KEtd[:], pd[0:DT, 384:512]).then_inc(keT_kept, 1)
                for c in range(NC):
                    act.wait_ge(o_ready, NC * h + c + 1)
                    nc.scalar.copy(o_tok[:, c, bass.ds(h * P, P)], po[c % 2][:, 0:P]).then_inc(o_kept, 1)
                act.wait_ge(oTd_ready, h + 1)
                nc.scalar.copy(oTd[:], pd[:, 128:160]).then_inc(oTd_kept, 1)
                act.wait_ge(od_ready, h + 1)
                nc.scalar.copy(o_tok[0:DT, NC, bass.ds(h * P, P)], pd[0:DT, 256:384]).then_inc(o_kept, 1)
            act.wait_ge(oms_ready, 1)
            nc.scalar.activation(ort[:], oss[:], ACT.Sqrt).then_inc(oroot_ready, 1)
            act.wait_ge(g_in, 32)
            nc.scalar.activation(g_tok[:, 0:NC, :], g_tok[:, 0:NC, :], ACT.Silu)
            nc.scalar.activation(g_tok[0:DT, NC, :], g_tok[0:DT, NC, :], ACT.Silu).then_inc(gsilu_ready, 1)

        @block.vector
        def _(dve):
            dve.wait_ge(small_in, 80)
            step = Steps(dve, lb_step)
            step(nc.vector.tensor_tensor(lmax[:], lgt[:, 0, :], lgt[:, 1, :], ALU.max))
            step(nc.vector.tensor_tensor(lgt[:], lgt[:], lmax[:].unsqueeze(1).to_broadcast([P, 2, HH]), ALU.subtract))
            dve.wait_ge(lexp_ready, 1)
            step(nc.vector.tensor_tensor(lsum[:], lgt[:, 0, :], lgt[:, 1, :], ALU.add))
            step(nc.vector.reciprocal(lsum[:], lsum[:]))
            step(nc.vector.tensor_tensor(lb[:], lgt[:, 0, :], lsum[:], ALU.mult))
            step(nc.vector.tensor_scalar(oml[:], lb[:], -1.0, 1.0, ALU.mult, ALU.add))
            nc.vector.memset(o_tok[:, NC, :], 0.0).then_inc(lb_ready, 1)
            for h in range(HH):
                dve.wait_ge(gates_ready, 2)
                nc.vector.tensor_scalar(kk[:, h, :], kk[:, h, :], oml[:, h:h + 1], None, ALU.mult)
                nc.vector.tensor_scalar(fg[:, h, :], fg[:, h, :], oml[:, h:h + 1], lb[:, h:h + 1], ALU.mult, ALU.add).then_inc(f_ready, 1)
            dve.wait_ge(logf_ready, 1)
            for h in range(HH):
                nc.vector.tensor_tensor_scan(fg[:, h, :], reset[:], fg[:, h, :], 0.0, ALU.mult, ALU.add).then_inc(a_ready, 1)
            dve.wait_ge(lb_ready, 1)
            for ahead in (s0_done, attT_ready, prod_ready):
                dve.sem_inc(ahead, 1)
            with dve.Fori(0, HH) as h:
                dve.wait_ge(copied, 4 * h + 4)
                ch = lambda x: x[:, 0:T].rearrange("p (c t) -> p c t", t=P)
                dc = lambda x: x[:, T:TOK].rearrange("p (c t) -> p c t", t=DS)
                nc.vector.tensor_tensor(ch(KE), ch(A)[:, :, P - 1:P].to_broadcast([P, NC, P]), ch(A), ALU.subtract)
                nc.vector.tensor_tensor(dc(KE), dc(A)[:, :, DS - 1:DS].to_broadcast([P, DB, DS]), dc(A), ALU.subtract).then_inc(d_ready, 1)
                for l, half in enumerate(HALVES):
                    a, w = halves(A, half), halves(W[:, l, :], half)
                    mid = a[:, :, half - 1:half].to_broadcast([P, a.shape[1], half])
                    nc.vector.tensor_tensor(w[:, :, 0:half], mid, a[:, :, 0:half], ALU.subtract)
                    nc.vector.tensor_tensor(w[:, :, half:], a[:, :, half:], mid, ALU.subtract).then_inc(d_ready, 1)
                base = (NL + 2) * h
                dve.wait_ge(e_ready, base + 1)
                nc.vector.tensor_tensor(QA[:], EA[:], Q[:], ALU.mult).then_inc(w_ready, 1)
                dve.wait_ge(e_ready, base + 2)
                nc.vector.tensor_tensor(KE[:], KE[:], K[:], ALU.mult).then_inc(w_ready, 1)
                for l, half in enumerate(HALVES):
                    w = halves(W[:, l, :], half)
                    dve.wait_ge(e_ready, base + l + 3)
                    nc.vector.tensor_tensor(w[:, :, 0:half], w[:, :, 0:half], halves(K, half)[:, :, 0:half], ALU.mult)
                    nc.vector.tensor_tensor(w[:, :, half:], w[:, :, half:], halves(Q, half)[:, :, half:], ALU.mult).then_inc(w_ready, 1)
                nc.vector.tensor_tensor(vsel[:], vd[:].unsqueeze(1).to_broadcast([DT, DB, P]),
                                        rowsel[:].unsqueeze(2).to_broadcast([DT, DB, P]), ALU.mult).then_inc(w_ready, 1)
                dve.wait_ge(s_out, 16 * h + 16)
                nc.vector.memset(S[:], 0.0).then_inc(s_ready, 1)

                def picked(c):
                    dve.wait_ge(att_ready, NC * h + c + 1)
                    dve.wait_ge(attT_ready, NC * h + c + 1)
                    b = 2 * (c % 2)
                    nc.vector.tensor_tensor(prod[:, 0:4, :], pa[b][:], hmask[:, 0:4, :], ALU.mult)
                    nc.vector.tensor_tensor(prod[:, 4:8, :], pa[b + 1][:], hmask[:, 4:8, :], ALU.mult).then_inc(prod_ready, 1)
                    dve.wait_ge(prod_ready, NC * h + c + 2)
                    if c >= 2:
                        dve.wait_ge(o_ready, NC * h + c - 1)
                    nc.vector.tensor_reduce(attT[:, c % 2, :], prod[:].rearrange("p l t -> p t l"), AX.X, ALU.add).then_inc(attT_ready, 1)

                picked(0)
                for c in range(NC):
                    if c + 1 < NC:
                        picked(c + 1)
                    dve.wait_ge(st_ready, NC * h + c + 1)
                    dve.wait_ge(s_ready, (NC + 1) * h + c + 1)
                    nc.vector.scalar_tensor_tensor(S[:], S[:], EA[:, c * P + P - 1:c * P + P], ps[:, 0:P], ALU.mult, ALU.add).then_inc(s_ready, 1)
                dve.wait_ge(attd_ready, h + 1)
                nc.vector.tensor_tensor(prodd[:], pd[0:DT, 0:96].rearrange("p (l t) -> p l t", l=3), hmask[0:DT, 5:8, 0:DT],
                                        ALU.mult).then_inc(prodd_ready, 1)
                dve.wait_ge(prodd_ready, h + 1)
                nc.vector.tensor_reduce(attTd[:], prodd[:].rearrange("p l t -> p t l"), AX.X, ALU.add).then_inc(attTd_ready, 1)
                dve.wait_ge(std_ready, h + 1)
                nc.vector.tensor_tensor(S0[:], S0[:], dc(EA)[:, :, DS - 1:DS].to_broadcast([P, DB, P]), ALU.mult).then_inc(s0_step, 1)
                dve.wait_ge(s0_step, h + 1)
                nc.vector.tensor_tensor(S0[:, 0:4, :], S0[:, 0:4, :], pa[2][:], ALU.add)
                nc.vector.tensor_tensor(S0[:, 4:8, :], S0[:, 4:8, :], pa[3][:], ALU.add).then_inc(s0_done, 1)
            dve.wait_ge(o_kept, HH * (NC + 1) + 1)
            step = Steps(dve, norm_step)
            sqr = v_tok
            step(nc.vector.tensor_tensor(sqr[:], o_tok[:], o_tok[:], ALU.mult))
            step(nc.vector.tensor_reduce(oss[:], sqr[:].rearrange("p t (h v) -> p (t h) v", h=HH), AX.X, ALU.add))
            nc.vector.tensor_scalar(oss[:], oss[:], 1.0 / P, EPS, ALU.mult, ALU.add).then_inc(oms_ready, 1)
            dve.wait_ge(oroot_ready, 1)
            step(nc.vector.reciprocal(ort[:], ort[:]))
            o36 = o_tok[:].rearrange("p t (h v) -> p (t h) v", h=HH)
            step(nc.vector.tensor_tensor(o36, o36, ort[:].unsqueeze(2).to_broadcast([P, NT * HH, P]), ALU.mult))
            step(nc.vector.tensor_tensor(o_tok[:], o_tok[:], normw[:].unsqueeze(1).to_broadcast([P, NT, HGW]), ALU.mult))
            dve.wait_ge(gsilu_ready, 1)
            nc.vector.tensor_tensor(o_tok[:, 0:NC, :], o_tok[:, 0:NC, :], g_tok[:, 0:NC, :], ALU.mult)
            nc.vector.tensor_tensor(o_tok[0:DT, NC, :], o_tok[0:DT, NC, :], g_tok[0:DT, NC, :], ALU.mult).then_inc(o_done, 1)

        @block.tensor
        def _(pe):
            with pe.Fori(0, HH) as h:
                wb = (NL + 3) * h
                pe.wait_ge(w_ready, wb + 2)
                pe.wait_ge(prod_ready, NC * h + 1)
                for j in range(2):
                    for c in range(4):
                        last = nc.tensor.transpose(pa[j][:, c, :], KE[:, (4 * j + c) * P:(4 * j + c + 1) * P], ident[:])
                    last.then_inc(keT_ready, 1)
                pe.wait_ge(o_kept, (NC + 1) * h + 1)
                nc.tensor.transpose(pd[0:DT, 384:512], KE[:, T:TOK], ident[:]).then_inc(keT_ready, 1)
                pe.wait_ge(w_ready, wb + NL + 3)
                pe.wait_ge(keT_kept, 3 * h + 3)
                pe.wait_ge(s0_done, h + 1)

                def products(c):
                    b = 2 * (c % 2)
                    if c >= 2:
                        pe.wait_ge(prod_ready, NC * h + c)
                    x = slice(c * P, c * P + P)
                    for l in range(NL):
                        nc.tensor.matmul(pa[b + l // 4][:, l % 4, :], W[:, l, x], W[:, l, x], start=True, stop=True)
                    nc.tensor.matmul(pa[b + 1][:, 3, :], K[:, x], Q[:, x], start=True, stop=True).then_inc(att_ready, 1)

                products(0)
                for c in range(NC):
                    if c + 1 < NC:
                        products(c + 1)
                    v = v_tok[:, c, bass.ds(h * P, P)]
                    pe.wait_ge(attT_ready, NC * h + c + 2)
                    if c >= 2:
                        pe.wait_ge(o_kept, (NC + 1) * h + c)
                    nc.tensor.matmul(po[c % 2][:, 0:P], attT[:, c % 2, :], v, start=True, stop=False)
                    pe.wait_ge(s_ready, (NC + 1) * h + c + 1)
                    nc.tensor.matmul(po[c % 2][:, 0:P], QA[:, c * P:c * P + P], S[:], start=False, stop=True).then_inc(o_ready, 1)
                    nc.tensor.matmul(ps[:, 0:P], KEt[:, c, :], v, start=True, stop=True).then_inc(st_ready, 1)
                for j in range(2):
                    nc.tensor.matmul(pd[0:DT, j * DT:(j + 1) * DT], W[:, 5 + j, T:TOK], W[:, 5 + j, T:TOK], start=True, stop=True)
                nc.tensor.matmul(pd[0:DT, 2 * DT:3 * DT], K[:, T:TOK], Q[:, T:TOK], start=True, stop=True).then_inc(attd_ready, 1)
                pe.wait_ge(attTd_ready, h + 1)
                nc.tensor.matmul(pd[:, 128:160], vd[:], attTd[:], start=True, stop=False)
                pe.wait_ge(s0_in, 16 * (h + 1))
                for b in range(DB):
                    last = nc.tensor.matmul(pd[:, 128 + DS * b:128 + DS * b + DS], S0[:, b, :], QA[:, T + DS * b:T + DS * b + DS],
                                            start=False, stop=(b == DB - 1))
                last.then_inc(oTd_ready, 1)
                pe.wait_ge(prod_ready, NC * (h + 1) + 1)
                for j in range(2):
                    last = nc.tensor.matmul(pa[2 + j][:].rearrange("p b v -> p (b v)"), KEtd[:],
                                            vsel[:, 4 * j:4 * j + 4, :].rearrange("p b v -> p (b v)"), start=True, stop=True)
                last.then_inc(std_ready, 1)
                pe.wait_ge(oTd_kept, h + 1)
                nc.tensor.transpose(pd[0:DT, 256:384], oTd[:], ident[:]).then_inc(od_ready, 1)


def sample_attention(nc, io, keep, scratch, consts_sb):
    ident = consts_sb["ident"]
    kcT_p, vc_p = keep["kcT_p"], keep["vc_p"]
    z = scratch["z_tok"]
    ROWTOK = 16
    NTL = 2 * DB

    with ExitStack() as ctx:
        sb = lambda name, shape, dt=F32: ctx.enter_context(nc.sbuf_tensor("a3_" + name, shape, dt))
        sem = lambda name: ctx.enter_context(nc.semaphore("p3_" + name))
        sb("w1_place", W1_SHAPE)
        w1 = keep["w1"]
        X = [sb(f"X{i}", [P, ROWTOK, 4, NG, DK]) for i in range(4)]
        XT = [sb(f"XT{i}", [P, 8, NG, P]) for i in range(2)]
        KsT = [sb(f"KsT{i}", [P, 4, P]) for i in range(2)]
        w2 = sb("w2", [P, 2, 2, DK])
        pe_T = sb("pe_T", [P, 2, 2, 8])
        bias = sb("bias", [P, 4])
        hs = sb("hs", [P, 2, NG, 256])
        kcT = sb("kcT", [P, 256])
        vc = sb("vc", [P, 2, NG, DK])
        qblk = sb("qblk", [P, DB, 64])
        qb = sb("qb", [P, 64])
        qc = sb("qc", [P, 32])
        new_tok = XT[1][0:DT].rearrange("p s g c -> p (s g c)")[:, 0:512]
        knT = sb("knT", [P, 2, DT])
        vn = sb("vn", [DS, 2, 2, P])
        Kw = sb("Kw", [P, 4, 256])
        KwT = KsT[0][:].rearrange("p s c -> p (s c)")
        PwT = KsT[1][:].rearrange("p s c -> p (s c)")[:, 0:320]
        wmask = sb("wmask", [64, 2 * DS])
        PS = sb("PS", [P, 2, ROWTOK, 32])
        q_raw = PS[:].rearrange("p k s q -> p (k s q)")[:, 0:R * DT].rearrange("p (r t) -> p r t", r=R)
        Sw = PS[0:64].rearrange("p k s q -> p (k s q)")[:, 0:WIN + DS]
        col = sb("col", [P, 24])
        nmw, dw, rw, nmc, dc, rc, rs = (col[0:64, i:i + 1] for i in range(7))
        m1, m2, mm, nm = (col[0:32, i:i + 1] for i in range(8, 12))
        gates = sb("gates", [64, DB, 3])
        ob = sb("ob", [64, 2, DK])
        Pc = sb("Pc", [64, 256])
        PcT = sb("PcT", [P, 2, 64])
        PcS = sb("PcS", [P, 2, 8])
        overlap = sb("overlap", [P, 2, 64])
        imp = sb("imp", [8, 62])
        top = sb("top", [8, 8])
        sel = sb("sel", [8, 64])
        selT = sb("selT", [64, 8])
        spread = sb("spread", [64, 2, P])
        c0 = sb("c0", [P, 2, 8])
        mx = sb("mx", [P, 2, 32])
        mxx = sb("mxx", [P, 32])
        nmask = sb("nmask", [32, DS])
        sn = sb("sn", [32, DS])
        diag = sb("diag", [32, 32])
        ones = sb("ones", [P, P])
        cc = sb("cc", [P, 2, 32])
        dp = sb("dp", [P, 2, 32])
        PnT = sb("PnT", [DS, 32])
        page = sb("page", [P, NTL], I32)
        pagef = sb("pagef", [P, NTL])
        part = sb("part", [P, 1])
        idx = sb("idx", [P, NTL], U32)
        ph = [ctx.enter_context(nc.psum_tensor(f"ph{i}", [P, 512], F32)) for i in range(4)]
        cb, wb = ph[0:2], ph[2:4]
        tb = [ctx.enter_context(nc.psum_tensor(f"tb{i}", [P, 512], F32)) for i in range(2)]
        st = [ctx.enter_context(nc.psum_tensor(f"st{i}", [P, 512], F32)) for i in range(2)]

        (page_in, small_in, w_in1, xp_in, idx_ready, setup_step, setup_done, bias_ready, bias_kept, kn_ready, kn_kept,
         prompt_done, gates_ready) = (sem(n) for n in (
             "page_in", "small_in", "w_in", "xp_in", "idx_ready", "setup_step", "setup_done", "bias_ready", "bias_kept",
             "kn_ready", "kn_kept", "prompt_done", "gates_ready"))
        w_carry = sem("w_carry")
        x_in = [consts_sb["soft"][f"p3_x_in{i}"] for i in range(4)]
        tr_ready, s_done, proj_ready, hs_ready = (sem(n) for n in ("tr_ready", "s_done", "proj_ready", "hs_ready"))
        kept = [sem("kept_dve"), sem("kept_act")]
        (kw_in, q_ready, w_tr, w_kT, w_s, w_step, w_max, w_e, w_pT, w_pk, w_o, w_done) = (sem(n) for n in (
            "kw_in", "q_ready", "w_tr", "w_kT", "w_s", "w_step", "w_max", "w_e", "w_pT", "w_pk", "w_o", "w_done"))
        (c_kv, c_kc, c_vc, c_s, c_step, c_max, c_e, c_p, c_pT, c_pk, c_imp, c_sel) = (sem(n) for n in (
            "c_kv", "c_kc", "c_vc", "c_s", "c_step", "c_max", "c_e", "c_p", "c_pT", "c_pk", "c_imp", "c_sel"))
        c_o = sem("c_o")
        (l_sT, l_sk, l_mask, l_step, l_mx, l_mT, l_D, l_mb, l_x, l_e, l_dp, l_nT, l_nk, pv_ready, b_done, b_out) = (
            sem(n) for n in ("l_sT", "l_sk", "l_mask", "l_step", "l_mx", "l_mT", "l_D", "l_mb", "l_x", "l_e", "l_dp",
                             "l_nT", "l_nk", "pv_ready", "b_done", "b_out"))

        block = ctx.enter_context(nc.Block())
        cache_rows = io["cache_nsa_kv"][0].rearrange("n (c t) s g d -> (n c) (t s g d)", t=ROWTOK)

        def move_pairs(who, kv, q, rows, copy):
            src = tb[who][:].rearrange("p (s u c) -> p s u c", s=2, u=2)
            for g in range(NG):
                for u in range(2):
                    last = copy(XT[kv][64 * u:64 * u + 64, 2 * q:2 * q + 2, g, 0:rows], src[64 * g:64 * g + 64, :, u, 0:rows])
            last.then_inc(kept[who], 1)

        def move_transposed(eng, who, b, e, copy):
            eng.wait_ge(tr_ready, 24 * b + e + 9)
            if 4 <= e < 8 or 12 <= e < 16:
                if e % 4 >= 2:
                    eng.wait_ge(s_done, 8 * b + 4 * (e // 8) + e % 4 - 1)
                copy(KsT[who][:].rearrange("p s c -> p (s c)"), tb[who][:]).then_inc(kept[who], 1)
            else:
                move_pairs(who, (e // 8 if e < 16 else (e - 16) // 4), e % 4, P, copy)

        @block.gpsimd
        def _(pool):
            pool.wait_ge(idx_ready, 1)
            for n in range(NTL):
                if n >= 4:
                    pool.wait_ge(pv_ready, (n - 4) // 2 + 2)
                elif n == 3:
                    pool.wait_ge(prompt_done, 1)
                nc.gpsimd.indirect_dma_start(X[n % 4][:].rearrange("p t s g d -> p (t s g d)"), None, cache_rows,
                                             bass.IndirectOffsetOnAxis(ap=idx[:, n:n + 1], axis=0)).then_inc(x_in[n % 4], 16)

        @block.sync
        def _(sp):
            flat = io["page_table"].rearrange("b (h p) -> (b h) p", h=2)
            for c in range(8):
                sp.dma_start(page[c:P:8, :], flat.rearrange("n p -> p n"), allow_slow_non_contiguous=True).then_inc(page_in, 16)
            sp.dma_start(part[:], io["c_part"]).then_inc(page_in, 16)
            sp.dma_start(X[3][0:NCP].rearrange("p t s g d -> p (t s g d)"),
                         io["kv_p"][0, 0].rearrange("(c t) s g d -> c (t s g d)", t=ROWTOK)).then_inc(xp_in, 16)
            for k in range(2):
                sp.dma_start(pe_T[:, k], io["cmp_pe"][0, k].rearrange("q (s u) d -> (u d) q s", u=2),
                             allow_slow_non_contiguous=True).then_inc(w_in1, 16)
            sp.dma_start(w2[:], io["cmp_w2"][0].rearrange("k (h p) d -> p k h d", p=P)).then_inc(w_in1, 16)
            for dst, src in ((wmask, "c_wmask"), (overlap, "c_overlap"), (spread, "c_spread"), (nmask, "c_nmask")):
                sp.dma_start(dst[:], io[src]).then_inc(small_in, 16)
            for g in range(NG):
                sp.dma_start(q_raw[64 * g:64 * g + 64], scratch["q_T"][:, R * g:R * g + R, T:TOK]).then_inc(small_in, 16)
            sp.dma_start(new_tok[:], z[T:TOK, 1280:1792]).then_inc(small_in, 16)
            sp.wait_ge(setup_done, 1)
            for g in range(NG):
                for t in range(DS):
                    for k in range(3):
                        sp.dma_start(gates[48 * g + R * t:48 * g + R * t + R, :, k:k + 1],
                                     z[T:TOK, 1792 + 8 * k + 4 * g:1792 + 8 * k + 4 * g + 4].rearrange("(b t) r -> t r b", t=DS)[t].unsqueeze(2),
                                     allow_slow_non_contiguous=True).then_inc(gates_ready, 16)
            sp.sem_inc(b_out, 32)
            with sp.Fori(0, DB // 2) as i:
                for j in range(2):
                    b = 2 * i + j
                    sp.wait_ge(w_done, b + 1)
                    sp.dma_start(Kw[:], io["cache_win_kv"][0, bass.ds(b, 1)].rearrange("o (c p) s g d -> p (o c) (s g d)", p=P)
                                 ).then_inc(kw_in, 16)
                    sp.dma_start(vn[:, j], z[bass.ds(DS * b + T, DS), 1280:1792].rearrange("t (a h c) -> t a h c", a=2, h=2)[:, :, 1]).then_inc(kw_in, 16)
                    sp.wait_ge(b_done, b + 2)
                    for g in range(NG):
                        dst = scratch["o_mix"][bass.ds(DS * b + T, DS), HGW + 256 * g:HGW + 256 * g + 256]
                        sp.dma_start(dst.rearrange("t (r d) -> t r d", d=DK), ob[48 * g:48 * g + 16, 0, :]).then_inc(b_out, 16)
            sp.wait_ge(b_out, 32 * DB + 32)

        @block.scalar
        def _(act):
            act.wait_ge(gates_ready, 16 * 24)
            nc.scalar.activation(gates[:], gates[:], ACT.Sigmoid).then_inc(gates_ready, 1)
            act.wait_ge(bias_ready, 1)
            nc.scalar.copy(bias[:], st[0][:, 0:4]).then_inc(bias_kept, 1)
            for e in range(1, 8, 2):
                act.wait_ge(tr_ready, e + 1)
                move_pairs(1, e // 4, e % 4, NCP, nc.scalar.copy)
            act.wait_ge(bias_kept, 1)
            for k in range(2):
                act.wait_ge(proj_ready, k + 1)
                if k == 1:
                    act.wait_ge(c_kv, 1)
                for m in range(2):
                    nc.scalar.activation(hs[:, m, :, 0:NCP - 1], ph[2 * k + m][:].rearrange("p (g n) -> p g n", g=NG)[:, :, 0:NCP - 1],
                                         ACT.Silu, bias=bias[:, 2 * k + m:2 * k + m + 1]).then_inc(hs_ready, 1)
            act.wait_ge(c_kv, 2)
            nc.scalar.copy(vc_p[0:NCP - 1].rearrange("p g d -> p (g d)"), tb[1][0:NCP - 1, 0:P]).then_inc(c_vc, 1)
            act.wait_ge(w_done, 1)
            with act.Fori(0, DB // 2) as i:
                for j in range(2):
                    b = 2 * i + j
                    move = lambda *groups: [move_transposed(act, 1, b, e, nc.scalar.copy) for e in groups]

                    def hidden(k):
                        act.wait_ge(proj_ready, 4 * b + 2 * k + 4)
                        for m in range(2):
                            nc.scalar.activation(hs[:, m, :, 0:NCD - 1],
                                                 ph[2 * k + m][:].rearrange("p (g n) -> p g n", g=NG)[:, :, 0:NCD - 1],
                                                 ACT.Silu, bias=bias[:, 2 * k + m:2 * k + m + 1]).then_inc(hs_ready, 1)

                    move(1, 3, 5, 7, 9)
                    act.wait_ge(w_max, b + 1)
                    nc.scalar.activation(Sw[:], Sw[:], ACT.Exp, bias=nmw, scale=SCALE, accum_out=dw).then_inc(w_e, 1)
                    move(11, 13, 15, 17, 19)
                    hidden(0)
                    move(21)
                    act.wait_ge(c_max, b + 1)
                    nc.scalar.activation(Pc[:, 0:NCD - 1], cb[0][0:64, 0:NCD - 1], ACT.Exp, bias=nmc, scale=SCALE,
                                         accum_out=dc).then_inc(c_e, 1)
                    move(23)
                    for k in range(2):
                        act.wait_ge(l_x, 2 * b + k + 1)
                        nc.scalar.activation(PS[:, k], PS[:, k], ACT.Exp, scale=SCALE).then_inc(l_e, 1)
                    nc.scalar.activation(sn[:], sn[:], ACT.Exp, bias=nm, scale=SCALE).then_inc(l_e, 1)
                    hidden(1)
                    act.wait_ge(c_kv, 2 * b + 4)
                    nc.scalar.copy(vc[:, 0].rearrange("p g d -> p (g d)"), tb[1][:, 0:P])
                    nc.scalar.copy(vc[0:P - 1, 1].rearrange("p g d -> p (g d)"), tb[1][0:P - 1, P:2 * P]).then_inc(c_vc, 1)

        @block.vector
        def _(dve):
            dve.wait_ge(page_in, 16 * 9)
            step = Steps(dve, setup_step)
            step(nc.vector.tensor_copy(pagef[:], page[:]))
            step(nc.vector.tensor_scalar(pagef[:], pagef[:], 8.0, part[:, 0:1], ALU.mult, ALU.add))
            nc.vector.tensor_copy(idx[:], pagef[:]).then_inc(idx_ready, 1)
            nc.vector.memset(gates[:], 0.0).then_inc(setup_done, 1)
            nc.vector.memset(ones[:], 1.0)
            nc.vector.memset(sel[:], 1.0)
            step(nc.vector.memset(qblk[:], 0.0))
            dve.wait_ge(small_in, 16 * 7)
            for g in range(NG):
                step(nc.vector.tensor_copy(qblk[64 * g:64 * g + 64, :, 48 * g:48 * g + 16].rearrange("p b (t r) -> p r b t", r=R),
                                           q_raw[64 * g:64 * g + 64].rearrange("p r (b t) -> p r b t", t=DS)))
            dve.wait_ge(kn_ready, 1)
            nc.vector.tensor_copy(knT[:].rearrange("p a t -> p (a t)"), st[1][:, 0:64]).then_inc(kn_kept, 1)
            for e in range(0, 8, 2):
                dve.wait_ge(tr_ready, e + 1)
                move_pairs(0, e // 4, e % 4, NCP, nc.vector.tensor_copy)
            dve.wait_ge(c_kv, 1)
            nc.vector.tensor_scalar(kcT_p[:], tb[0][0:64, 0:P].rearrange("p (g n) -> p g n", g=NG)[:, :, 0:NCP - 1],
                                    SCALE, None, ALU.mult).then_inc(c_kc, 1)
            dve.wait_ge(gates_ready, 16 * 24 + 1)
            for ahead in (b_done, pv_ready, w_done, kn_kept):
                dve.sem_inc(ahead, 1)
            with dve.Fori(0, DB // 2) as i:
                for j in range(2):
                    b = 2 * i + j
                    gate = lambda k: gates[:, bass.ds(b, 1), k:k + 1].rearrange("p o k -> p (o k)")
                    dve.wait_ge(pv_ready, b + 1)
                    qsrc = qblk[:, bass.ds(b, 1), :].rearrange("p o q -> p (o q)")
                    nc.vector.tensor_copy(qb[:], qsrc)
                    nc.vector.tensor_copy(qc[:, 0:16], qblk[:, bass.ds(b, 1), 0:16].rearrange("p o q -> p (o q)"))
                    nc.vector.tensor_copy(qc[:, 16:32], qblk[:, bass.ds(b, 1), 48:64].rearrange("p o q -> p (o q)")).then_inc(q_ready, 1)
                    move = lambda *groups: [move_transposed(dve, 0, b, e, nc.vector.tensor_copy) for e in groups]
                    largest = lambda k: nc.vector.tensor_reduce(mx[:, k, :], st[k][:].rearrange("p (s q) -> p q s", q=32), AX.X, ALU.max)
                    move(0, 2, 4, 6, 8)
                    dve.wait_ge(w_tr, b + 1)
                    nc.vector.tensor_copy(KwT[:], wb[0][:]).then_inc(w_kT, 1)
                    dve.wait_ge(w_s, b + 1)
                    step = Steps(dve, w_step, 3 * b)
                    nc.vector.tensor_copy(Sw[:, DS:WIN], wb[0][0:64, DS:])
                    nc.vector.tensor_tensor(Sw[:, 0:DS], wb[0][0:64, 0:DS], wmask[:, 0:DS], ALU.add)
                    step(nc.vector.tensor_tensor(Sw[:, WIN:], wb[1][0:64, 0:DS], wmask[:, DS:], ALU.add))
                    step(nc.vector.tensor_reduce(nmw, Sw[:], AX.X, ALU.max, negate=True))
                    nc.vector.tensor_scalar(nmw, nmw, SCALE, None, ALU.mult).then_inc(w_max, 1)
                    move(10)
                    dve.wait_ge(w_pT, b + 1)
                    nc.vector.tensor_copy(PwT[:, 0:256], wb[0][:, 0:256])
                    nc.vector.tensor_copy(PwT[0:DS, 256:320], wb[0][0:DS, 256:320]).then_inc(w_pk, 1)
                    dve.wait_ge(w_e, b + 1)
                    step(nc.vector.reciprocal(rw, dw))
                    dve.wait_ge(w_o, b + 1)
                    dve.wait_ge(b_out, 32 * b + 32)
                    nc.vector.tensor_scalar(ob[:, 0, :], wb[1][0:64, 0:DK], rw, gate(2), ALU.mult, ALU.mult).then_inc(w_done, 1)
                    dve.wait_ge(s_done, 8 * b + 4)
                    largest(0)
                    move(12, 14, 16, 18)
                    dve.wait_ge(s_done, 8 * b + 8)
                    largest(1)
                    move(20)
                    dve.wait_ge(c_kv, 2 * b + 3)
                    nc.vector.tensor_copy(kcT[:, 0:NCD - 1], cb[0][:, 0:NCD - 1]).then_inc(c_kc, 1)
                    dve.wait_ge(c_s, b + 1)
                    step = Steps(dve, c_step, 10 * b)
                    step(nc.vector.tensor_reduce(nmc, cb[0][0:64, 0:NCD - 1], AX.X, ALU.max, negate=True))
                    nc.vector.tensor_scalar(nmc, nmc, SCALE, None, ALU.mult).then_inc(c_max, 1)
                    dve.wait_ge(c_e, b + 1)
                    step(nc.vector.reciprocal(rc, dc))
                    nc.vector.tensor_scalar(Pc[:, 0:NCD - 1], Pc[:, 0:NCD - 1], rc, None, ALU.mult).then_inc(c_p, 1)
                    move(22)
                    dve.wait_ge(c_pT, b + 1)
                    nc.vector.tensor_copy(PcT[:, 0, :], cb[1][:, 0:64])
                    step(nc.vector.tensor_copy(PcT[0:P - 1, 1, :], cb[1][0:P - 1, 64:128]))
                    for k in range(2):
                        r = P - k
                        for g in range(NG):
                            last = nc.vector.tensor_reduce(PcS[0:r, k, 4 * g:4 * g + 4],
                                                           PcT[0:r, k, 48 * g:48 * g + 16].rearrange("p (t r) -> p t r", r=R),
                                                           AX.X, ALU.add)
                    last.then_inc(c_pk, 1)
                    dve.wait_ge(c_imp, b + 1)
                    step(nc.vector.tensor_copy(imp[:], cb[1][0:8, 1:63]))
                    dve.sem_inc(w_carry, 1)
                    step(nc.vector.max(top[:], imp[:]))
                    dve.sem_inc(w_carry, 1)
                    step(nc.vector.match_replace(imp[:], top[:], imp[:], -1.0))
                    dve.sem_inc(w_carry, 1)
                    step(nc.vector.max(top[:], imp[:]))
                    step(nc.vector.memset(top[:, 5:8], -1.0))
                    dve.sem_inc(w_carry, 1)
                    step(nc.vector.match_replace(imp[:], top[:], imp[:], -1.0))
                    nc.vector.tensor_scalar(sel[:, 1:63], imp[:], 0.0, None, ALU.is_lt).then_inc(c_sel, 1)
                    dve.wait_ge(l_sT, b + 1)
                    nc.vector.tensor_copy(selT[:], cb[1][0:64, 0:8]).then_inc(l_sk, 1)
                    dve.wait_ge(l_mask, b + 1)
                    step2 = Steps(dve, l_step, 8 * b)
                    step2(nc.vector.tensor_scalar(c0[:].rearrange("p a q -> p (a q)"), cb[1][:, 0:16], BIG, -BIG, ALU.mult, ALU.add))
                    step2(nc.vector.tensor_tensor(mx[:].rearrange("p a (q r) -> p (a q) r", r=R), mx[:].rearrange("p a (q r) -> p (a q) r", r=R),
                                                  c0[:].rearrange("p a q -> p (a q)").unsqueeze(2).to_broadcast([P, 16, R]), ALU.add))
                    nc.vector.tensor_tensor(mxx[:], mx[:, 0, :], mx[:, 1, :], ALU.max).then_inc(l_mx, 1)
                    dve.wait_ge(l_mT, b + 1)
                    nc.vector.tensor_reduce(m1, cb[0][0:32, 0:P], AX.X, ALU.max)
                    step2(nc.vector.tensor_tensor(sn[:], cb[0][0:32, P:P + DS], nmask[:], ALU.add))
                    step2(nc.vector.tensor_reduce(m2, sn[:], AX.X, ALU.max))
                    step2(nc.vector.tensor_tensor(mm, m1, m2, ALU.max))
                    nc.vector.tensor_scalar(nm, mm, -SCALE, None, ALU.mult)
                    nc.vector.tensor_scalar(diag[:], ident[0:32, 0:32], mm, None, ALU.mult).then_inc(l_D, 1)
                    dve.wait_ge(l_mb, b + 1)
                    for k in range(2):
                        last = nc.vector.tensor_tensor(cc[:, k, :].rearrange("p (q r) -> p q r", r=R),
                                                       c0[:, k, :].unsqueeze(2).to_broadcast([P, 8, R]),
                                                       cb[1][:, 0:32].rearrange("p (q r) -> p q r", r=R), ALU.subtract)
                    step2(last)
                    for k in range(2):
                        nc.vector.tensor_tensor(PS[:, k], st[k][:].rearrange("p (s q) -> p s q", q=32),
                                                cc[:, k, :].unsqueeze(1).to_broadcast([P, ROWTOK, 32]), ALU.add).then_inc(l_x, 1)
                    dve.wait_ge(l_nT, b + 1)
                    nc.vector.tensor_copy(PnT[:], cb[0][0:DS, 0:32]).then_inc(l_nk, 1)
                    for k in range(2):
                        last = nc.vector.tensor_reduce(dp[:, k, :], PS[:, k].rearrange("p s q -> p q s"), AX.X, ALU.add)
                    last.then_inc(l_dp, 1)
                    dve.wait_ge(pv_ready, b + 2)
                    step2(nc.vector.reciprocal(rs, cb[1][0:64, DK:DK + 1]))
                    step(nc.vector.tensor_scalar(rs, rs, gate(1), None, ALU.mult))
                    step2(nc.vector.scalar_tensor_tensor(ob[:, 0, :], cb[1][0:64, 0:DK], rs, ob[:, 0, :], ALU.mult, ALU.add))
                    dve.wait_ge(c_o, b + 1)
                    nc.vector.scalar_tensor_tensor(ob[:, 0, :], tb[0][0:64, 0:DK], gate(0), ob[:, 0, :], ALU.mult, ALU.add).then_inc(b_done, 1)
                    assert step.n == 10 and step2.n == 8

        @block.tensor
        def _(pe):
            pe.wait_ge(consts_sb["soft"]["p3_w1_in"], 16)
            pe.wait_ge(w_in1, 48)
            for k in range(2):
                for m in range(2):
                    for q in range(2):
                        for s in range(8):
                            last = nc.tensor.matmul(st[0][:, 2 * k + m:2 * k + m + 1], w1[:, k, q, s, m * P:(m + 1) * P],
                                                    pe_T[:, k, q, s:s + 1], start=(q + s == 0), stop=(q + s == 8))
            last.then_inc(bias_ready, 1)
            pe.wait_ge(small_in, 16 * 7)
            for a in range(2):
                last = nc.tensor.transpose(st[1][:, DT * a:DT * a + DT], new_tok[:, 256 * a:256 * a + P], ident[0:DT, 0:DT])
            last.then_inc(kn_ready, 1)

            def transposes(x, bank, slot, q, rows):
                for s in range(4):
                    last = nc.tensor.transpose(tb[bank][:, s * P:s * P + rows], x[0:rows, 4 * q + s, slot].rearrange("p g d -> p (g d)"),
                                               ident[0:rows, 0:rows])
                last.then_inc(tr_ready, 1)

            def project(k, half, rows, between=None):
                turned = XT[k if half is None else half]
                for m in range(2):
                    out = ph[2 * k + m][:].rearrange("p (g n) -> p g n", g=NG)
                    for q in range(2):
                        if between:
                            between(2 * m + q)
                        if half is None:
                            dst, src, w = 0, q, rows - 1
                        elif half == 0:
                            dst, src, w = 0, q, P - q
                        else:
                            dst, src, w = P - q, 0, P
                        for s in range(8):
                            last = nc.tensor.matmul(out[:, :, dst:dst + w], w1[:, k, q, s, m * P:(m + 1) * P],
                                                    turned[:, s, :, src:src + w], start=(not half and q + s == 0),
                                                    stop=(q == 1 and s == 7), skip_group_check=True)
                last.then_inc(proj_ready, 1)

            def key_blocks(bank, n_blocks, prev):
                pe.wait_ge(hs_ready, prev + 2)
                for g in range(NG):
                    out = bank[0:64, 64 * g:64 * g + n_blocks] if n_blocks < P else bank[64 * g:64 * g + 64, 0:n_blocks]
                    for m in range(2):
                        last = nc.tensor.matmul(out, w2[:, 0, m, :], hs[:, m, g, 0:n_blocks], start=(m == 0), stop=(m == 1))
                last.then_inc(c_kv, 1)

            def value_blocks(n_blocks, prev):
                pe.wait_ge(hs_ready, prev + 4)
                for t in range((n_blocks + P - 1) // P):
                    w = min(P, n_blocks - t * P)
                    for g in range(NG):
                        for m in range(2):
                            last = nc.tensor.matmul(tb[1][0:w, P * t + DK * g:P * t + DK * g + DK], hs[:, m, g, t * P:t * P + w],
                                                    w2[:, 1, m, :], start=(m == 0), stop=(m == 1))
                last.then_inc(c_kv, 1)

            pe.wait_ge(xp_in, 16)
            for e in range(8):
                if e >= 2:
                    pe.wait_ge(kept[e % 2], e // 2)
                transposes(X[3], e % 2, e // 4, e % 4, NCP)
            pe.wait_ge(kept[0], 4)
            pe.wait_ge(kept[1], 4)
            for k in range(2):
                project(k, None, NCP)
            key_blocks(tb[0], NCP - 1, 0)
            value_blocks(NCP - 1, 0)
            pe.wait_ge(c_kc, 1)
            pe.wait_ge(c_vc, 1)
            pe.sem_inc(prompt_done, 1)
            pe.wait_ge(kn_kept, 2)
            with pe.Fori(0, DB // 2) as i:
                for j in range(2):
                    b = 2 * i + j
                    newk = lambda a: knT[:, a, bass.ds(DS * b, DS)]

                    def scores(e):
                        pe.wait_ge(kept[e % 2], 12 * b + e // 2 + 5)
                        for s in range(4):
                            o = (4 * (e % 4) + s) * 32
                            last = nc.tensor.matmul(st[e // 8][:, o:o + 32], KsT[e % 2][:, s, :], qc[:], start=True, stop=True)
                        last.then_inc(s_done, 1)

                    def turn(e):
                        pe.wait_ge(kept[e % 2], 12 * b + e // 2 + 4)
                        if e < 16:
                            tile, slot = e // 8, 2 * (e // 4 % 2)
                        else:
                            tile, slot = (e - 16) // 4, 1
                        transposes(X[2 * j + tile], e % 2, slot, e % 4, P)

                    def turn_and_score(e0):
                        for e in range(e0, e0 + 4):
                            turn(e)
                            if e > e0:
                                scores(e - 1)
                        scores(e0 + 3)

                    def window(q):
                        if q == 0:
                            pe.wait_ge(kw_in, 32 * (b + 1))
                            for c in range(4):
                                last = nc.tensor.transpose(wb[0][:, c * P:(c + 1) * P], Kw[:, c, 0:P], ident[:])
                            last.then_inc(w_tr, 1)
                        elif q == 1:
                            pe.wait_ge(w_kT, b + 1)
                            nc.tensor.matmul(wb[0][0:64, :], qb[:], KwT[:], start=True, stop=True)
                            nc.tensor.matmul(wb[1][0:64, 0:DS], qb[:], newk(1), start=True, stop=True).then_inc(w_s, 1)
                        elif q == 2:
                            pe.wait_ge(w_e, b + 1)
                            pe.sem_inc(w_carry, 1)
                            for c in range(4):
                                nc.tensor.transpose(wb[0][:, c * 64:(c + 1) * 64], Sw[:, c * P:(c + 1) * P], ident[0:64, 0:64])
                            nc.tensor.transpose(wb[0][0:DS, 256:320], Sw[:, WIN:], ident[0:64, 0:64]).then_inc(w_pT, 1)
                        else:
                            pe.wait_ge(w_pk, b + 1)
                            for g in range(NG):
                                out = wb[1][32 * g:32 * g + 32, 0:DK]
                                for c in range(4):
                                    nc.tensor.matmul(out, PwT[:, 64 * c + 32 * g:64 * c + 32 * g + 32],
                                                     Kw[:, c, P + DK * g:P + DK * g + DK], start=(c == 0), stop=False)
                                last = nc.tensor.matmul(out, PwT[0:DS, 256 + 32 * g:288 + 32 * g],
                                                        vn[:, j, 1, DK * g:DK * g + DK], start=False, stop=True)
                            last.then_inc(w_o, 1)

                    def choose(q):
                        if q == 0:
                            key_blocks(cb[0], NCD - 1, 4 * b + 4)
                        elif q == 1:
                            pe.wait_ge(c_kc, b + 2)
                            nc.tensor.matmul(cb[0][0:64, 0:NCD - 1], qb[:], kcT[:, 0:NCD - 1], start=True, stop=True).then_inc(c_s, 1)
                        elif q == 2:
                            pe.wait_ge(c_p, b + 1)
                            pe.sem_inc(w_carry, 1)
                            for t in range(2):
                                w = P - t
                                last = nc.tensor.transpose(cb[1][0:w, 64 * t:64 * t + 64], Pc[:, t * P:t * P + w], ident[0:64, 0:64])
                            last.then_inc(c_pT, 1)
                        elif q == 3:
                            pe.wait_ge(c_pk, b + 1)
                            for t in range(2):
                                w = P - t
                                last = nc.tensor.matmul(cb[1][0:8, 0:64], PcS[0:w, t, :], overlap[0:w, t, :], start=(t == 0), stop=(t == 1))
                            last.then_inc(c_imp, 1)
                        elif q == 4:
                            pe.wait_ge(c_sel, b + 1)
                            pe.sem_inc(w_carry, 1)
                            nc.tensor.transpose(cb[1][0:64, 0:8], sel[:], ident[0:8, 0:8]).then_inc(l_sT, 1)
                        elif q == 5:
                            pe.wait_ge(l_sk, b + 1)
                            for k in range(2):
                                last = nc.tensor.matmul(cb[1][:, 8 * k:8 * k + 8], spread[:, k, :], selT[:], start=True, stop=True)
                            last.then_inc(l_mask, 1)
                        elif q == 6:
                            pe.wait_ge(l_mx, b + 1)
                            nc.tensor.transpose(cb[0][0:32, 0:P], mxx[:], ident[:])
                            nc.tensor.matmul(cb[0][0:32, P:P + DS], qc[:], newk(0), start=True, stop=True).then_inc(l_mT, 1)
                        else:
                            pe.wait_ge(l_D, b + 1)
                            nc.tensor.matmul(cb[1][:, 0:32], ones[0:32, :], diag[:], start=True, stop=True).then_inc(l_mb, 1)

                    def keys_gap(q):
                        if q == 0:
                            pe.wait_ge(x_in[2 * j + 1], 16 * (i + 1))
                        turn(8 + q)
                        window(q)

                    def values_gap(q):
                        turn(20 + q)
                        choose(q)

                    def all_kept(e):
                        for w in range(2):
                            pe.wait_ge(kept[w], 12 * b + e // 2 + 5)

                    pe.wait_ge(b_done, b + 1)
                    pe.wait_ge(q_ready, b + 1)
                    pe.wait_ge(x_in[2 * j], 16 * (i + 1))
                    for e in range(4):
                        turn(e)
                    turn_and_score(4)
                    project(0, 0, P, between=keys_gap)
                    turn_and_score(12)
                    all_kept(11)
                    project(0, 1, P, between=lambda q: turn(16 + q))
                    all_kept(19)
                    pe.wait_ge(w_done, b + 2)
                    project(1, 0, P, between=values_gap)
                    all_kept(23)
                    project(1, 1, P, between=lambda q: choose(4 + q))
                    pe.wait_ge(l_e, 3 * b + 3)
                    pe.sem_inc(w_carry, 1)
                    nc.tensor.transpose(cb[0][0:DS, 0:32], sn[:], ident[0:32, 0:32]).then_inc(l_nT, 1)
                    value_blocks(NCD - 1, 4 * b + 4)
                    pe.wait_ge(l_nk, b + 1)
                    pe.wait_ge(l_dp, b + 1)
                    for g in range(NG):
                        den = cb[1][32 * g:32 * g + 32, DK:DK + 1]
                        for k in range(2):
                            nc.tensor.matmul(den, dp[:, k, :], ones[:, 0:1], start=(k == 0), stop=False)
                        nc.tensor.matmul(den, PnT[:], ones[0:DS, 0:1], start=False, stop=True)
                        out = cb[1][32 * g:32 * g + 32, 0:DK]
                        for k in range(2):
                            for s in range(ROWTOK):
                                nc.tensor.matmul(out, PS[:, k, s, :], X[2 * j + k][:, s, 3, g, :], start=(k + s == 0), stop=False)
                        last = nc.tensor.matmul(out, PnT[:], vn[:, j, 0, DK * g:DK * g + DK], start=False, stop=True)
                    last.then_inc(pv_ready, 1)
                    pe.wait_ge(c_vc, b + 2)
                    for g in range(NG):
                        for t in range(2):
                            w = P - t
                            last = nc.tensor.matmul(tb[0][32 * g:32 * g + 32, 0:DK], PcT[0:w, t, 32 * g:32 * g + 32], vc[0:w, t, g, :],
                                                    start=(t == 0), stop=(t == 1))
                    last.then_inc(c_o, 1)


def prompt_attention(nc, io, keep, scratch, consts_sb):
    ident = consts_sb["ident"]
    kcT_p, vc_p = keep["kcT_p"], keep["vc_p"]
    z = scratch["z_tok"]
    NQ = T // P
    NBK = NCP - 1
    CMP, SLC, WND = 0, 1, 2

    class Item:
        pass

    items, groups, kinds = [], [], []
    for j in range(2):
        for kind in (SLC, WND, CMP):
            kinds.append((j, kind))
            for qt in range(NQ) if kind != CMP else [0]:
                it = Item()
                it.j, it.kind, it.qt, it.n, it.c = j, kind, qt, len(items), len(kinds) - 1
                it.k0 = max(0, qt - 4) if kind == WND else 0
                it.blocks = list(range(NQ)) if kind == CMP else list(range(it.k0, qt + 1))
                it.groups = []
                for a in range(0, len(it.blocks), 4):
                    it.groups.append(len(groups))
                    groups.append((it, a, min(4, len(it.blocks) - a)))
                it.last = kind == CMP or qt == NQ - 1
                items.append(it)
    NI, NGR, NKD = len(items), len(groups), len(kinds)
    assert NI % 2 == 0 and NGR % 2 == 0 and NKD % 2 == 0

    with ExitStack() as ctx:
        sb = lambda name, shape: ctx.enter_context(nc.sbuf_tensor("a4_" + name, shape, F32))
        sem = lambda name: ctx.enter_context(nc.semaphore("p4_" + name))
        kv = sb("kv", [P, NQ, 512])
        KT = sb("KT", [64, 2, NG, T])
        q = sb("q", [64, 2, T])
        Pr = [sb(f"Pr{i}", [P, T]) for i in range(2)]
        PT = [sb(f"PT{i}", [P, 4, P]) for i in range(2)]
        nm = sb("nm", [P, NI])
        nmc = sb("nmc", [P, 2, NQ])
        den = sb("den", [P, NKD, NQ])
        gates = sb("gates", [P, NQ, 24])
        causal = sb("causal", [P, P])
        older = sb("older", [P, P])
        cmask = sb("cmask", [P, NQ, NBK])
        osum = sb("osum", [P, NQ, DK])
        o = sb("o", [P, NQ, NH * DK])
        ps = [ctx.enter_context(nc.psum_tensor(f"s{i}", [P, T], F32)) for i in range(2)]
        pt = [ctx.enter_context(nc.psum_tensor(f"pt{i}", [P, 4, P], F32)) for i in range(2)]
        pv = [ctx.enter_context(nc.psum_tensor(f"pv{i}", [P, NQ, DK], F32)) for i in range(2)]

        kv_in, small_in, kT_ready, q_in, gates_ready = (sem(n) for n in ("kv_in", "small_in", "kT_ready", "q_in0", "gates_ready"))
        q_in = [q_in, sem("q_in1")]
        kT_kept = [sem("kT_kept_dve"), sem("kT_kept_act")]
        s_ready, masked, cmp_step, max_ready, e_ready, t_ready, pv_ready, kind_step, kind_done, o_out, den_ready = (sem(n) for n in (
            "s_ready", "masked", "cmp_step", "max_ready", "e_ready", "t_ready", "pv_ready", "kind_step", "kind_done", "o_out",
            "den_ready"))
        heads_done, w_carry = sem("heads_done"), sem("w_carry")
        kept = [sem("kept_dve"), sem("kept_act")]

        block = ctx.enter_context(nc.Block())

        def move_group(eng, i, k, copy):
            it, a, n = groups[k]
            rows = NBK if it.kind == CMP else P
            eng.wait_ge(pv_ready, NGR * i + k + 1)
            eng.wait_ge(t_ready, NGR * i + k + 1)
            copy(PT[k % 2][0:rows, 0:n, :], pt[k % 2][0:rows, 0:n, :]).then_inc(kept[k % 2], 1)

        def move_keys(eng, e, copy):
            a, g, half = e // 4, e // 2 % 2, e % 2
            eng.wait_ge(kT_ready, e + 1)
            copy(KT[:, a, g, 512 * half:512 * half + 512], pt[e % 2][0:64].rearrange("p b c -> p (b c)")).then_inc(kT_kept[e % 2], 1)

        @block.sync
        def _(sp):
            sp.dma_start(kv[:], z[0:T, 1280:1792].rearrange("(t p) n -> p t n", p=P)).then_inc(kv_in, 16)
            for dst, src in ((causal, "c_causal"), (older, "c_older"), (cmask, "c_cmask")):
                sp.dma_start(dst[:], io[src]).then_inc(small_in, 16)
            sp.dma_start(gates[:], z[0:T, 1792:1816].rearrange("(t p) n -> p t n", p=P)).then_inc(small_in, 16)
            with sp.Fori(0, NH // 2) as i:
                for j in range(2):
                    sp.wait_ge(heads_done, 2 * i + j + 1)
                    sp.dma_start(q[:, j, :], scratch["q_T"][:, bass.ds(2 * i + j, 1), 0:T].rearrange("p o t -> p (o t)")).then_inc(q_in[j], 16)
            sp.wait_ge(kind_done, NKD * (NH // 2) + 2)
            sp.dma_start(scratch["o_mix"][0:T, HGW:D].rearrange("(t p) n -> p t n", p=P), o[:]).then_inc(o_out, 16)
            sp.wait_ge(o_out, 16)

        @block.scalar
        def _(act):
            act.wait_ge(small_in, 16 * 4)
            nc.scalar.activation(gates[:], gates[:], ACT.Sigmoid).then_inc(gates_ready, 1)
            for e in range(1, 8, 2):
                move_keys(act, e, lambda o_, i_: nc.scalar.mul(o_, i_, SCALE))
            act.wait_ge(kT_kept[1], 4)
            act.sem_inc(e_ready, 2)
            act.sem_inc(kept[1], 1)
            with act.Fori(0, NH // 2) as i:

                def probabilities(it):
                    act.wait_ge(max_ready, NI * i + it.n + 1)
                    p = Pr[it.n % 2]
                    if it.kind == CMP:
                        nc.scalar.activation(p[:, 0:NQ * NBK], p[:, 0:NQ * NBK], ACT.Exp).then_inc(e_ready, 1)
                    else:
                        w = len(it.blocks) * P
                        nc.scalar.activation(p[:, 0:w], ps[it.n % 2][:, 0:w], ACT.Exp, bias=nm[:, it.n:it.n + 1],
                                             accum_out=den[:, it.c, it.qt:it.qt + 1]).then_inc(e_ready, 1)

                probabilities(items[0])
                for it in items:
                    if it.n + 1 < NI:
                        probabilities(items[it.n + 1])
                    for k in it.groups:
                        if k % 2 == 1:
                            move_group(act, i, k, nc.scalar.copy)

        @block.vector
        def _(dve):
            for e in range(0, 8, 2):
                move_keys(dve, e, lambda o_, i_: nc.vector.tensor_scalar(o_, i_, SCALE, None, ALU.mult))
            dve.wait_ge(small_in, 16 * 4)
            dve.wait_ge(gates_ready, 1)
            dve.wait_ge(kT_kept[0], 4)
            dve.sem_inc(kept[0], 1)
            dve.sem_inc(kind_done, 2)
            dve.sem_inc(heads_done, 2)
            with dve.Fori(0, NH // 2) as i:
                n_masked, n_cmp, n_kind = NI - 2, 8, 3 * NKD
                at = {"masked": 0}
                cstep = Steps(dve, cmp_step, n_cmp * i)
                kstep = Steps(dve, kind_step, n_kind * i)

                def maximum(it):
                    s = ps[it.n % 2]
                    dve.wait_ge(s_ready, NI * i + it.n + 1)
                    if it.kind == CMP:
                        s3 = s[:, 0:NQ * NBK].rearrange("p (t n) -> p t n", t=NQ)
                        cstep(nc.vector.tensor_tensor(s3, s3, cmask[:], ALU.add))
                        cstep(nc.vector.tensor_reduce(nmc[:, it.j, :], s3, AX.X, ALU.max))
                        dve.sem_inc(heads_done, 1)
                        cstep(nc.vector.tensor_scalar(nmc[:, it.j, :], nmc[:, it.j, :], -BIG / 1e10, None, ALU.max))
                        nc.vector.tensor_tensor(Pr[it.n % 2][:, 0:NQ * NBK].rearrange("p (t n) -> p t n", t=NQ), s3,
                                                nmc[:, it.j, :].unsqueeze(2).to_broadcast([P, NQ, NBK]), ALU.subtract).then_inc(max_ready, 1)
                        return
                    w = len(it.blocks) * P
                    if it.kind == WND and len(it.blocks) == 5:
                        nc.vector.tensor_tensor(s[:, 0:P], s[:, 0:P], older[:], ALU.add)
                    nc.vector.tensor_tensor(s[:, w - P:w], s[:, w - P:w], causal[:], ALU.add).then_inc(masked, 1)
                    at["masked"] += 1
                    dve.wait_ge(masked, n_masked * i + at["masked"])
                    nc.vector.tensor_reduce(nm[:, it.n:it.n + 1], s[:, 0:w], AX.X, ALU.max, negate=True).then_inc(max_ready, 1)

                def finish_kind(it):
                    h = 2 * i + it.j
                    d = den[:, it.c, :]
                    dve.wait_ge(e_ready, NI * i + it.n + 3)
                    if it.kind == CMP:
                        dve.wait_ge(den_ready, 2 * i + it.j + 1)
                        cstep(nc.vector.tensor_scalar(d, d, 1e-30, None, ALU.max))
                    kstep(nc.vector.reciprocal(d, d))
                    gate = gates[:, :, bass.ds(h + 8 * it.kind, 1)].rearrange("p t o -> p (t o)")
                    kstep(nc.vector.tensor_tensor(d, d, gate, ALU.mult))
                    dve.wait_ge(pv_ready, NGR * i + it.groups[-1] + 3)
                    dst = o[:, :, bass.ds(DK * h, DK)]
                    rs = d.unsqueeze(2).to_broadcast([P, NQ, DK])
                    if it.kind == SLC:
                        kstep(nc.vector.tensor_tensor(dst, pv[it.c % 2][:], rs, ALU.mult))
                        dve.sem_inc(kind_done, 1)
                    else:
                        kstep(nc.vector.tensor_tensor(osum[:], pv[it.c % 2][:], rs, ALU.mult))
                        nc.vector.tensor_tensor(dst, dst, osum[:], ALU.add).then_inc(kind_done, 1)

                maximum(items[0])
                pending = None
                for it in items:
                    if it.n + 1 < NI:
                        maximum(items[it.n + 1])
                    if it.kind == CMP:
                        dve.wait_ge(e_ready, NI * i + it.n + 3)
                        nc.vector.tensor_reduce(den[:, it.c, :], Pr[it.n % 2][:, 0:NQ * NBK].rearrange("p (t n) -> p t n", t=NQ),
                                                AX.X, ALU.add).then_inc(den_ready, 1)
                    for k in it.groups:
                        if k % 2 == 0:
                            move_group(dve, i, k, nc.vector.tensor_copy)
                    if pending is not None:
                        finish_kind(pending)
                    pending = it if it.last else None
                finish_kind(pending)
                assert cstep.n == n_cmp and kstep.n == n_kind and at["masked"] == n_masked

        @block.tensor
        def _(pe):
            pe.wait_ge(kv_in, 16)
            for e in range(8):
                a, g, half = e // 4, e // 2 % 2, e % 2
                if e >= 2:
                    pe.wait_ge(kT_kept[e % 2], e // 2)
                for b in range(4):
                    last = nc.tensor.transpose(pt[e % 2][0:64, b, :], kv[:, 4 * half + b, 256 * a + DK * g:256 * a + DK * g + DK], ident[:])
                last.then_inc(kT_ready, 1)
            pe.wait_ge(kT_kept[0], 4)
            pe.wait_ge(kT_kept[1], 4)
            pe.sem_inc(pv_ready, 2)
            with pe.Fori(0, NH // 2) as i:
                grp = i // 2

                def scores(it):
                    s = ps[it.n % 2]
                    pe.wait_ge(e_ready, NI * i + it.n + 1)
                    if it.qt == 0 and it.kind == SLC:
                        pe.wait_ge(q_in[it.j], 16 * i + 16)
                    pe.sem_inc(w_carry, 1)
                    if it.kind == CMP:
                        for t in range(NQ):
                            last = nc.tensor.matmul(s[:, NBK * t:NBK * t + NBK], q[:, it.j, t * P:t * P + P],
                                                    kcT_p[:, bass.ds(grp, 1), :].rearrange("p o n -> p (o n)"), start=True, stop=True)
                    else:
                        w = len(it.blocks) * P
                        for c in range(0, w, 512):
                            n = min(512, w - c)
                            keys = KT[:, it.kind - 1, bass.ds(grp, 1), it.k0 * P + c:it.k0 * P + c + n].rearrange("p o n -> p (o n)")
                            last = nc.tensor.matmul(s[:, c:c + n], q[:, it.j, it.qt * P:it.qt * P + P], keys, start=True, stop=True)
                    last.then_inc(s_ready, 1)

                def turn(k):
                    it, a, n = groups[k]
                    if a == 0:
                        pe.wait_ge(e_ready, NI * i + it.n + 3)
                    pe.wait_ge(kept[k % 2], NGR // 2 * i + k // 2 + 1)
                    if it.kind == CMP:
                        pe.sem_inc(w_carry, 1)
                    for b in range(n):
                        if it.kind == CMP:
                            last = nc.tensor.transpose(pt[k % 2][0:NBK, b, :], Pr[it.n % 2][:, NBK * (a + b):NBK * (a + b) + NBK], ident[:])
                        else:
                            last = nc.tensor.transpose(pt[k % 2][:, b, :], Pr[it.n % 2][:, P * (a + b):P * (a + b) + P], ident[:])
                    last.then_inc(t_ready, 1)

                def values(k):
                    it, a, n = groups[k]
                    if it.qt == 0 and a == 0:
                        pe.wait_ge(kind_done, NKD * i + it.c + 1)
                    pe.wait_ge(kept[k % 2], NGR // 2 * i + k // 2 + 2)
                    if it.kind == CMP:
                        pe.sem_inc(w_carry, 1)
                    for b in range(n):
                        if it.kind == CMP:
                            last = nc.tensor.matmul(pv[it.c % 2][:, a + b, :], PT[k % 2][0:NBK, b, :],
                                                    vc_p[:, bass.ds(grp, 1), :].rearrange("p o d -> p (o d)"), start=True, stop=True)
                        else:
                            last = nc.tensor.matmul(pv[it.c % 2][:, it.qt, :], PT[k % 2][:, b, :],
                                                    kv[:, it.blocks[a + b], bass.ds(grp * DK + (256 * (it.kind - 1) + P), DK)],
                                                    start=(a + b == 0), stop=(a + b == len(it.blocks) - 1))
                    last.then_inc(pv_ready, 1)

                scores(items[0])
                for it in items:
                    if it.n + 1 < NI:
                        scores(items[it.n + 1])
                    for k in it.groups:
                        turn(k)
                        if k > 0:
                            values(k - 1)
                values(NGR - 1)


def rows_of(t):
    return P if t < NT - 1 else DT


def project_out(nc, io, keep, scratch, consts_sb):
    ident, hH, hL = consts_sb["ident"], keep["hH"], keep["hL"]
    with ExitStack() as ctx:
        sb = lambda name, shape: ctx.enter_context(nc.sbuf_tensor("a5_" + name, shape, F32))
        sem = lambda name: ctx.enter_context(nc.semaphore("p5_" + name))
        wH5, wL5 = (ctx.enter_context(nc.sbuf_tensor(n, [P, KD, D], F32R)) for n in ("wH5", "wL5"))
        raw = keep["raw"][:].rearrange("p a k n -> p a (k n)")
        o = sb("o", [P, 3, D])
        x = sb("x", [P, 3, D])
        x1 = sb("x1", [P, 2, D])
        xs = sb("xs", [P, 2, D])
        oH, oL = keep["wH"], keep["wL"]
        sq = sb("sq", [P, D])
        ss, rt, g2 = sb("ss", [P, NT]), sb("rt", [P, NT]), sb("g2", [P, KD])
        to = [ctx.enter_context(nc.psum_tensor(f"to{i}", [P, 4, P], F32)) for i in range(2)]
        py = [ctx.enter_context(nc.psum_tensor(f"py{i}", [P, 512], F32)) for i in range(4)]
        th = [ctx.enter_context(nc.psum_tensor(f"th{i}", [P, 4, P], F32)) for i in range(2)]
        soft = consts_sb["soft"]
        w_in = [soft["p5_w_in0"], soft["p5_w_in1"]]
        wH_ready, wL_ready, oL_ready = sem("wH_ready"), sem("wL_ready"), sem("oL_ready")
        g2_in, x1_out = sem("g2_in"), [soft["p5_x1_out0"], soft["p5_x1_out1"]]
        o_in = [sem(f"o_in{i}") for i in range(3)]
        (oT_ready, oT_kept, y_ready, x1_ready, ss_ready, ms_ready, root_ready, rstd_ready, xs_ready, hT_ready, hT_kept) = (
            sem(n) for n in ("oT_ready", "oT_kept", "y_ready", "x1_ready", "ss_ready", "ms_ready", "root_ready", "rstd_ready",
                             "xs_ready", "hT_ready", "hT_kept"))
        hH_ready = sem("hH_ready")
        block = ctx.enter_context(nc.Block())

        @block.sync
        def _(sp):
            sp.dma_start(g2[:], io["norm2"].rearrange("a (k p) -> p (a k)", p=P), allow_slow_non_contiguous=True).then_inc(g2_in, 16)
            for t in range(NT):
                r = rows_of(t)
                if t >= 3:
                    sp.wait_ge(x1_ready, 2 * (t - 2))
                sp.dma_start(o[0:r, t % 3, :], scratch["o_mix"][t * P:t * P + r, :]).then_inc(o_in[t % 3], 16)
                src = io["x_prompt"][0, t * P:(t + 1) * P, :] if t < NT - 1 else io["x_sample"].rearrange("b t d -> (b t) d")
                sp.dma_start(x[0:r, t % 3, :], src).then_inc(o_in[t % 3], 16)

        @block.gpsimd
        def _(pool):
            for k in range(KD):
                if k >= 2:
                    pool.wait_ge(wL_ready, k - 1)
                pool.dma_start(raw[:, k % 2], io["w_out"][0, k * P:(k + 1) * P, :]).then_inc(w_in[k % 2], 16)
            for t in range(NT):
                r = rows_of(t)
                pool.wait_ge(x1_ready, 2 * t + 2)
                pool.dma_start(scratch["x1"][t * P:t * P + r, :], x1[0:r, t % 2, :]).then_inc(x1_out[t % 2], 16)
            pool.wait_ge(x1_out[0], 16 * 5)
            pool.wait_ge(x1_out[1], 16 * 4)

        @block.scalar
        def _(act):
            for k in range(KD):
                act.wait_ge(w_in[k % 2], 16 * (k // 2 + 1))
                nc.scalar.copy(wH5[:, k], raw[:, k % 2]).then_inc(wH_ready, 1)

            def high_of_o(t):
                r = rows_of(t)
                for h in range(2):
                    act.wait_ge(oT_ready, 2 * t + h + 1)
                    if h == 0 and t >= 2:
                        act.wait_ge(y_ready, 2 * (t - 1))
                    nc.scalar.copy(oH[:, t % 2, 4 * h:4 * h + 4, 0:r], to[h][:, :, 0:r]).then_inc(oT_kept, 1)

            high_of_o(0)
            for t in range(NT):
                r = rows_of(t)
                if t + 1 < NT:
                    high_of_o(t + 1)
                act.wait_ge(x1_ready, 2 * t + 2)
                if t >= 1:
                    act.wait_ge(ss_ready, t)
                nc.scalar.activation(sq[0:r, :], x1[0:r, t % 2, :], ACT.Square, accum_out=ss[0:r, t:t + 1]).then_inc(ss_ready, 1)
                act.wait_ge(ms_ready, t + 1)
                nc.scalar.activation(rt[0:r, t:t + 1], ss[0:r, t:t + 1], ACT.Sqrt).then_inc(root_ready, 1)

        @block.vector
        def _(dve):
            for k in range(KD):
                dve.wait_ge(wH_ready, k + 1)
                nc.vector.tensor_tensor(wL5[:, k], raw[:, k % 2], wH5[:, k].bitcast(F32), ALU.subtract).then_inc(wL_ready, 1)
            dve.wait_ge(g2_in, 16)

            def rest_of_o(t):
                r = rows_of(t)
                for h in range(2):
                    dve.wait_ge(oT_kept, 2 * t + h + 1)
                    nc.vector.tensor_tensor(oL[:, t % 2, 4 * h:4 * h + 4, 0:r], to[h][:, :, 0:r],
                                            oH[:, t % 2, 4 * h:4 * h + 4, 0:r].bitcast(F32), ALU.subtract).then_inc(oL_ready, 1)

            def norm(t):
                r = rows_of(t)
                dve.wait_ge(ss_ready, t + 1)
                nc.vector.tensor_scalar(ss[0:r, t:t + 1], ss[0:r, t:t + 1], 1.0 / D, EPS, ALU.mult, ALU.add).then_inc(ms_ready, 1)
                dve.wait_ge(root_ready, t + 1)
                nc.vector.reciprocal(rt[0:r, t:t + 1], rt[0:r, t:t + 1]).then_inc(rstd_ready, 1)
                dve.wait_ge(rstd_ready, t + 1)
                if t >= 2:
                    dve.wait_ge(hT_ready, 2 * (t - 1))
                nc.vector.tensor_scalar(xs[0:r, t % 2, :], x1[0:r, t % 2, :], rt[0:r, t:t + 1], None, ALU.mult).then_inc(xs_ready, 1)

            def keep_hT(t):
                r = rows_of(t)
                for h in range(2):
                    dve.wait_ge(hT_ready, 2 * t + h + 1)
                    nc.vector.tensor_tensor(hH[:, 4 * h:4 * h + 4, t * P:t * P + r], th[h][:, :, 0:r],
                                            g2[:, 4 * h:4 * h + 4].unsqueeze(2).to_broadcast([P, 4, r]), ALU.mult).then_inc(hH_ready, 1)
                    dve.wait_ge(hH_ready, 2 * t + h + 1)
                    for k in range(4):
                        last = nc.vector.scalar_tensor_tensor(hL[:, 4 * h + k, t * P:t * P + r], th[h][:, k, 0:r],
                                                              g2[:, 4 * h + k:4 * h + k + 1],
                                                              hH[:, 4 * h + k, t * P:t * P + r].bitcast(F32), ALU.mult, ALU.subtract)
                    last.then_inc(hT_kept, 1)

            rest_of_o(0)
            for t in range(NT):
                r = rows_of(t)
                if t + 1 < NT:
                    rest_of_o(t + 1)
                dve.wait_ge(o_in[t % 3], 32 * (t // 3 + 1))
                for h in range(2):
                    if h == 0 and t >= 2:
                        dve.wait_ge(x1_out[t % 2], 16 * (t // 2))
                        dve.wait_ge(xs_ready, t - 1)
                    dve.wait_ge(y_ready, 2 * t + h + 1)
                    nc.vector.tensor_tensor(x1[0:r, t % 2, 512 * h:512 * h + 512], py[2 * (t % 2) + h][0:r, :],
                                            x[0:r, t % 3, 512 * h:512 * h + 512], ALU.add).then_inc(x1_ready, 1)
                norm(t)
                if t >= 1:
                    keep_hT(t - 1)
            keep_hT(NT - 1)

        @block.tensor
        def _(pe):
            def turn_o(t):
                r = rows_of(t)
                pe.wait_ge(o_in[t % 3], 32 * (t // 3 + 1))
                for h in range(2):
                    if t >= 1:
                        pe.wait_ge(oL_ready, 2 * (t - 1) + h + 1)
                    for k in range(4):
                        last = nc.tensor.transpose(to[h][:, k, 0:r], o[0:r, t % 3, (4 * h + k) * P:(4 * h + k + 1) * P], ident[0:r, 0:r])
                    last.then_inc(oT_ready, 1)

            def turn_h(t):
                r = rows_of(t)
                pe.wait_ge(xs_ready, t + 1)
                for h in range(2):
                    if t >= 1:
                        pe.wait_ge(hT_kept, 2 * (t - 1) + h + 1)
                    for k in range(4):
                        last = nc.tensor.transpose(th[h][:, k, 0:r], xs[0:r, t % 2, (4 * h + k) * P:(4 * h + k + 1) * P], ident[0:r, 0:r])
                    last.then_inc(hT_ready, 1)

            turn_o(0)
            for t in range(NT):
                r = rows_of(t)
                if t + 1 < NT:
                    turn_o(t + 1)
                pe.wait_ge(oL_ready, 2 * t + 2)
                for h in range(2):
                    if t >= 2:
                        pe.wait_ge(x1_ready, 2 * (t - 2) + h + 1)
                    for k in range(KD):
                        if t == 0 and h == 0:
                            pe.wait_ge(wL_ready, k + 1)
                        for part, (op, wp) in enumerate(((oH, wH5), (oH, wL5), (oL, wH5))):
                            last = nc.tensor.matmul(py[2 * (t % 2) + h][0:r, :], op[:, t % 2, k, 0:r], wp[:, k, 512 * h:512 * h + 512],
                                                    start=(k + part == 0), stop=(k == KD - 1 and part == 2))
                    last.then_inc(y_ready, 1)
                if t >= 1:
                    turn_h(t - 1)
            turn_h(NT - 1)


def feed_forward(nc, io, keep, scratch, consts_sb):
    ident, y, wd, small_tail = consts_sb["ident"], keep["y"], keep["wd"], keep["tail_tok"]
    hH, hL = keep["hH"], keep["hL"]
    NF = FF // P
    UW = 2 + T + DB * (2 + DS)
    PARTS = [(0, 352), (352, 352), (704, 352)]
    with ExitStack() as ctx:
        sb = lambda name, shape: ctx.enter_context(nc.sbuf_tensor("a6_" + name, shape, F32))
        sem = lambda name: ctx.enter_context(nc.semaphore("p6_" + name))
        aT = sb("aT", [P, NF, TOK])
        raw, wH, wL = keep["raw"], keep["wH"], keep["wL"]
        U = [sb(f"U{i}", [P, UW]) for i in range(2)]
        C = sb("C", [P, TOK])
        flat = aT[:].rearrange("p f t -> p (f t)")
        small, past = flat[0:4, 0:FF], flat[0:2 * DB, FF:2 * FF]
        cw = sb("cw", [P, NF, 4])
        pastT = sb("pastT", [P, NF, 2 * DB])
        tails = sb("tails", [P, NF, 2 * DB + 2])
        cwj = sb("cwj", [P, 2, 4])
        ss, rt = sb("ss", [P, NT]), sb("rt", [P, NT])
        bank = [ctx.enter_context(nc.psum_tensor(f"f{i}", [P, 512], F32)) for i in range(8)]
        (small_in, cw_ready, cw_kept, past_kept, wd_free, u_ready, v_ready, u_kept, c_step, c_ready, g_ready, a_ready) = (
            sem(n) for n in ("small_in", "cw_ready", "cw_kept", "past_kept", "wd_free", "u_ready", "v_ready", "u_kept", "c_step",
                             "c_ready", "g_ready", "a_ready"))
        wH_ready, wL_ready, wd_half = sem("wH_ready"), sem("wL_ready"), sem("wd_half")
        wu_in = [sem("wu_in0"), sem("wu_in1")]
        wd_in = [consts_sb["soft"][f"p6_wd_in{i}"] for i in range(2)]
        (x1_in, nf_in, d_ready, y_ready, ss_ready, ms_ready, root_ready, out_step, out_ready, y_out, t_ready, t_kept, t_out) = (
            sem(n) for n in ("x1_in", "nf_in", "d_ready", "y_ready", "ss_ready", "ms_ready", "root_ready", "out_step", "out_ready",
                             "y_out", "t_ready", "t_kept", "t_out"))
        junk = U[0][:, 0:D]
        normf = U[1][:, 0:D]
        block = ctx.enter_context(nc.Block())
        prompt = lambda u, s: u[:, s:s + T]
        sample = lambda u, s: u[:, 2 + T:].rearrange("p (b t) -> p b t", b=DB)[:, :, s:s + DS]

        def finish(t):
            dve = nc.vector
            r = rows_of(t)
            dve.wait_ge(ss_ready, t + 1)
            nc.vector.tensor_scalar(ss[0:r, t:t + 1], ss[0:r, t:t + 1], 1.0 / D, EPS, ALU.mult, ALU.add).then_inc(ms_ready, 1)
            dve.wait_ge(root_ready, t + 1)
            nc.vector.reciprocal(rt[0:r, t:t + 1], rt[0:r, t:t + 1]).then_inc(out_step, 1)
            if t == 0:
                dve.wait_ge(nf_in, 16)
            dve.wait_ge(out_step, t + 1)
            nc.vector.scalar_tensor_tensor(y[0:r, t, :], y[0:r, t, :], rt[0:r, t:t + 1], normf[0:r], ALU.mult, ALU.mult).then_inc(out_ready, 1)

        @block.sync
        def _(sp):
            sp.dma_start(small[0:3, :], io["conv_w"][0]).then_inc(small_in, 16)
            sp.dma_start(small[3:4, :], io["conv_b"]).then_inc(small_in, 16)
            sp.dma_start(past, io["state_ffn_conv"][0].rearrange("b t f -> (b t) f")).then_inc(small_in, 16)
            wg = io["w_gate"][0].rearrange("(k p) n -> p k n", p=P)
            wv = io["w_val"][0].rearrange("(k p) n -> p k n", p=P)
            with sp.Fori(0, NF) as f:
                for a, w in enumerate((wg, wv)):
                    sp.wait_ge(wL_ready, 2 * f + a + 1)
                    sp.dma_start(raw[:, a], w[:, :, bass.ds(f * P, P)]).then_inc(wu_in[a], 16)
            sp.wait_ge(v_ready, NF + 2)
            for f0, f1 in ((0, NF // 4), (NF // 4, NF // 2)):
                sp.dma_start(wd[:, 0, f0:f1], io["w_down"][0].rearrange("(f p) n -> p f n", p=P)[:, f0:f1, 0:QW]).then_inc(wd_half, 16)
            sp.dma_start(y[:, 0:NT - 1, :], scratch["x1"][0:T].rearrange("(t p) n -> p t n", p=P)).then_inc(x1_in, 16)
            sp.dma_start(y[0:DT, NT - 1, :], scratch["x1"][T:TOK]).then_inc(x1_in, 16)
            sp.wait_ge(a_ready, NF + 1)
            sp.dma_start(normf, io["norm_f"].rearrange("(a n) -> a n", a=1).to_broadcast([P, D])).then_inc(nf_in, 16)
            sp.wait_ge(t_kept, 6)
            sp.dma_start(io["cv_p"][0, 0], small_tail[0:2, :]).then_inc(t_out, 16)
            sp.dma_start(io["cv_s"][0].rearrange("b t f -> (b t) f"), small_tail[2:18, :]).then_inc(t_out, 16)
            for t in range(NT):
                sp.wait_ge(out_ready, t + 1)
                dst = io["y_prompt"][0, t * P:(t + 1) * P, :] if t < NT - 1 else io["y_sample"].rearrange("b t d -> (b t) d")
                sp.dma_start(dst, y[0:rows_of(t), t, :]).then_inc(y_out, 16)
            sp.wait_ge(t_out, 32)
            sp.wait_ge(y_out, 16 * NT)

        @block.gpsimd
        def _(pool):
            w = io["w_down"][0].rearrange("(f p) n -> p f n", p=P)
            pool.wait_ge(v_ready, NF + 2)
            for c in range(4):
                if c >= 2:
                    pool.wait_ge(d_ready, NT * (c - 1))
                f0 = NF // 2 if c == 0 else 0
                pool.dma_start(wd[:, c % 2, f0:], w[:, f0:, c * QW:(c + 1) * QW]).then_inc(wd_in[c % 2], 16)

        @block.scalar
        def _(act):
            act.wait_ge(cw_ready, 2)
            nc.scalar.copy(pastT[:].rearrange("p f t -> p (f t)"), bank[7][:, 0:NF * 2 * DB]).then_inc(past_kept, 1)

            def high_part(f, a):
                act.wait_ge((u_ready, v_ready)[a], f + 2)
                act.wait_ge(wu_in[a], 16 * f + 16)
                nc.scalar.copy(wH[:, a].rearrange("p k n -> p (k n)"), raw[:, a].rearrange("p k n -> p (k n)")).then_inc(wH_ready, 1)

            def gate_tile(f, j, more):
                if more:
                    high_part(f + 1, 0)
                act.wait_ge(u_ready, f + 3)
                act.wait_ge(a_ready, f + 1)
                nc.scalar.copy(U[j][:, 2:354], bank[0][:, 0:352])
                nc.scalar.copy(U[j][:, 354:706], bank[1][:, 0:352])
                nc.scalar.copy(U[j][:, 706:T + 2], bank[2][:, 0:320])
                nc.scalar.copy(sample(U[j], 2), bank[2][:, 320:352].rearrange("p (b t) -> p b t", b=DB)).then_inc(u_kept, 1)
                act.wait_ge(c_ready, f + 1)
                nc.scalar.activation(C[:], C[:], ACT.Gelu_apprx_tanh).then_inc(g_ready, 1)
                if more:
                    high_part(f + 1, 1)

            high_part(0, 0)
            high_part(0, 1)
            with act.Fori(0, NF // 2 - 1) as i:
                for j in range(2):
                    gate_tile(2 * i + j, j, True)
            gate_tile(NF - 2, 0, True)
            gate_tile(NF - 1, 1, False)
            for q in range(6):
                act.wait_ge(t_ready, q + 1)
                n = min(4, NF - 4 * q)
                nc.scalar.copy(small_tail[:, 512 * q:512 * q + P * n], bank[6 + q % 2][0:18, 0:P * n]).then_inc(t_kept, 1)
            for t in range(NT):
                r = rows_of(t)
                act.wait_ge(y_ready, 3 * NT + t + 1)
                if t >= 1:
                    act.wait_ge(ss_ready, t)
                else:
                    act.wait_ge(a_ready, NF + 1)
                nc.scalar.activation(junk[0:r], y[0:r, t, :], ACT.Square, accum_out=ss[0:r, t:t + 1]).then_inc(ss_ready, 1)
                act.wait_ge(ms_ready, t + 1)
                nc.scalar.activation(rt[0:r, t:t + 1], ss[0:r, t:t + 1], ACT.Sqrt).then_inc(root_ready, 1)

        @block.vector
        def _(dve):
            dve.wait_ge(cw_ready, 1)
            nc.vector.tensor_copy(cw[:].rearrange("p f t -> p (f t)"), bank[6][:, 0:NF * 4]).then_inc(cw_kept, 1)
            for j in range(2):
                nc.vector.memset(U[j][:, 0:2], 0.0).then_inc(cw_kept, 1)
            dve.wait_ge(past_kept, 1)
            dve.wait_ge(cw_kept, 3)
            dve.sem_inc(a_ready, 1)
            dve.sem_inc(g_ready, 1)
            dve.sem_inc(wL_ready, 2)

            def rest(f, a):
                dve.wait_ge(wH_ready, 2 * f + a + 1)
                nc.vector.tensor_tensor(wL[:, a], raw[:, a], wH[:, a].bitcast(F32), ALU.subtract).then_inc(wL_ready, 1)

            def product_tile(f, j, more):
                at = bass.ds(f, 1)
                if more:
                    rest(f + 1, 0)
                step = Steps(dve, c_step, 6 * f)
                u = U[j]
                nc.vector.tensor_copy(cwj[:, j, :], cw[:, at, :].rearrange("p o t -> p (o t)"))
                step(nc.vector.tensor_copy(sample(u, 0)[:, :, 0:2], pastT[:, at, :].rearrange("p o (b t) -> p (o b) t", b=DB)))
                dve.wait_ge(u_kept, f + 1)
                wj = lambda k: cwj[:, j, k:k + 1]
                c_p, c_s = C[:, 0:T], C[:, T:TOK].rearrange("p (b t) -> p b t", b=DB)
                step(nc.vector.tensor_scalar(c_p, prompt(u, 0), wj(0), wj(3), ALU.mult, ALU.add))
                step(nc.vector.tensor_scalar(c_s, sample(u, 0), wj(0), wj(3), ALU.mult, ALU.add))
                step(nc.vector.scalar_tensor_tensor(c_p, prompt(u, 1), wj(1), c_p, ALU.mult, ALU.add))
                step(nc.vector.scalar_tensor_tensor(c_s, sample(u, 1), wj(1), c_s, ALU.mult, ALU.add))
                nc.vector.scalar_tensor_tensor(c_p, prompt(u, 2), wj(2), c_p, ALU.mult, ALU.add)
                nc.vector.scalar_tensor_tensor(c_s, sample(u, 2), wj(2), c_s, ALU.mult, ALU.add).then_inc(c_ready, 1)
                nc.vector.tensor_copy(tails[:, at, 0:2].rearrange("p o t -> p (o t)"), u[:, T:T + 2])
                step(nc.vector.tensor_copy(tails[:, at, 2:].rearrange("p o (b t) -> p (o b) t", b=DB),
                                           u[:, 2 + T:].rearrange("p (b t) -> p b t", b=DB)[:, :, DS:DS + 2]))
                dve.wait_ge(g_ready, f + 2)
                dve.wait_ge(v_ready, f + 3)
                for n, (c0, w) in enumerate(PARTS):
                    last = nc.vector.tensor_tensor(aT[:, at, c0:c0 + w].rearrange("p o t -> p (o t)"), bank[3 + n][:, 0:w],
                                                   C[:, c0:c0 + w], ALU.mult)
                last.then_inc(a_ready, 1)
                assert step.n == 6
                dve.wait_ge(a_ready, f + 2)
                if more:
                    rest(f + 1, 1)

            rest(0, 0)
            rest(0, 1)
            with dve.Fori(0, NF // 2 - 1) as i:
                for j in range(2):
                    product_tile(2 * i + j, j, True)
            product_tile(NF - 2, 0, True)
            product_tile(NF - 1, 1, False)
            dve.wait_ge(x1_in, 32)
            n_y = 0
            for c in range(4):
                for t in range(NT):
                    r = rows_of(t)
                    n_y += 1
                    dve.wait_ge(d_ready, n_y)
                    dst = y[0:r, t, c * QW:(c + 1) * QW]
                    nc.vector.tensor_tensor(dst, dst, bank[t % 3][0:r, 0:QW], ALU.add).then_inc(y_ready, 1)
                    if c == 3 and t >= 1:
                        finish(t - 1)
            finish(NT - 1)

        @block.tensor
        def _(pe):
            pe.wait_ge(small_in, 48)
            for f in range(NF):
                last = nc.tensor.transpose(bank[6][:, 4 * f:4 * f + 4], small[:, f * P:(f + 1) * P], ident[0:4, 0:4])
            last.then_inc(cw_ready, 1)
            for f in range(NF):
                last = nc.tensor.transpose(bank[7][:, 16 * f:16 * f + 16], past[:, f * P:(f + 1) * P], ident[0:16, 0:16])
            last.then_inc(cw_ready, 1)
            pe.wait_ge(cw_kept, 1)
            pe.sem_inc(u_ready, 2)
            pe.sem_inc(v_ready, 2)
            pe.wait_ge(a_ready, 1)
            with pe.Fori(0, NF // 2) as i:
                for j in range(2):
                    f = 2 * i + j
                    pe.wait_ge(g_ready, f + 1)
                    for a in range(2):
                        pe.wait_ge(wL_ready, 2 * f + a + 3)
                        if a == 1:
                            pe.wait_ge(a_ready, f + 1)
                        for n, (c0, w) in enumerate(PARTS):
                            for k in range(KD):
                                for part, (wp, hp) in enumerate(((wH, hH), (wH, hL), (wL, hH))):
                                    last = nc.tensor.matmul(bank[3 * a + n][:, 0:w], wp[:, a, k, :], hp[:, k, c0:c0 + w],
                                                            start=(k + part == 0), stop=(k == KD - 1 and part == 2))
                        last.then_inc((u_ready, v_ready)[a], 1)
            n_d = 0
            for c in range(4):
                if c == 0:
                    pe.wait_ge(wd_half, 32)
                else:
                    pe.wait_ge(wd_in[c % 2], 16 * (c // 2 + 1))
                if c == 0:
                    pe.wait_ge(a_ready, NF + 1)
                for t in range(NT):
                    r = rows_of(t)
                    if n_d >= 3:
                        pe.wait_ge(y_ready, n_d - 2)
                    for f in range(NF):
                        if n_d == 0 and f == NF // 2:
                            pe.wait_ge(wd_in[0], 16)
                        last = nc.tensor.matmul(bank[t % 3][0:r, 0:QW], aT[:, f, t * P:t * P + r], wd[:, c % 2, f, :],
                                                start=(f == 0), stop=(f == NF - 1))
                    last.then_inc(d_ready, 1)
                    n_d += 1
                    if c == 0 and t < 6:
                        if t >= 2:
                            pe.wait_ge(t_kept, t - 1)
                        for k in range(min(4, NF - 4 * t)):
                            last = nc.tensor.transpose(bank[6 + t % 2][0:18, k * P:(k + 1) * P], tails[:, 4 * t + k, :], ident[:])
                        last.then_inc(t_ready, 1)


def clear_semaphores(nc, first):
    with nc.Block() as block:
        @block.vector
        def _(dve):
            dve.sem_clear(range(first, 256))


def hybrid_step(nc, io):
    with ExitStack() as ctx:
        sb = lambda name, shape: ctx.enter_context(nc.sbuf_tensor(name, shape, F32))
        scratch = {
            "z_tok": nc.dram_tensor("z_tok", [TOK, 1816], F32).ap(),
            "q_T": nc.dram_tensor("q_T", [64, NH, TOK], F32).ap(),
            "x1": nc.dram_tensor("x1", [TOK, D], F32).ap(),
            "o_mix": nc.dram_tensor("o_mix", [TOK, D], F32).ap(),
        }
        consts = {"ident": sb("ident", [P, P]), "in": ctx.enter_context(nc.semaphore("ident_in"))}
        with nc.Block() as block:
            @block.sync
            def _(sp):
                sp.dma_start(consts["ident"][:], io["c_ident"]).then_inc(consts["in"], 16)
                sp.wait_ge(consts["in"], 16)
        consts["soft"] = {n: ctx.enter_context(nc.semaphore(n)) for n in (
            "p1_w_in0", "p1_cached", "p3_w1_in", "p3_x_in0", "p3_x_in1", "p3_x_in2", "p3_x_in3", "p5_w_in0", "p5_w_in1", "p5_x1_out0",
            "p5_x1_out1", "p6_wd_in0", "p6_wd_in1")}
        first = max(s.num for s in [consts["in"], *consts["soft"].values()]) + 1
        keep = {}
        with ExitStack() as mid:
            keep["kcT_p"] = mid.enter_context(nc.sbuf_tensor("kcT_p", [DK, NG, NCP - 1], F32))
            keep["vc_p"] = mid.enter_context(nc.sbuf_tensor("vc_p", [NCP - 1, NG, DK], F32))
            with ExitStack() as later:
                keep["w1"] = later.enter_context(nc.sbuf_tensor("w1", W1_SHAPE, F32))
            with ExitStack() as low:
                keep["qn"] = low.enter_context(nc.sbuf_tensor("qn", [64, NH, TOK], F32))
                keep["qh"] = low.enter_context(nc.sbuf_tensor("qh", [P, HH, TOK], F32))
                keep["fg"] = low.enter_context(nc.sbuf_tensor("fg", [P, HH, TOK], F32))
                project_in(nc, io, keep, scratch, consts)
                clear_semaphores(nc, first)
                hgrn(nc, io, keep, scratch, consts)
            clear_semaphores(nc, first)
            sample_attention(nc, io, keep, scratch, consts)
            clear_semaphores(nc, first)
            prompt_attention(nc, io, keep, scratch, consts)
        with ExitStack() as high:
            at = lambda stack, name, shape, dt=F32: stack.enter_context(nc.sbuf_tensor(name, shape, dt))
            with ExitStack() as later:
                keep["y"] = at(later, "y", [P, NT, D])
                keep["wd"] = at(later, "wd", [P, 2, FF // P, QW])
                keep["tail_tok"] = at(later, "tail_tok", [2 * DB + 2, FF])
            keep["hH"] = at(high, "hH", [P, KD, TOK], F32R)
            at(high, "behind_hH", [P, NT * D - KD * TOK])
            keep["hL"] = at(high, "hL", [P, KD, TOK], F32R)
            keep["raw"] = at(high, "raw", [P, 2, KD, P])
            keep["wH"] = at(high, "wH", [P, 2, KD, P], F32R)
            keep["wL"] = at(high, "wL", [P, 2, KD, P], F32R)
            clear_semaphores(nc, first)
            project_out(nc, io, keep, scratch, consts)
            clear_semaphores(nc, first)
            feed_forward(nc, io, keep, scratch, consts)


_INS = ["x_prompt", "x_sample", "cache_nsa_kv", "cache_win_kv", "state_hgrn", "state_ffn_conv", "page_table", "norm1", "w_in",
        "hg_lb_logits", "hg_norm", "cmp_pe", "cmp_w1", "cmp_w2", "w_out", "norm2", "w_gate", "w_val", "conv_w", "conv_b",
        "w_down", "norm_f"]
_OUTS = {"y_prompt": (1, T, D), "y_sample": (DB, DS, D), "kv_p": (1, 1, T, 4, 2, 64), "kv_s": (1, DB, DS, 4, 2, 64),
         "win_p": (1, 1, WIN, 2, 2, 64), "win_s": (1, DB, WIN, 2, 2, 64), "hg_p": (1, 1, HH, 128, 128),
         "hg_s": (1, DB, HH, 128, 128), "cv_p": (1, 1, 2, FF), "cv_s": (1, DB, 2, FF)}


def kernel(**inputs):
    import numpy as _np
    import concourse.bacc as _bacc
    from concourse import mybir as _mybir
    from concourse.bass_utils import run_bass_kernel_spmd as _run

    nc = _bacc.Bacc("TRN2", target_bir_lowering=False, num_devices=1)
    arrays, io = {}, {}
    for name in _INS:
        a = _np.ascontiguousarray(inputs[name])
        arrays[f"in_{name}"] = a
        io[name] = nc.dram_tensor(f"in_{name}", a.shape, _mybir.dt.from_np(a.dtype), kind="ExternalInput").ap()
    for name, a in shape_constants().items():
        arrays[name] = a
        io[name] = nc.dram_tensor(name, a.shape, _mybir.dt.from_np(a.dtype), kind="ExternalInput").ap()
    for name, shape in _OUTS.items():
        io[name] = nc.dram_tensor(f"out_{name}", shape, _mybir.dt.float32, kind="ExternalOutput").ap()
    hybrid_step(nc, io)
    r = _run(nc, [arrays], core_ids=[0])
    return tuple(r.results[0][f"out_{name}"] for name in _OUTS)
```
